# Optimizing a Trainium2 kernel written in Bass

```python
import jax, jax.numpy as jnp
from jax import lax
import numpy as np

D_MODEL = 1024
BATCH = 1
SEQ = 128
DEPTH = 1
DEC_BATCH = 1
DEC_SEQ = 512
PAST_LEN = 128

GRID_W = 64
RW_HD = 64
RW_W = D_MODEL // 2
RW_HEADS = RW_W // RW_HD
RW_DECAY_LORA = 64
RW_AAA_LORA = 64
RW_GATE_LORA = 128
RW_DECAY_SCALE = 0.606531
RW_LN_EPS = 64e-5
GLA_HEADS = 4
GLA_V_W = D_MODEL - RW_W
GLA_QK_W = GLA_V_W // 2
GLA_DV = GLA_V_W // GLA_HEADS
GLA_DK = GLA_QK_W // GLA_HEADS
GLA_GK_LORA = 16
GLA_GATE_NORM = 16.0
GLA_CHUNK = 32
N_GROUPS = 4
EXPERTS_PER_GROUP = 4
N_EXPERTS = N_GROUPS * EXPERTS_PER_GROUP
D_EXPERT = 256
TOP_K_IN_GROUP = 2
N_MOD = 6
EPS = 1e-6
IN_SPLITS = (RW_W, RW_W, RW_W, RW_DECAY_LORA, RW_DECAY_LORA, RW_AAA_LORA, RW_AAA_LORA, RW_GATE_LORA,
             GLA_QK_W, GLA_QK_W, GLA_V_W, GLA_V_W, GLA_GK_LORA, GLA_GK_LORA)
D_IN = RW_W * 3 + RW_DECAY_LORA * 2 + RW_AAA_LORA * 2 + RW_GATE_LORA + GLA_QK_W * 2 + GLA_V_W * 2 + GLA_GK_LORA * 2

kernel_name = "bidir_rwkv7_gla_hier_moe_prefix_ctx"

def split_cols(x, sizes):
    offsets = [int(o) for o in np.cumsum(sizes)[:-1]]
    return jnp.split(x, offsets, axis=-1)

def rmsnorm(x, g):
    xf = x.astype(jnp.float32)
    return xf * lax.rsqrt(jnp.mean(xf * xf, axis=-1, keepdims=True) + EPS) * g.astype(jnp.float32)

def short_conv(x, w, grid):
    B, T, C = x.shape
    w = w.astype(jnp.float32)
    if grid:
        rows = T // GRID_W
        xg = jnp.pad(x.reshape(B, rows, GRID_W, C), ((0, 0), (1, 1), (1, 1), (0, 0)))
        out = sum(xg[:, i:i + rows, j:j + GRID_W, :] * w[i, j] for i in range(3) for j in range(3))
        return out.reshape(B, T, C)
    xp = jnp.pad(x, ((0, 0), (1, 1), (0, 0)))
    return sum(xp[:, j:j + T, :] * w[1, j] for j in range(3))

def rwkv_scan(r, w, k, a_vec, b_vec, v, s0, reverse):
    def step(S, inp):
        r_t, w_t, k_t, a_t, b_t, v_t = inp
        sa = jnp.einsum('bhvk,bhk->bhv', S, a_t)
        S = S * w_t[:, :, None, :] + sa[..., None] * b_t[:, :, None, :] + v_t[..., None] * k_t[:, :, None, :]
        return S, jnp.einsum('bhvk,bhk->bhv', S, r_t)
    xs = tuple(jnp.moveaxis(t, 1, 0) for t in (r, w, k, a_vec, b_vec, v))
    s_fin, ys = lax.scan(step, s0, xs, reverse=reverse)
    return jnp.moveaxis(ys, 0, 1), s_fin

def rwkv_mixer(r, k, v, lw, la, lg, s0, grid, p):
    B, T, _ = r.shape
    heads = lambda t: t.reshape(B, T, RW_HEADS, RW_HD)
    rkv = short_conv(jnp.concatenate([r, k, v], axis=-1), p['rw_conv'], grid)
    r, k, v = jnp.split(rkv, 3, axis=-1)
    g = jax.nn.sigmoid(lg) @ p['rw_g2']
    kk = heads(k * p['rw_k_k'])
    kk = kk * lax.rsqrt(jnp.sum(kk * kk, axis=-1, keepdims=True) + EPS)
    rh, kh, vh = heads(r), heads(k), heads(v)
    s0 = s0.astype(jnp.float32)
    ys, finals = [], []
    for d in range(2):
        w = jnp.exp(-RW_DECAY_SCALE * jax.nn.sigmoid(p['rw_w0'][d] + jnp.tanh(lw[d]) @ p['rw_w2'][d]))
        a = jax.nn.sigmoid(p['rw_a0'][d] + la[d] @ p['rw_a2'][d])
        kd = heads(k * (1.0 + (a - 1.0) * p['rw_k_a']))
        y, s_fin = rwkv_scan(rh, heads(w), kd, -kk, kk * heads(a), vh, s0[:, d], reverse=(d == 1))
        ys.append(y)
        finals.append(s_fin)
    y = ys[0] + ys[1]
    mu = jnp.mean(y, axis=-1, keepdims=True)
    var = jnp.mean(jnp.square(y - mu), axis=-1, keepdims=True)
    yn = ((y - mu) * lax.rsqrt(var + RW_LN_EPS)).reshape(B, T, RW_W) * p['rw_ln_w'] + p['rw_ln_b']
    bonus = (jnp.sum(rh * kh * p['rw_r_k'], axis=-1, keepdims=True) * vh).reshape(B, T, RW_W)
    return (yn + bonus) * g, jnp.stack(finals, axis=1)

def gla_chunk_scan(q, k, v, gk, s0):
    B, T = q.shape[:2]
    nc = T // GLA_CHUNK
    chunk = lambda t: jnp.moveaxis(t.reshape(B, nc, GLA_CHUNK, *t.shape[2:]), 1, 0)
    mask = np.tril(np.ones((GLA_CHUNK, GLA_CHUNK), dtype=bool))[None, :, :, None, None]

    def step(S, inp):
        qc, kc, vc, gc = inp
        bcum = jnp.cumsum(gc, axis=1)
        diff = bcum[:, :, None] - bcum[:, None, :]
        decay = jnp.where(mask, jnp.exp(jnp.where(mask, diff, 0.0)), 0.0)
        A = jnp.einsum('bihd,bjhd,bijhd->bhij', qc, kc, decay)
        o = jnp.einsum('bhij,bjhv->bihv', A, vc) + jnp.einsum('bihd,bhdv->bihv', qc * jnp.exp(bcum), S)
        blast = bcum[:, -1]
        S = S * jnp.exp(blast)[..., None] + jnp.einsum('bjhd,bjhv->bhdv', kc * jnp.exp(blast[:, None] - bcum), vc)
        return S, o

    s_fin, o = lax.scan(step, s0, tuple(chunk(t) for t in (q, k, v, gk)))
    return jnp.moveaxis(o, 0, 1).reshape(B, T, GLA_HEADS, GLA_DV), s_fin

def gla_mixer(q, k, v, og, lgk, s0, p):
    B, T, _ = q.shape
    qh = q.reshape(B, T, GLA_HEADS, GLA_DK) * (GLA_DK ** -0.5)
    kh = k.reshape(B, T, GLA_HEADS, GLA_DK)
    vh = v.reshape(B, T, GLA_HEADS, GLA_DV)
    s0 = s0.astype(jnp.float32)
    outs, finals = [], []
    for d in range(2):
        gk = (jax.nn.log_sigmoid(lgk[d] @ p['gla_gk2'][d] + p['gla_gk_b'][d]) / GLA_GATE_NORM).reshape(B, T, GLA_HEADS, GLA_DK)
        if d == 0:
            o, s_fin = gla_chunk_scan(qh, kh, vh, gk, s0[:, d])
        else:
            o, s_fin = gla_chunk_scan(qh[:, ::-1], kh[:, ::-1], vh[:, ::-1], gk[:, ::-1], s0[:, d])
            o = o[:, ::-1]
        outs.append(o)
        finals.append(s_fin)
    o = rmsnorm(outs[0] + outs[1], p['gla_norm_g']).reshape(B, T, GLA_V_W)
    return o * jax.nn.silu(og), jnp.stack(finals, axis=1)

def hier_moe(h, p):
    B, T, D = h.shape
    hf = h.reshape(B * T, D)
    n_tok = hf.shape[0]
    g_logits = (hf @ p['moe_w_group'] + p['moe_b_group']).astype(jnp.float32)
    g_prob = jax.nn.softmax(g_logits, axis=-1)
    g_idx = jnp.argmax(g_logits, axis=-1)
    g_w = jnp.take_along_axis(g_prob, g_idx[:, None], axis=1)
    e_logits = (hf @ p['moe_w_expert'] + p['moe_b_expert']).astype(jnp.float32).reshape(n_tok, N_GROUPS, EXPERTS_PER_GROUP)
    e_sel = jnp.take_along_axis(e_logits, g_idx[:, None, None], axis=1)[:, 0]
    top_v, top_i = lax.top_k(jax.nn.softmax(e_sel, axis=-1), TOP_K_IN_GROUP)
    wts = g_w * top_v / jnp.sum(top_v, axis=-1, keepdims=True)
    e_idx = g_idx[:, None] * EXPERTS_PER_GROUP + top_i
    combine = jnp.sum(jax.nn.one_hot(e_idx, N_EXPERTS, dtype=jnp.float32) * wts[..., None], axis=1)
    up = jnp.einsum('td,edf->tef', hf, p['moe_w1'])
    gate = jnp.einsum('td,edf->tef', hf, p['moe_w3'])
    act = jax.nn.silu(gate) * up * combine[:, :, None]
    return jnp.einsum('tef,efd->td', act, p['moe_w2']).reshape(B, T, D)

def trunk_layer(x, cond, s_rw0, s_gla0, grid, p):
    B = x.shape[0]
    mod = (jax.nn.silu(cond.astype(jnp.float32)) @ p['w_ada'] + p['b_ada']).reshape(B, N_MOD, D_MODEL)
    sh1, sc1, ga1, sh2, sc2, ga2 = [mod[:, i][:, None, :] for i in range(N_MOD)]
    h = rmsnorm(x, p['norm1_g']) * (1.0 + sc1) + sh1
    (r, k, v, lw_f, lw_b, la_f, la_b, lg, q_g, k_g, v_g, og, lgk_f, lgk_b) = split_cols(h @ p['w_in'], IN_SPLITS)
    y_rw, s_rw = rwkv_mixer(r, k, v, (lw_f, lw_b), (la_f, la_b), lg, s_rw0, grid, p)
    y_gla, s_gla = gla_mixer(q_g, k_g, v_g, og, (lgk_f, lgk_b), s_gla0, p)
    mix = jnp.concatenate([y_rw, y_gla], axis=-1) @ p['w_out']
    x = x + (ga1 * mix).astype(x.dtype)
    h2 = rmsnorm(x, p['norm2_g']) * (1.0 + sc2) + sh2
    x = x + (ga2 * hier_moe(h2, p)).astype(x.dtype)
    return x, s_rw, s_gla

def setup_inputs(seed: int = 0) -> dict:
    key = jax.random.key(seed)
    ks = jax.random.split(key, 40)
    nrm = lambda i, shape, s: jax.random.normal(ks[i], shape, jnp.float32) * s
    L = DEPTH
    return {
        'x_prompt': nrm(0, (BATCH, SEQ, D_MODEL), 1.0),
        'x_sample': nrm(1, (DEC_BATCH, DEC_SEQ, D_MODEL), 1.0),
        'state_rwkv': nrm(2, (DEC_BATCH, L, 2, RW_HEADS, RW_HD, RW_HD), 0.3),
        'state_gla': nrm(3, (DEC_BATCH, L, 2, GLA_HEADS, GLA_DK, GLA_DV), 0.3),
        'c': nrm(4, (DEC_BATCH, D_MODEL), 1.0),
        'c_ctx': nrm(5, (D_MODEL,), 1.0),
        'norm1_g': 1.0 + nrm(6, (L, D_MODEL), 0.02),
        'norm2_g': 1.0 + nrm(7, (L, D_MODEL), 0.02),
        'w_ada': nrm(8, (L, D_MODEL, N_MOD * D_MODEL), 0.5 * D_MODEL ** -0.5),
        'b_ada': nrm(9, (L, N_MOD * D_MODEL), 0.02),
        'w_in': nrm(10, (L, D_MODEL, D_IN), D_MODEL ** -0.5),
        'w_out': nrm(11, (L, RW_W + GLA_V_W, D_MODEL), (RW_W + GLA_V_W) ** -0.5),
        'rw_conv': nrm(12, (L, 3, 3, 3 * RW_W), 1.0 / 3.0),
        'rw_w0': nrm(13, (L, 2, RW_W), 0.5),
        'rw_w2': nrm(14, (L, 2, RW_DECAY_LORA, RW_W), 0.5 * RW_DECAY_LORA ** -0.5),
        'rw_a0': nrm(15, (L, 2, RW_W), 0.5),
        'rw_a2': nrm(16, (L, 2, RW_AAA_LORA, RW_W), 0.5 * RW_AAA_LORA ** -0.5),
        'rw_g2': nrm(17, (L, RW_GATE_LORA, RW_W), RW_GATE_LORA ** -0.5),
        'rw_k_k': 0.85 + nrm(18, (L, RW_W), 0.05),
        'rw_k_a': 1.0 + nrm(19, (L, RW_W), 0.05),
        'rw_r_k': nrm(20, (L, RW_HEADS, RW_HD), 0.1),
        'rw_ln_w': 1.0 + nrm(21, (L, RW_W), 0.02),
        'rw_ln_b': nrm(22, (L, RW_W), 0.02),
        'gla_gk2': nrm(23, (L, 2, GLA_GK_LORA, GLA_QK_W), 0.5 * GLA_GK_LORA ** -0.5),
        'gla_gk_b': 1.0 + nrm(24, (L, 2, GLA_QK_W), 0.5),
        'gla_norm_g': 1.0 + nrm(25, (L, GLA_DV), 0.02),
        'moe_w_group': nrm(26, (L, D_MODEL, N_GROUPS), D_MODEL ** -0.5),
        'moe_b_group': nrm(27, (L, N_GROUPS), 0.01),
        'moe_w_expert': nrm(28, (L, D_MODEL, N_EXPERTS), D_MODEL ** -0.5),
        'moe_b_expert': nrm(29, (L, N_EXPERTS), 0.01),
        'moe_w1': nrm(30, (L, N_EXPERTS, D_MODEL, D_EXPERT), D_MODEL ** -0.5),
        'moe_w3': nrm(31, (L, N_EXPERTS, D_MODEL, D_EXPERT), D_MODEL ** -0.5),
        'moe_w2': nrm(32, (L, N_EXPERTS, D_EXPERT, D_MODEL), D_EXPERT ** -0.5),
        'final_g': 1.0 + nrm(33, (D_MODEL,), 0.02),
    }

def reference(x_prompt, x_sample, state_rwkv, state_gla, c, c_ctx, norm1_g, norm2_g, w_ada, b_ada, w_in, w_out,
              rw_conv, rw_w0, rw_w2, rw_a0, rw_a2, rw_g2, rw_k_k, rw_k_a, rw_r_k, rw_ln_w, rw_ln_b,
              gla_gk2, gla_gk_b, gla_norm_g, moe_w_group, moe_b_group, moe_w_expert, moe_b_expert,
              moe_w1, moe_w3, moe_w2, final_g):
    def layer_params(l):
        return {'norm1_g': norm1_g[l], 'norm2_g': norm2_g[l], 'w_ada': w_ada[l], 'b_ada': b_ada[l],
                'w_in': w_in[l], 'w_out': w_out[l], 'rw_conv': rw_conv[l], 'rw_w0': rw_w0[l], 'rw_w2': rw_w2[l],
                'rw_a0': rw_a0[l], 'rw_a2': rw_a2[l], 'rw_g2': rw_g2[l], 'rw_k_k': rw_k_k[l], 'rw_k_a': rw_k_a[l],
                'rw_r_k': rw_r_k[l], 'rw_ln_w': rw_ln_w[l], 'rw_ln_b': rw_ln_b[l], 'gla_gk2': gla_gk2[l],
                'gla_gk_b': gla_gk_b[l], 'gla_norm_g': gla_norm_g[l], 'moe_w_group': moe_w_group[l],
                'moe_b_group': moe_b_group[l], 'moe_w_expert': moe_w_expert[l], 'moe_b_expert': moe_b_expert[l],
                'moe_w1': moe_w1[l], 'moe_w3': moe_w3[l], 'moe_w2': moe_w2[l]}

    b_ctx = x_prompt.shape[0]
    ctx_cond = jnp.broadcast_to(c_ctx[None, :], (b_ctx, D_MODEL))
    x = x_prompt
    rw_states, gla_states = [], []
    for l in range(DEPTH):
        zeros_rw = jnp.zeros((b_ctx, 2, RW_HEADS, RW_HD, RW_HD), jnp.float32)
        zeros_gla = jnp.zeros((b_ctx, 2, GLA_HEADS, GLA_DK, GLA_DV), jnp.float32)
        x, s_rw, s_gla = trunk_layer(x, ctx_cond, zeros_rw, zeros_gla, False, layer_params(l))
        rw_states.append(s_rw)
        gla_states.append(s_gla)
    y_prompt = rmsnorm(x, final_g).astype(x_prompt.dtype)
    new_state_rwkv = jnp.stack(rw_states, axis=1)
    new_state_gla = jnp.stack(gla_states, axis=1)

    xs = x_sample
    for l in range(DEPTH):
        xs, _, _ = trunk_layer(xs, c, state_rwkv[:, l], state_gla[:, l], True, layer_params(l))
    y_sample = rmsnorm(xs, final_g).astype(x_sample.dtype)
    return (y_prompt, y_sample, new_state_rwkv, new_state_gla)


_drawn_inputs = setup_inputs


def setup_inputs(seed=0):
    import zlib

    import numpy as np

    out = dict(_drawn_inputs(seed))
    spreads = {}
    factors = {'state_rwkv': 8.0,
     'state_gla': 8.0,
     'norm2_g': 4.752,
     'rw_k_k': 4.494,
     'rw_ln_w': 8.0,
     'rw_ln_b': 8.0,
     'gla_norm_g': 8.0,
     'moe_b_group': 8.0,
     'moe_b_expert': 8.0,
     'final_g': 2.839}
    for name, (base, spread) in spreads.items():
        noise = np.random.default_rng([zlib.crc32(name.encode()), seed]).standard_normal(out[name].shape)
        drawn = base * np.exp(spread * noise) if base else spread * noise
        out[name] = __import__('jax').numpy.asarray(drawn.astype(out[name].dtype))
    for name, factor in factors.items():
        out[name] = (out[name] * factor).astype(out[name].dtype)
    return out
```

```python
import concourse.bass as bass
from concourse import mybir
from contextlib import ExitStack


def trunk_program(nc, x_prompt, x_sample, state_rwkv, state_gla, c, c_ctx, norm1_g, norm2_g, w_ada, b_ada,
                  w_in, w_out, rw_conv, rw_w0, rw_w2, rw_a0, rw_a2, rw_g2, rw_k_k, rw_k_a, rw_r_k,
                  rw_ln_w, rw_ln_b, gla_gk2, gla_gk_b, gla_norm_g, moe_w_group, moe_b_group,
                  moe_w_expert, moe_b_expert, moe_w1, moe_w3, moe_w2, final_g,
                  y_prompt, y_sample, new_state_rwkv, new_state_gla):
    f32 = mybir.dt.float32
    i32 = mybir.dt.int32
    u32 = mybir.dt.uint32
    ALU = mybir.AluOpType
    ACT = mybir.ActivationFunctionType
    AXX = mybir.AxisListType.X

    P = 128
    D = x_prompt.shape[2]
    KT = D // P
    CTX = x_prompt.shape[1]
    LAT = x_sample.shape[1]
    NT = (CTX + LAT) // P
    T = CTX + LAT
    GW = 64
    GH = LAT // GW
    RW = rw_ln_w.shape[1]
    HD = rw_r_k.shape[2]
    RC = RW // P
    NH = RW // HD
    DV = gla_norm_g.shape[1]
    GH_N = RW // DV
    GQ = gla_gk2.shape[3]
    GC = GQ // P
    LORA = rw_w2.shape[2]
    GKL = gla_gk2.shape[2]
    NMOD = w_ada.shape[2] // D
    NE = moe_w1.shape[1]
    NG = moe_w_group.shape[2]
    EPG = NE // NG
    F = moe_w1.shape[3]
    FT = F // P
    CH = 64
    EPS = 1e-6
    LN_EPS = 64e-5
    DECAY = -0.606531
    CLAMP = 80.0
    oR, oK, oV = 0, RW, 2 * RW
    oLW, oLA, oLG = 3 * RW, 3 * RW + 2 * LORA, 3 * RW + 4 * LORA
    oQG = oLG + P
    oVG = oQG + 2 * GQ
    oOG = oVG + RW
    oLGK = oOG + RW

    ctx = ExitStack()
    with ctx:
        def sb(name, n, parts=P):
            return ctx.enter_context(nc.sbuf_tensor(name, [parts, n], f32))

        def sem(name):
            return ctx.enter_context(nc.semaphore(name))

        SLAB = KT * 512
        RING = 2
        RAWL = (GH + 2) * (GW + 2)
        RAW = RAWL + CTX + 2
        region0 = sb("region0", RING * SLAB + 2 * RAW + 4)
        region1 = sb("region1", KT * T + 2 * GC * T + 2 * GC * T)
        region2 = sb("region2", NT * RW)
        region3 = sb("region3", NT * D)
        rk_r = sb("rk_r", 2 * RC * T)
        kk_b = sb("kk_b", RC * T)
        vtok_b = sb("vtok_b", NT * RW)
        cl_b = sb("cl_b", 2 * RC * T)
        lora_b = sb("lora_b", 3 * T)
        yg_b = sb("yg_b", NT * RW)
        ident = sb("ident", P)
        blk = sb("blk", P)
        mask = sb("mask", 2 * 2 * HD)
        maskD = sb("maskD", 2 * 2 * HD)
        maskA = sb("maskA", 2 * 3 * HD)
        w2_sb = sb("w2_sb", RW)
        a2_sb = sb("a2_sb", RW)
        gk2_sb = sb("gk2_sb", GQ)
        NV1 = NMOD * KT + 2 * KT + 2 * RC * 2 + 3 * RC + 2 * GC
        NV2 = 9 * 3 * RC
        vec = sb("vec", NV1 + NV2 + 2 * KT)
        mod = sb("mod", NMOD * KT * 2)
        gsc = sb("gsc", 2 * KT * 2)
        bonus = sb("bonus", NT * NH)
        small = sb("small", 128)
        identh = sb("identh", HD)

        ring = region0[:, 0:RING * SLAB].rearrange("p (s k n) -> p s k n", s=RING, k=KT)
        raw = region0[:, RING * SLAB:RING * SLAB + 2 * RAW].rearrange("p (b n) -> p b n", b=2)
        hT = region1[:, 0:KT * T].rearrange("p (k t) -> p k t", k=KT)
        o = KT * T
        qk_g = region1[:, o:o + 2 * GC * T].rearrange("p (c t) -> p c t", t=T)
        gcl = region1[:, o + 2 * GC * T:o + 4 * GC * T].rearrange("p (d c t) -> p d c t", d=2, t=T)
        vg = region2[:, :].rearrange("p (t n) -> p t n", t=NT)
        x_sb = region3[:, :].rearrange("p (t n) -> p t n", t=NT)
        sq = region3[:, 0:RC * T].rearrange("p (c t) -> p c t", t=T)
        vT = region3[:, RC * T:2 * RC * T].rearrange("p (c t) -> p c t", t=T)
        aa = region3[:, :].rearrange("p (d c t) -> p d c t", d=2, t=T)
        rT = rk_r[:, 0:RC * T].rearrange("p (c t) -> p c t", t=T)
        kT = rk_r[:, RC * T:].rearrange("p (c t) -> p c t", t=T)
        kkT = kk_b[:, :].rearrange("p (c t) -> p c t", t=T)
        vtok = vtok_b[:, :].rearrange("p (t n) -> p t n", t=NT)
        cl = cl_b[:, :].rearrange("p (d c t) -> p d c t", d=2, t=T)
        prod = cl_b[:, 0:RC * T].rearrange("p (c t) -> p c t", t=T)
        goacc = cl_b[:, RC * T:].rearrange("p (t n) -> p t n", t=NT)
        tlw = lora_b[:, 0:T]
        laT = lora_b[:, T:2 * T]
        slg = lora_b[:, 2 * T:3 * T]
        yg = yg_b[:, :].rearrange("p (t n) -> p t n", t=NT)
        vb_ada = 0
        vn1 = NMOD * KT
        vn2 = vn1 + KT
        vw0 = vn2 + KT
        va0 = vw0 + 2 * RC
        vkk = va0 + 2 * RC
        vka = vkk + RC
        vrk = vka + RC
        vgb = vrk + RC
        vcv = NV1
        vcond = NV1 + NV2
        modv = mod[:, :].rearrange("p (b c) -> p b c", c=2)
        gscv = gsc[:, :].rearrange("p (m b c) -> p m b c", m=2, c=2)
        condv = vec[:, vcond:vcond + 2 * KT].rearrange("p (c k) -> p c k", c=2)
        eps6 = small[:, 0:1]
        epsln = small[:, 1:2]
        oneka = small[:, 4:4 + RC]
        negka = small[:, 22:22 + RC]
        ssum = small[:, 8:8 + NT]
        rstd = small[:, 16:16 + NT]
        scond = small[:, 32:32 + 2 * KT]
        condt = scond.rearrange("p (c k) -> p c k", c=2)
        stmp = small[:, 48:48 + 2 * KT]

        pcs = small[:, 64:80].rearrange("p (d h c) -> p d h c", d=2, c=2)

        GW_N = 2400

        def gla_view(d, off, n):
            return region3[:, d * GW_N + off:d * GW_N + off + n]

        class G:
            pass
        gws = []
        for d in range(2):
            g = G()
            g.q = gla_view(d, 0, 256).rearrange("p (c t) -> p c t", c=GC)
            g.k = gla_view(d, 256, 256).rearrange("p (c t) -> p c t", c=GC)
            g.ktok = gla_view(d, 512, 256).rearrange("p (h k) -> p h k", h=GH_N)
            g.sT = gla_view(d, 768, 256).rearrange("p (h i) -> p h i", h=GH_N)
            g.df = gla_view(d, 1024, 256)
            g.e1 = gla_view(d, 1280, 256)
            g.e2 = gla_view(d, 1536, 256)
            g.m = gla_view(d, 1792, 4).rearrange("p (c j) -> p c j", c=GC)
            g.em = gla_view(d, 1796, 4).rearrange("p (c j) -> p c j", c=GC)
            g.pc = gla_view(d, 1800, 4).rearrange("p (c j) -> p c j", c=GC)
            g.kv = gla_view(d, 1808, 512).rearrange("p (c j v) -> p c j v", c=GC, j=2)
            gws.append(g)
        GM = region1[:, 1280:1280 + 3584].rearrange("p (n d c v) -> p n d c v", d=2, c=GC, v=DV)
        gng = region1[:, 1280 + 3584:1280 + 3584 + DV]
        smask = region1[:, 0:2 * T].rearrange("p (d t) -> p d t", d=2)
        gmask = lora_b[:, 0:2 * T].rearrange("p (d t) -> p d t", d=2)

        segs = []
        for d, reg in enumerate((region0, region1)):
            g = G()

            def view(off, n, pat=None, **kw):
                v = reg[:, off:off + n]
                return v.rearrange(pat, **kw) if pat else v
            g.AR = view(0, 1024, "p (a h c i) -> p h c a i", h=RC, c=2, a=2)
            g.b = view(1024, 512, "p (h t) -> p h t", h=RC)
            g.k = view(1536, 512, "p (h t) -> p h t", h=RC)
            g.WU = view(1024, 1024, "p (h n) -> p h n", h=NH)
            g.X = view(2048, 1024, "p (h n) -> p h n", h=NH)
            g.t2 = view(2048, 512, "p (h t) -> p h t", h=RC)
            g.B3 = view(3072, 1536, "p (a h i) -> p a h i", a=3, h=NH)
            g.ktok = view(4608, 512, "p (h k) -> p h k", h=NH)
            g.K2 = view(5120, 1024, "p (a h i) -> p a h i", a=2, h=NH)
            g.A3 = view(6144, 1536, "p (a h i) -> p a h i", a=3, h=NH)
            g.GT = view(6144, 512, "p (h c i) -> p h c i", h=RC, c=2)
            g.QT = view(6656, 512, "p (h c i) -> p h c i", h=RC, c=2)
            g.H = view(7168, 512, "p (c h i) -> p c h i", c=2, h=RC)
            g.D2 = view(7680, 512, "p (h i) -> p h i", h=NH)
            g.D2t = view(8192, 512, "p (h i) -> p h i", h=NH)
            g.X0 = view(8704, 512, "p (h i) -> p h i", h=NH)
            g.X1 = view(9216, 512, "p (h i) -> p h i", h=NH)
            g.E1 = view(7680, 528, "p (h i) -> p h i", h=2 * RC)
            g.E2 = view(8208, 512, "p (h t) -> p h t", h=RC)
            g.t1 = view(8720, 512, "p (h t) -> p h t", h=RC)
            g.tmp = view(7680, 256, "p (h v) -> p h v", h=RC)
            segs.append(g)
        MR = lora_b[:, 0:1024].rearrange("p (n d h v) -> p n d h v", n=2, d=2, h=RC)
        MM = region1[:, 9728:10240].rearrange("p (d h v) -> p d h v", d=2, h=RC)
        s0buf = region2[0:HD, 512:512 + 2 * RW].rearrange("v (d n) -> v d n", d=2)
        stbuf = region2[0:HD, 1536:1536 + 2 * RW].rearrange("v (d n) -> v d n", d=2)
        yacc = region2[:, :].rearrange("p (t n) -> p t n", t=NT)

        gbuf = region1[:, 0:6 * D].rearrange("p (v c n) -> p v c n", v=3, c=2)
        xt = region1[:, 6 * D:7 * D]
        ya = region1[:, 7 * D:7 * D + RW]
        rs8 = small[:, 116:124]
        ss1 = small[:, 28:29]
        grs20 = small[:, 84:84 + NT * GH_N]
        sqj = region1[:, 7 * D + RW:7 * D + 2 * RW]
        yT = region1[:, 8 * D:9 * D].rearrange("p (k t) -> p k t", k=KT)
        h2 = region1[:, 9 * D:10 * D]
        lnw = region0[:, RING * SLAB:RING * SLAB + RW]
        lnb = region0[:, RING * SLAB + RW:RING * SLAB + 2 * RW]
        g2_sb = region0[:, RING * SLAB + 2 * RW:RING * SLAB + 3 * RW]
        NR = NG + NE
        wr = w2_sb[:, 0:KT * NR].rearrange("p (k n) -> p k n", k=KT)
        br = w2_sb[:, KT * NR:KT * NR + NR]
        lgt = w2_sb[:, 200:200 + NT * NR].rearrange("p (t n) -> p t n", t=NT)
        picked = w2_sb[:, 304:304 + NT * NE]
        picked_v = picked.rearrange("p (t n) -> p t n", t=NT)
        rtmp = w2_sb[:, 384:384 + NT * NE].rearrange("p (t n) -> p t n", t=NT)
        slot0 = w2_sb[:, 464:464 + NE]
        tokid = w2_sb[:, 480:480 + NT]
        upper = maskA[:, 0:P]
        ones = maskA[:, P:2 * P]
        iota = maskA[:, 2 * P:3 * P]
        onehot = vtok_b[:, 0:2 * NT * P].rearrange("p (j t s) -> p j t s", j=2, t=NT)
        rt = a2_sb[:, :]
        fg = kk_b[:, 0:D]
        junk = kk_b[:, D:2 * D]
        x1 = region3[:, :].rearrange("p (t n) -> p t n", t=NT)
        xg = rk_r[:, 0:3 * D].rearrange("p (s n) -> p s n", s=3)
        xgT = rk_r[:, 3 * D:5 * D].rearrange("p (s k t) -> p s k t", s=2, k=KT)
        yg2 = rk_r[:, 0:4 * D].rearrange("p (s j n) -> p s j n", s=2, j=2)
        yo = cl_b[:, 0:2 * D].rearrange("p (s n) -> p s n", s=2)
        idx = ctx.enter_context(nc.sbuf_tensor("slot_tokens", [P, NE], u32))
        pos = ctx.enter_context(nc.sbuf_tensor("pick_slots", [P, 2 * NT], u32))
        most = ctx.enter_context(nc.sbuf_tensor("largest_count", [1, 1], i32))
        h2_dram = nc.dram_tensor("h2_rows_dram", (T, D), f32, kind="Internal").ap()
        ys_dram = nc.dram_tensor("expert_rows_dram", (NE * P, D), f32, kind="Internal").ap()
        h2T = rk_r[:, :].rearrange("p (k t) -> p k t", k=KT)
        acc = cl_b[:, :].rearrange("p (t n) -> p t n", t=NT)
        w2r = region1[:, 0:4 * D].rearrange("p (s f n) -> p s f n", s=2, f=FT)
        ga2b = region1[:, 4 * D:6 * D].rearrange("p (c n) -> p c n", c=2)
        sg = region1[:, 6 * D:6 * D + 2 * F].rearrange("p (s f) -> p s f", s=2)
        ac = region1[:, 7 * D:7 * D + 2 * F].rearrange("p (s f) -> p s f", s=2)
        aT = region1[:, 8 * D:8 * D + 2 * F].rearrange("p (s f t) -> p s f t", s=2, f=FT)

        NB = 8
        PS = [ctx.enter_context(nc.psum_tensor(f"bank{i}", [P, 512], f32)) for i in range(NB)]
        filled = sem("filled")
        drained = [sem(f"drained{i}") for i in range(NB)]

        PAIRS = [(0, 0)] + [(i, NT - i) for i in range(1, NT)]

        jobs = [("rows",)]
        for n in range(4):
            jobs += [("ada", n), ("adaT", n)]
        jobs += [("hl", k) for k in range(KT)] + [("hc", 0), ("hc", 1)]
        chan = ["q0", "q1", "g0", "g1"]
        tail = [f"r{i}" for i in range(RC)] + [f"k{i}" for i in range(RC)] + [f"v{i}" for i in range(RC)] + ["lw", "la", "lg"]
        for n in chan:
            jobs += [("pl", n), ("pc", n)]
        jobs += [("vg", t) for t in range(NT)] + [("og", t) for t in range(NT)]
        jobs += [("lgkl",), ("lgkc",)]
        jobs += [("gkl", d, i) for d in range(2) for i in range(GC)] + [("gkc",)]
        for n in tail:
            jobs += [("pl", n), ("pc", n)]
            if n == f"k{RC - 1}":
                jobs += [("kl", i) for i in range(RC)] + [("kc",), ("bonus",)]
            if n == f"v{RC - 1}":
                jobs += [("vt", t) for t in range(NT)]
        for p in range(NT):
            jobs += [("g1", p, d) for d in range(2)]
            for d in range(2):
                jobs += [("goA", p, d), ("gkv", p, d)]
            jobs += [("goB", p, 0), ("goB", p, 1)]
        for d in range(2):
            jobs += [("wl", d, i) for i in range(RC)] + [("wc", d)]
            jobs += [("al", d, i) for i in range(RC)] + [("ac", d)]
        for n in range(4, 2 * NMOD):
            jobs += [("ada", n), ("adaT", n)]
        SEG = ["tA", "tB", "tK"]
        INV = ["D2", "D2t", "D4", "X2", "D4t", "X3", "D8t", "X4", "X4t", "Z1", "X5", "X5t", "Z2", "X6"]
        for p in range(NT):
            if p == 1:
                jobs += [("s0",)]
            for d in range(2):
                jobs += [(n, p, d) for n in ("b0", "k0", "A", "b1", "k1", "tA", "tB", "tK", "AV")]
            for n in INV:
                jobs += [(n, p, d) for d in range(2)]
            for d in range(2):
                jobs += [("WU", p, d, 0), ("WU", p, d, 1)]
            for d in range(2):
                jobs += [("G", p, d, 0), ("G", p, d, 1), ("H", p, d, 0), ("H", p, d, 1)]
            jobs += [("seq", p, d, 0) for d in range(2)]
            jobs += [("seq", p, d, 1) for d in range(2)]
            for d in range(2):
                jobs += [("Ya", p, d), ("Yb", p, d)]
            if p == 0:
                jobs += [("st", 0), ("st", 1)]
        jobs += [("rowb", v, cnd, h) for v in ("ga1", "sc2", "sh2") for cnd in range(2) for h in range(2)]
        for t in range(NT):
            jobs += [("gate", t), ("yT", t, 0), ("yT", t, 1), ("out", t, 0), ("out", t, 1),
                     ("hT2", t, 0), ("hT2", t, 1), ("router", t)]
        jobs += [("rowb", "ga2", cnd, h) for cnd in range(2) for h in range(2)]
        jobs += [("rank",)]
        for r in range(NT):
            jobs += [("ids", r)]
            for e in range(NE):
                i = r * NE + e
                if e == 0:
                    jobs += [("xT", i, 0), ("xT", i, 1)]
                jobs += [("ug", i)]
                if e < NE - 1:
                    jobs += [("xT", i + 1, 0), ("xT", i + 1, 1)]
                if e > 0:
                    jobs += [("dn", i - 1, 0), ("dn", i - 1, 1)]
                jobs += [("aT", i)]
            jobs += [("dn", i, 0), ("dn", i, 1)]
        J = {k: i for i, k in enumerate(jobs)}
        assert len(J) == len(jobs)

        def bank(key):
            return PS[J[key] % NB]

        def wait_filled(eng, *key):
            eng.wait_ge(filled, J[key] + 1)

        def wait_result(eng, *key):
            eng.wait_ge(drained[J[key] % NB], J[key] // NB + 1)

        slabs = [("ada", n) for n in range(4)] + ["qk", "vg", "og", "lgk", "r", "k", "v", "lora"] + \
                [("ada", n) for n in range(4, 2 * NMOD)]
        NS1 = len(slabs)
        slab_in = [sem(f"slab_in{i}") for i in range(RING)]

        s_small = sem("small_loads")
        s_x = sem("x_loads")
        s_const = sem("constants")
        s_xn = sem("xn_ready")
        s_cond = sem("cond_ready")
        s_g1 = sem("gain1_ready")
        s_adarow = sem("ada_rows")
        s_conv = sem("conv_done")
        s_kk = sem("kk_squares")
        s_prod = sem("bonus_products")
        s_lora = sem("lora_inputs")
        s_lgx = sem("gla_gates_in")
        s_lgt = sem("gla_gates_mid")
        s_gcl = sem("gla_cumsums")
        s_wx = sem("decay_in")
        s_wm = sem("decay_mid")
        s_cl = sem("decay_cumsums")
        s_dve = sem("vector_steps")
        s_act = sem("scalar_steps")
        s_pool = sem("pool_steps")

        block = ctx.enter_context(nc.Block())

        def steps(eng, chain):
            count = {}

            def tell(ins, s):
                count[s.name] = count.get(s.name, 0) + 1
                ins.then_inc(s, 1)
                eng.wait_ge(s, count[s.name])

            def own(ins):
                tell(ins, chain)

            def out_of(ins, *key):
                ins.then_inc(drained[J[key] % NB], 1)
                eng.wait_ge(drained[J[key] % NB], J[key] // NB + 1)
            return own, tell, out_of


        s_turn = sem("array_half_done")
        s_eps = sem("epsilons")
        s_ogx = sem("og_bounded")
        s_xnr = sem("x_normalised")
        s_bon = sem("bonus_inputs")
        s_gz = sem("gla_zero_states")
        s_g2 = sem("adaln_complete")
        s_X1 = sem("inverse_start")
        MCUR = [0] + [(p - 1) % 2 for p in range(1, NT)]
        lgkT = kk_b[0:48, 0:T]

        def adarow(n):
            return region0[0:2, RING * SLAB + (n % 2) * 512:RING * SLAB + (n % 2) * 512 + 512]
        rt_v, at_ = {}, 0
        for nme, shp in (("pref", (NG,)), ("hg", (NT, NG)), ("mg", (NT,)), ("gd", (NT, NG)), ("ge", (NT, NG)), ("sel", (NT, EPG, NG)),
                         ("es", (NT, EPG)), ("h1", (NT, EPG)), ("h2", (NT, EPG)), ("m", (NT,)), ("m1", (NT,)), ("m2", (NT,)),
                         ("E", (NT,)), ("w1", (NT,)), ("w2", (NT,)), ("o1", (NT, NE)), ("o2", (NT, NE)), ("rk", (2 * NT,)),
                         ("ps", (2 * NT,)), ("wt", (2 * NT,)), ("in", (2 * NT,)), ("ib", (2 * NT,)), ("wr", (2 * NT,)), ("mc", (1,))):
            n_ = 1
            for z in shp:
                n_ *= z
            v_ = a2_sb[:, at_:at_ + n_]
            if len(shp) == 2:
                v_ = v_.rearrange("p (t n) -> p t n", t=shp[0])
            if len(shp) == 3:
                v_ = v_.rearrange("p (t n m) -> p t n m", t=shp[0], n=shp[1])
            rt_v[nme] = v_
            at_ += n_
        LAST = {("ada", n): ("ada", n) for n in range(2 * NMOD)}
        LAST.update({"qk": ("pc", "g1"), "vg": ("vg", NT - 1), "og": ("og", NT - 1), "lgk": ("lgkc",), "r": ("pc", f"r{RC - 1}"),
                     "k": ("pc", f"k{RC - 1}"), "v": ("pc", f"v{RC - 1}"), "lora": ("pc", "lg")})
        s_condt = sem("condition_columns")
        s_rawz = sem("conv_borders_zero")
        s_sig = sem("silu_gate")
        s_gm = sem("gla_masks")
        s_kkn = sem("kk_normalised")
        s_gseg = sem("gla_exponents")
        s_gexp = sem("gla_exps")
        s_gq = sem("gla_qk_scaled")
        s_gM = sem("gla_decayed_states")
        s_gst = sem("gla_context_states")
        s_gin = sem("gla_states_loaded")
        s_gfin = sem("gla_sums")
        s_grs = sem("gla_rstd")
        s_gdone = sem("gla_done")
        s_seg = sem("segment_start")
        s_E = sem("segment_exps")
        s_t1 = sem("segment_products")
        s_f = sem("segment_k_factors")
        s_ops = sem("segment_operands")
        s_mst = sem("rwkv_state_steps")
        s_zero = sem("rwkv_zero_states")
        s_rin = sem("rwkv_states_loaded")
        s_rst = sem("rwkv_states_out")
        s_gout = sem("gla_states_out")
        s_wo = sem("late_loads")
        s_rwdone = sem("rwkv_done")
        s_y = sem("head_norm_stats")
        s_yr = sem("head_norm_rstd")
        s_ya = sem("rwkv_rows")
        s_xt = sem("x_again")
        s_x1 = sem("x1_rows")
        s_x1r = sem("x1_rstd")
        s_h2 = sem("h2_rows")
        s_rg = sem("router_in")
        s_rex = sem("router_exps")
        s_sg = sem("gate_exps")
        s_ac = sem("expert_acts")
        s_w13 = [sem(f"w13_in{i}") for i in range(2)]
        s_w2 = [sem(f"w2_in{i}") for i in range(2)]
        s_h2d = sem("h2_stored")
        s_tri = sem("routing_constants")
        s_pick = sem("picks_ready")
        s_most = sem("largest_count_ready")
        s_oh = sem("slot_onehots")
        s_idx = sem("slot_tokens_ready")
        s_xg = [sem(f"gathered{i}") for i in range(3)]
        s_ys = [sem(f"expert_rows_stored{i}") for i in range(2)]
        s_moe = sem("experts_done")
        s_yg = [sem(f"expert_rows_in{i}") for i in range(2)]
        s_dve2 = sem("vector_last_steps")
        s_act2 = sem("scalar_last_steps")
        s_pos = sem("pick_slots_ready")
        s_comb = sem("expert_rows_added")
        s_fin = sem("x1_complete")
        s_finr = sem("final_rstd")
        s_yout = sem("y_out")
        s_ydma = sem("y_stored")

        def first(p, d):
            return d == 0 if p == 0 else p < NT - p

        def rounds(eng, body):
            body(0)
            eng.wait_ge(s_most, 1)
            n = eng.value_load(most[0:1, 0:1], min_val=0, max_val=T)
            for r in range(1, NT):
                with eng.If(n > r * P):
                    body(r)

        def chunk(d, k):
            return k if d == 0 else 1 - k

        def bc(ap, axis, n):
            v = ap.unsqueeze(axis)
            shape = list(v.shape)
            shape[axis] = n
            return v.broadcast_to(shape)

        w_in_v = w_in[0].rearrange("(k p) n -> p k n", p=P)
        w_out_v = w_out[0].rearrange("(k p) n -> p k n", p=P)
        w_ada_v = w_ada[0].rearrange("(k p) n -> p k n", p=P)

        def slab_dmas(sp, i):
            what = slabs[i]
            s = i % RING
            if isinstance(what, tuple):
                n = what[1]
                sp.dma_start(ring[:, s], w_ada_v[:, :, n * 512:(n + 1) * 512]).then_inc(slab_in[s], 16)
                return
            lo, n = {"qk": (oQG, 512), "vg": (oVG, 512), "og": (oOG, 512), "lgk": (oLGK, 2 * GKL), "r": (oR, 512),
                     "k": (oK, 512), "v": (oV, 512), "lora": (oLW, 384)}[what]
            sp.dma_start(ring[:, s, :, 0:n], w_in_v[:, :, lo:lo + n]).then_inc(slab_in[s], 16)

        @block.sync
        def _(sp):
            rows1 = [(b_ada[0].rearrange("(r c) -> r c", c=P), NMOD * KT), (norm1_g[0].rearrange("(r c) -> r c", c=P), KT),
                     (norm2_g[0].rearrange("(r c) -> r c", c=P), KT),
                     (rw_w0[0].rearrange("d (r c) -> (d r) c", c=P), 2 * RC), (rw_a0[0].rearrange("d (r c) -> (d r) c", c=P), 2 * RC),
                     (rw_k_k[0].rearrange("(r c) -> r c", c=P), RC), (rw_k_a[0].rearrange("(r c) -> r c", c=P), RC),
                     (rw_r_k[0].rearrange("(r a) c -> r (a c)", a=2), RC), (gla_gk_b[0].rearrange("d (r c) -> (d r) c", c=P), 2 * GC)]
            at = 0
            for src, n in rows1:
                sp.dma_start(region1[at:at + n, 0:P], src).then_inc(s_small, 16)
                at += n
            sp.dma_start(region1[0:NV2, P:2 * P], rw_conv[0].rearrange("i j (r c) -> (i j r) c", c=P)).then_inc(s_small, 16)
            sp.dma_start(region1[0:KT, 2 * P:3 * P], c_ctx.rearrange("(r c) -> r c", c=P)).then_inc(s_small, 16)
            sp.dma_start(region1[KT:2 * KT, 2 * P:3 * P], c[0].rearrange("(r c) -> r c", c=P)).then_inc(s_small, 16)
            sp.dma_start(w2_sb[:, :], rw_w2[0].rearrange("d k n -> (d k) n")).then_inc(s_small, 16)
            sp.dma_start(a2_sb[:, :], rw_a2[0].rearrange("d k n -> (d k) n")).then_inc(s_small, 16)
            sp.dma_start(gk2_sb[0:GKL, :], gla_gk2[0, 0]).then_inc(s_small, 16)
            sp.dma_start(gk2_sb[32:32 + GKL, :], gla_gk2[0, 1]).then_inc(s_small, 16)
            sp.dma_start(x_sb[:, 0], x_prompt[0]).then_inc(s_x, 16)
            for t in range(1, NT):
                sp.dma_start(x_sb[:, t], x_sample[0, (t - 1) * P:t * P, :]).then_inc(s_x, 16)
            for i in range(NS1):
                if i >= RING:
                    wait_filled(sp, *LAST[slabs[i - RING]])
                slab_dmas(sp, i)
            sp.wait_ge(s_gdone, 1)
            for d in range(2):
                sp.dma_start(s0buf[:, d].rearrange("v (h k) -> v h k", h=NH), state_rwkv[0, 0, d].rearrange("h v k -> v h k")).then_inc(s_rin, 16)
            sp.wait_ge(s_rwdone, 1)
            sp.dma_start(lnw, rw_ln_w[0].partition_broadcast(P)).then_inc(s_wo, 16)
            sp.dma_start(lnb, rw_ln_b[0].partition_broadcast(P)).then_inc(s_wo, 16)
            sp.dma_start(g2_sb, rw_g2[0]).then_inc(s_wo, 16)
            sp.dma_start(wr[:, :, 0:NG], moe_w_group[0].rearrange("(k p) n -> p k n", p=P)).then_inc(s_wo, 16)
            sp.dma_start(wr[:, :, NG:NR], moe_w_expert[0].rearrange("(k p) n -> p k n", p=P)).then_inc(s_wo, 16)
            sp.dma_start(br[:, 0:NG], moe_b_group[0].partition_broadcast(P)).then_inc(s_wo, 16)
            sp.dma_start(br[:, NG:NR], moe_b_expert[0].partition_broadcast(P)).then_inc(s_wo, 16)
            sp.dma_start(fg, final_g.partition_broadcast(P)).then_inc(s_wo, 16)
            for h in range(2):
                sp.dma_start(ring[:, h], w_out_v[:, :, h * 512:(h + 1) * 512]).then_inc(s_wo, 16)
            sp.dma_start(xt, x_prompt[0]).then_inc(s_xt, 16)
            for t in range(NT):
                if t < NT - 1:
                    sp.wait_ge(s_x1, t + 1)
                    sp.dma_start(xt, x_sample[0, t * P:(t + 1) * P, :]).then_inc(s_xt, 16)
                sp.wait_ge(s_h2, t + 1)
                sp.dma_start(h2_dram[t * P:(t + 1) * P, :], h2).then_inc(s_h2d, 16)

            def load_experts(r):
                for e in range(NE):
                    i = r * NE + e
                    s = i % 2
                    if i < 2:
                        wait_filled(sp, "router", NT - 1)
                    else:
                        wait_filled(sp, "ug", i - 2)
                    sp.dma_start(ring[:, s, :, 0:F], moe_w1[0, e].rearrange("(k p) n -> p k n", p=P)).then_inc(s_w13[s], 16)
                    sp.dma_start(ring[:, s, :, F:2 * F], moe_w3[0, e].rearrange("(k p) n -> p k n", p=P)).then_inc(s_w13[s], 16)
                    if i >= 2:
                        wait_filled(sp, "dn", i - 2, 1)
                    sp.dma_start(w2r[:, s], moe_w2[0, e].rearrange("(f p) n -> p f n", p=P)).then_inc(s_w2[s], 16)
            rounds(sp, load_experts)
            for t in range(NT):
                sp.wait_ge(s_yout, t + 1)
                sp.dma_start(y_prompt[0] if t == 0 else y_sample[0, (t - 1) * P:t * P, :], acc[:, t]).then_inc(s_ydma, 16)
            sp.wait_ge(s_ydma, 16 * NT)

        @block.gpsimd
        def _(pool):
            own, tell, _o = steps(pool, s_pool)

            def select(ap, pattern, base, ch, op, fill=0.0):
                own(pool.affine_select(out=ap, in_=ap, compare_op=op, fill=fill, base=base, pattern=pattern, channel_multiplier=ch))
            own(pool.memset(ident[:, :], 0.0))
            select(ident[:, :], [[-1, P]], 0, 1, ALU.not_equal, 1.0)
            own(pool.memset(blk[:, :], 0.0))
            own(pool.memset(blk[0:HD, 0:HD], 1.0))
            own(pool.memset(blk[HD:P, HD:P], 1.0))
            own(pool.tensor_tensor(identh[:, :], ident[:, 0:HD], ident[:, HD:P], ALU.add))
            own(pool.memset(mask[:, :], 1.0))
            own(pool.memset(maskA[:, :], 1.0))
            mk = mask[:, :].rearrange("p (d a i) -> p d a i", d=2, a=2)
            mD = maskD[:, :].rearrange("p (d a i) -> p d a i", d=2, a=2)
            mA = maskA[:, :].rearrange("p (d a i) -> p d a i", d=2, a=3)
            for half in (slice(0, HD), slice(HD, P)):
                select(mk[half, 0, 0], [[1, HD]], -1, -1, ALU.is_ge)
                select(mk[half, 0, 1], [[1, HD]], 0, -1, ALU.is_ge)
                select(mk[half, 1, 0], [[-1, HD]], -1, 1, ALU.is_ge)
                select(mk[half, 1, 1], [[-1, HD]], 0, 1, ALU.is_ge)
                for d in range(2):
                    for a, w in ((0, 16), (1, 32)):
                        v = mA[half, d, a].rearrange("p (n w) -> p n w", w=w)
                        select(v, [[-w, HD // w], [0, w]], 0, 1, ALU.is_ge)
                        select(v, [[w, HD // w], [0, w]], w - 1, -1, ALU.is_ge)
            for d in range(2):
                own(pool.tensor_tensor(mD[:, d, 0], mk[:, d, 0], mA[:, d, 0], ALU.mult))
                own(pool.tensor_copy(mD[:, d, 1], mk[:, d, 1]))
                own(pool.tensor_tensor(mA[:, d, 2], mA[:, d, 2], mA[:, d, 1], ALU.subtract))
                own(pool.tensor_tensor(mA[:, d, 1], mA[:, d, 1], mA[:, d, 0], ALU.subtract))
                for a in range(3):
                    own(pool.tensor_tensor(mA[:, d, a], mA[:, d, a], mk[:, 1 - d, 0], ALU.mult))
            tell(pool.memset(small[:, 2:3], 1.0), s_const)
            pool.wait_ge(s_g1, 1)
            tell(pool.memset(region0[:, RING * SLAB:RING * SLAB + 2 * RAW], 0.0), s_rawz)
            pool.wait_ge(s_sig, 3)
            tell(pool.tensor_tensor(yg_b[:, :], yg_b[:, :], cl_b[:, RC * T:2 * RC * T], ALU.mult), s_sig)
            for i in range(RC):
                pool.wait_ge(s_kk, i + 1)
                tell(pool.tensor_tensor(sq[:, i], kkT[:, i], kkT[:, i], ALU.mult), s_prod)
            for p in range(NT):
                for d in range(2):
                    g, t = gws[d], PAIRS[p][d]
                    pool.wait_ge(s_gexp, 2 * p + d + 1)
                    if p >= 1:
                        wait_filled(pool, "goB", p - 1, 1)
                    own(pool.tensor_tensor(g.q, qk_g[:, 0:GC, t * P:(t + 1) * P], g.e1.rearrange("p (c t) -> p c t", c=GC), ALU.mult))
                    tell(pool.tensor_tensor(g.k, qk_g[:, GC:2 * GC, t * P:(t + 1) * P], g.e2.rearrange("p (c t) -> p c t", c=GC), ALU.mult), s_gq)
            for p in range(NT):
                for d in range(2):
                    g, t = segs[d], PAIRS[p][d]
                    tok = slice(t * P, (t + 1) * P)
                    pool.wait_ge(s_seg, 2 * p + d + 1)
                    tell(pool.tensor_tensor(g.t1, kkT[:, :, tok], aa[:, d, :, tok], ALU.mult), s_t1)
                    pool.wait_ge(s_f, 2 * p + d + 1)
                    tell(pool.tensor_tensor(g.t2, g.t2, kT[:, :, tok], ALU.mult), s_t1)
            pool.wait_ge(s_rwdone, 1)
            pool.wait_ge(s_wo, 160)
            own(pool.memset(upper, 1.0))
            select(upper, [[1, P]], -1, -1, ALU.is_ge)
            own(pool.memset(ones, 1.0))
            own(pool.iota(iota, [[1, P]], base=0, channel_multiplier=0, allow_small_or_imprecise_dtypes=True))
            own(pool.iota(slot0, [[P, NE]], base=0, channel_multiplier=0, allow_small_or_imprecise_dtypes=True))
            tell(pool.iota(tokid, [[P, NT]], base=0, channel_multiplier=1, allow_small_or_imprecise_dtypes=True), s_tri)

            def gather_rows(r):
                if r == 0:
                    pool.wait_ge(s_h2d, 16 * NT)
                else:
                    pool.wait_ge(s_comb, NT * r)
                pool.wait_ge(s_idx, r + 1)
                for e in range(NE):
                    i = r * NE + e
                    if i >= 3:
                        wait_filled(pool, "xT", i - 3, 1)
                    pool.indirect_dma_start(out=xg[:, i % 3], out_offset=None, in_=h2_dram,
                                            in_offset=bass.IndirectOffsetOnAxis(ap=idx[:, e:e + 1], axis=0)).then_inc(s_xg[i % 3], 16)
                pool.wait_ge(s_moe, r + 1)
                pool.wait_ge(s_pos, r + 1)
                for t in range(NT):
                    n = r * NT + t
                    if t >= 2:
                        pool.wait_ge(s_comb, n - 1)
                    for j in range(2):
                        pool.indirect_dma_start(out=yg2[:, t % 2, j], out_offset=None, in_=ys_dram,
                                                in_offset=bass.IndirectOffsetOnAxis(ap=pos[:, j * NT + t:j * NT + t + 1], axis=0)).then_inc(s_yg[t % 2], 16)
            rounds(pool, gather_rows)
        @block.scalar
        def _(act):
            own, tell, out_of = steps(act, s_act)

            def A(out, in_, func=ACT.Copy, **kw):
                return act.activation(out, in_, func, **kw)

            def copy_out(dst, key, src=None, scale=1.0):
                wait_filled(act, *key)
                src = bank(key)[:, :] if src is None else src
                out_of(A(dst, src, scale=scale), *key)

            act.preload_act_table_set("natural_log_exp_and_others")
            act.wait_ge(s_x, 16 * NT)
            act.wait_ge(s_eps, 1)
            for t in range(NT):
                own(A(kk_b[:, 0:D], x_sb[:, t], ACT.Square, accum_out=ssum[:, t:t + 1]))
            own(A(rstd, ssum, ACT.Ln, scale=1.0 / D, bias=eps6))
            tell(A(rstd, rstd, ACT.Exp, scale=-0.5), s_xn)
            wait_result(act, "rows")
            tell(A(stmp, vec[:, vcond:vcond + 2 * KT], ACT.Exp, scale=-1.0), s_cond)
            act.wait_ge(s_g1, 1)
            for k in range(0, KT, 2):
                wait_filled(act, "hl", k)
                out_of(A(hT[:, k, P:T], bank(("hl", k))[:, :], ACT.Identity, scale=gscv[:, 0, k, 1:2], bias=modv[:, k, 1:2]), "hl", k)
            wait_filled(act, "hc", 0)
            for k in range(KT // 2):
                ins = A(hT[:, k, 0:P], bank(("hc", 0))[:, k * P:(k + 1) * P], ACT.Identity, scale=gscv[:, 0, k, 0:1], bias=modv[:, k, 0:1])
                if k < KT // 2 - 1:
                    own(ins)
            out_of(ins, "hc", 0)
            for n, i in (("q0", 0), ("q1", 1), ("g0", GC), ("g1", GC + 1)):
                sc = HD ** -0.5 if n[0] == "q" else 1.0
                copy_out(qk_g[:, i, P:T], ("pl", n), scale=sc)
                copy_out(qk_g[:, i, 0:P], ("pc", n), bank(("pc", n))[:, 0:P], scale=sc)
            for t in range(NT):
                copy_out(vg[:, t], ("vg", t))
            act.wait_ge(s_ogx, 1)
            sgm = cl_b[:, RC * T:2 * RC * T]
            tell(A(sgm, yg_b[:, :], ACT.Exp, scale=-1.0), s_sig)
            tell(A(sgm, sgm, ACT.Ln, bias=1.0), s_sig)
            tell(A(sgm, sgm, ACT.Exp, scale=-1.0), s_sig)
            act.wait_ge(s_lgx, 1)
            glt = cl_b[:, 0:RC * T]
            own(A(glt, region1[:, KT * T + 2 * GC * T:KT * T + 4 * GC * T], ACT.Abs))
            own(A(glt, glt, ACT.Exp, scale=-1.0))
            tell(A(glt, glt, ACT.Ln, bias=1.0), s_lgt)
            act.wait_ge(s_rawz, 1)
            for c_, n in enumerate(tail[:3 * RC]):
                b = c_ % 2
                if c_ >= 2:
                    act.wait_ge(s_conv, c_ - 1)
                lat = raw[:, b, 0:RAWL].rearrange("p (y x) -> p y x", x=GW + 2)
                copy_out(lat[:, 1:GH + 1, 1:GW + 1], ("pl", n), bank(("pl", n))[:, :].rearrange("p (y x) -> p y x", x=GW))
                copy_out(raw[:, b, RAWL + 1:RAWL + 1 + P], ("pc", n), bank(("pc", n))[:, 0:P])
                if n == f"k{RC - 1}":
                    for i in range(RC):
                        wait_filled(act, "kl", i)
                        if i == 0:
                            wait_filled(act, "kc")
                        out_of(A(sq[:, i, P:T], bank(("kl", i))[:, :], ACT.Ln, bias=eps6), "kl", i)
                    out_of(A(sq[:, :, 0:P], bank(("kc",))[:, :].rearrange("p (c t) -> p c t", c=RC), ACT.Ln, bias=eps6), "kc")
                    tell(A(sq, sq, ACT.Exp, scale=-0.5), s_kkn)
                if n == f"v{RC - 1}":
                    for t in range(NT):
                        copy_out(vtok[:, t], ("vt", t))
            act.wait_ge(s_gcl, 1)
            copy_out(laT[:, P:T], ("pl", "la"))
            copy_out(laT[:, 0:P], ("pc", "la"), bank(("pc", "la"))[:, 0:P])
            act.wait_ge(s_lora, 1)
            own(A(tlw, tlw, ACT.Exp, scale=2.0))
            own(A(tlw, tlw, ACT.Ln, bias=1.0))
            tell(A(tlw, tlw, ACT.Exp, scale=-1.0), s_lgt)
            own(A(slg, slg, ACT.Exp, scale=-1.0))
            own(A(slg, slg, ACT.Ln, bias=1.0))
            tell(A(slg, slg, ACT.Exp, scale=-1.0), s_lgt)
            act.wait_ge(s_gz, 1)
            wait_filled(act, "pc", "lg")
            for d in range(2):
                for h in range(2):
                    act.dma_start(GM[h * HD:(h + 1) * HD, 1, d], state_gla[0, 0, d].rearrange("(c a) k v -> a k c v", a=2)[h]).then_inc(s_gin, 16)
            act.dma_start(gng, gla_norm_g[0].partition_broadcast(P)).then_inc(s_gin, 16)
            for p in range(NT):
                if p == 1:
                    act.wait_ge(s_gM, 2)
                    for d in range(2):
                        for h in range(2):
                            act.dma_start(new_state_gla[0, 0, d].rearrange("(c a) k v -> a k c v", a=2)[h], GM[h * HD:(h + 1) * HD, 0, d]).then_inc(s_gout, 16)
                for d in range(2):
                    g = gws[d]
                    act.wait_ge(s_gseg, 2 * p + d + 1)
                    own(A(g.e1, g.df, ACT.Exp, scale=1.0 / 16))
                    own(A(g.e2, g.df, ACT.Exp, scale=-1.0 / 16))
                    own(A(g.em, g.m, ACT.Exp, scale=1.0 / 16))
                    tell(A(g.pc, g.m, ACT.Exp, scale=2.0 / 16), s_gexp)
            act.wait_ge(s_gfin, 1)
            own(A(grs20, grs20, ACT.Ln, scale=1.0 / DV, bias=eps6))
            tell(A(grs20, grs20, ACT.Exp, scale=-0.5), s_grs)
            for d in range(2):
                for j, buf in ((0, cl), (1, aa)):
                    act.wait_ge(s_wx, 2 * d + j + 1)
                    v = buf[:, d]
                    own(A(v, v, ACT.Exp, scale=-1.0))
                    own(A(v, v, ACT.Ln, bias=1.0))
                    tell(A(v, v, ACT.Exp, scale=-1.0), s_wm)
            for p in range(NT):
                for d in range(2):
                    g, t = segs[d], PAIRS[p][d]
                    act.wait_ge(s_seg, 2 * p + d + 1)
                    cs = cl[:, d, :, t * P:(t + 1) * P]
                    own(A(g.E1[:, :, 1:HD + 1].rearrange("p (h c) i -> p h c i", c=2), cs.rearrange("p h (c i) -> p h c i", c=2), ACT.Exp))
                    tell(A(g.E2, cs, ACT.Exp, scale=-1.0), s_E)
                for d in range(2):
                    g = segs[d]
                    copy_out(g.X[:, :, 0:HD], ("tA", p, d), bank(("tA", p, d))[:, :].rearrange("p (h k) -> p h k", k=HD))
                    copy_out(g.B3[:, 2], ("tB", p, d), bank(("tB", p, d))[:, :].rearrange("p (h k) -> p h k", k=HD))
                    copy_out(g.ktok, ("tK", p, d), bank(("tK", p, d))[:, :].rearrange("p (h k) -> p h k", k=HD))
                    copy_out(g.X[:, :, HD:2 * HD], ("AV", p, d), bank(("AV", p, d))[:, :].rearrange("p (h k) -> p h k", k=HD))
                for n, dst in (("D2", "D2"), ("D2t", "D2t"), ("D4", "D4"), ("D4t", "D4t"), ("D8t", "D2t"), ("X4t", "D2"),
                               ("Z1", "Dt"), ("X5t", "D2"), ("Z2", "Dt")):
                    for d in range(2):
                        g = segs[d]
                        if n == "D4":
                            act.wait_ge(s_X1, 2 * p + d + 1)
                        to = {"D2": g.D2, "D2t": g.D2t, "D4": g.B3[:, 0], "D4t": g.A3[:, 0], "Dt": g.A3[:, 0]}[dst]
                        copy_out(to, (n, p, d), bank((n, p, d))[:, :].rearrange("p (h k) -> p h k", k=HD))
                for d in range(2):
                    g = segs[d]
                    for j in range(2):
                        copy_out(g.WU[:, 4 * j:4 * j + 4], ("WU", p, d, j), bank(("WU", p, d, j))[:, :].rearrange("p (h k) -> p h k", k=2 * HD))
                for d in range(2):
                    t = PAIRS[p][d]
                    if first(p, d):
                        if p == 1:
                            act.wait_ge(s_rst, 32)
                        copy_out(yacc[:, t], ("Ya", p, d))
                if p == 0:
                    for d in range(2):
                        wait_filled(act, "st", d)
                        out_of(A(stbuf[:, d], bank(("st", d))[0:HD, :]), "st", d)
                        act.dma_start(new_state_rwkv[0, 0, d].rearrange("h v k -> v h k"),
                                      stbuf[:, d].rearrange("v (h k) -> v h k", h=NH)).then_inc(s_rst, 16)
                    wait_filled(act, "s0")
                    wait_filled(act, "st", 1)
                    out_of(A(MR[:, 0], bank(("s0",))[:, :].rearrange("p (d h v) -> p d h v", d=2, h=RC)), "s0")
            for v, nme in enumerate(("ga1", "sc2", "sh2")):
                for cnd in range(2):
                    for h in range(2):
                        copy_out(gbuf[:, v, cnd, h * 512:(h + 1) * 512], ("rowb", nme, cnd, h))
            for t in range(NT):
                act.wait_ge(s_y, t + 1)
                own(A(rs8, rs8, ACT.Ln, scale=1.0 / HD, bias=epsln))
                tell(A(rs8, rs8, ACT.Exp, scale=-0.5), s_yr)
                if t >= 1:
                    wait_filled(act, "out", t - 1, 1)
                for j in range(2):
                    copy_out(yT[:, 4 * j:4 * j + 4], ("yT", t, j), bank(("yT", t, j))[:, :].rearrange("p (k t) -> p k t", k=4))
                act.wait_ge(s_x1, t + 1)
                own(A(junk, x1[:, t], ACT.Square, accum_out=ss1))
                own(A(ss1, ss1, ACT.Ln, scale=1.0 / D, bias=eps6))
                tell(A(ss1, ss1, ACT.Exp, scale=-0.5), s_x1r)
                for j in range(2):
                    copy_out(h2T[:, 4 * j:4 * j + 4, t * P:(t + 1) * P], ("hT2", t, j), bank(("hT2", t, j))[:, :].rearrange("p (k t) -> p k t", k=4))
            act.wait_ge(s_rg, 1)
            tell(A(rt_v["ge"], rt_v["gd"], ACT.Exp), s_rex)
            act.wait_ge(s_rg, 2)
            tell(A(rt_v["E"], rt_v["E"], ACT.Exp), s_rex)
            for cnd in range(2):
                for h in range(2):
                    copy_out(ga2b[:, cnd, h * 512:(h + 1) * 512], ("rowb", "ga2", cnd, h))

            def expert_copies(r):
                def expert_rows(i):
                    if i >= 2:
                        act.wait_ge(s_ys[i % 2], 16 * (i // 2))
                    for h in range(2):
                        copy_out(yo[:, i % 2, h * 512:(h + 1) * 512], ("dn", i, h))
                    at = (i % NE) * P
                    act.dma_start(ys_dram[at:at + P, :], yo[:, i % 2]).then_inc(s_ys[i % 2], 16)

                for e in range(NE):
                    i = r * NE + e
                    if e == 0:
                        for j in range(2):
                            copy_out(xgT[:, i % 2, 4 * j:4 * j + 4], ("xT", i, j), bank(("xT", i, j))[:, :].rearrange("p (k t) -> p k t", k=4))
                    wait_filled(act, "ug", i)
                    if i >= 2:
                        wait_result(act, "ug", i - 2)
                    tell(A(sg[:, i % 2], bank(("ug", i))[:, F:2 * F], ACT.Exp, scale=-1.0), s_sg)
                    if e < NE - 1:
                        for j in range(2):
                            copy_out(xgT[:, (i + 1) % 2, 4 * j:4 * j + 4], ("xT", i + 1, j),
                                     bank(("xT", i + 1, j))[:, :].rearrange("p (k t) -> p k t", k=4))
                    if e > 0:
                        expert_rows(i - 1)
                    copy_out(aT[:, i % 2], ("aT", i), bank(("aT", i))[:, 0:FT * P].rearrange("p (f t) -> p f t", f=FT))
                expert_rows(i)
                for s in range(2):
                    act.wait_ge(s_ys[s], 8 * (i + 1))
                tell(A(small[:, 3:4], ss1), s_moe)
            rounds(act, expert_copies)
            own, tell, out_of = steps(act, s_act2)
            act.wait_ge(s_fin, 1)
            for t in range(NT):
                own(A(junk, x1[:, t], ACT.Square, accum_out=rstd[:, t:t + 1]))
                own(A(rstd[:, t:t + 1], rstd[:, t:t + 1], ACT.Ln, scale=1.0 / D, bias=eps6))
                tell(A(rstd[:, t:t + 1], rstd[:, t:t + 1], ACT.Exp, scale=-0.5), s_finr)
            act.wait_ge(s_rst, 32)

        @block.vector
        def _(dve):
            own, tell, out_of = steps(dve, s_dve)
            TT, TS, STT = dve.tensor_tensor, dve.tensor_scalar, dve.scalar_tensor_tensor
            mk = mask[:, :].rearrange("p (d a i) -> p d a i", d=2, a=2)
            mD = maskD[:, :].rearrange("p (d a i) -> p d a i", d=2, a=2)
            mA = maskA[:, :].rearrange("p (d a i) -> p d a i", d=2, a=3)

            def scan_masks(m):
                own(dve.memset(m, 1.0))
                for d in range(2):
                    at = 0 if d == 0 else CH - 1
                    own(dve.memset(m[:, d].rearrange("p (n i) -> p n i", i=CH)[:, :, at:at + 1], 0.0))

            def chunk_sums(v, m, d):
                if d == 0:
                    own(dve.tensor_tensor_scan(v, m[:, 0], v, 0.0, ALU.mult, ALU.add))
                else:
                    own(dve.tensor_tensor_scan(v[:, ::-1], m[:, 1, ::-1], v[:, ::-1], 0.0, ALU.mult, ALU.add))

            own(dve.memset(eps6, EPS))
            tell(dve.memset(epsln, LN_EPS), s_eps)
            scan_masks(gmask)
            wait_filled(dve, "rows")
            out_of(dve.tensor_copy(vec[:, :], bank(("rows",))[:, 0:NV1 + NV2 + 2 * KT]), "rows")
            dve.wait_ge(s_cond, 1)
            own(TS(stmp, stmp, 1.0, None, ALU.add))
            own(dve.reciprocal(stmp, stmp))
            tell(TT(scond, stmp, vec[:, vcond:vcond + 2 * KT], ALU.mult), s_condt)
            own(TS(oneka, vec[:, vka:vka + RC], -1.0, 1.0, ALU.mult, ALU.add))
            own(TS(negka, vec[:, vka:vka + RC], -1.0, None, ALU.mult))

            def ada_out(n):
                wait_filled(dve, "ada", n)
                if n >= 2:
                    wait_filled(dve, "adaT", n - 2)
                out_of(dve.tensor_copy(adarow(n), bank(("ada", n))[0:2, :]), "ada", n)
                wait_filled(dve, "adaT", n)
                out_of(TT(modv[:, 4 * n:4 * n + 4, :], bank(("adaT", n))[:, 0:8].rearrange("p (b c) -> p b c", c=2),
                          bc(vec[:, vb_ada + 4 * n:vb_ada + 4 * n + 4], 2, 2), ALU.add), "adaT", n)

            for n in range(4):
                ada_out(n)
            tell(STT(gscv[:, 0], modv[:, KT:2 * KT, :], 1.0, bc(vec[:, vn1:vn1 + KT], 2, 2), ALU.add, ALU.mult), s_g1)
            dve.wait_ge(s_xn, 1)
            for t in range(NT):
                ins = TS(x_sb[:, t], x_sb[:, t], rstd[:, t:t + 1], None, ALU.mult)
                own(ins) if t < NT - 1 else tell(ins, s_xnr)
            for k in range(1, KT, 2):
                wait_filled(dve, "hl", k)
                out_of(TS(hT[:, k, P:T], bank(("hl", k))[:, :], gscv[:, 0, k, 1:2], modv[:, k, 1:2], ALU.mult, ALU.add), "hl", k)
            wait_filled(dve, "hc", 1)
            for j in range(KT // 2):
                k = KT // 2 + j
                ins = TS(hT[:, k, 0:P], bank(("hc", 1))[:, j * P:(j + 1) * P], gscv[:, 0, k, 0:1], modv[:, k, 0:1], ALU.mult, ALU.add)
                if j < KT // 2 - 1:
                    own(ins)
            out_of(ins, "hc", 1)
            for t in range(NT):
                wait_filled(dve, "og", t)
                out_of(TS(yg[:, t], bank(("og", t))[:, :], -40.0, None, ALU.max), "og", t)
            tell(dve.memset(small[:, 2:3], 1.0), s_ogx)
            dve.wait_ge(s_xn, 1)
            for key, sl, n in ((("lgkl",), slice(P, T), LAT), (("lgkc",), slice(0, P), P)):
                wait_filled(dve, *key)
                own(dve.tensor_copy(lgkT[0:GKL, sl], bank(key)[0:GKL, 0:n]))
                out_of(dve.tensor_copy(lgkT[32:32 + GKL, sl], bank(key)[32:32 + GKL, 0:n]), *key)
            for d in range(2):
                for i in range(GC):
                    wait_filled(dve, "gkl", d, i)
                    out_of(TS(gcl[:, d, i, P:T], bank(("gkl", d, i))[:, :], vec[:, vgb + d * GC + i:vgb + d * GC + i + 1], None, ALU.add), "gkl", d, i)
            wait_filled(dve, "gkc")
            for d in range(2):
                for i in range(GC):
                    j = d * GC + i
                    ins = TS(gcl[:, d, i, 0:P], bank(("gkc",))[:, j * P:(j + 1) * P], vec[:, vgb + j:vgb + j + 1], None, ALU.add)
                    if j < 2 * GC - 1:
                        own(ins)
            out_of(ins, "gkc")
            tell(dve.memset(small[:, 2:3], 1.0), s_lgx)
            dve.wait_ge(s_lgt, 1)
            g_all = region1[:, KT * T + 2 * GC * T:KT * T + 4 * GC * T]
            own(STT(g_all, g_all, 0.0, cl_b[:, 0:RC * T], ALU.min, ALU.subtract))
            for d in range(2):
                for i in range(GC):
                    chunk_sums(gcl[:, d, i], gmask, d)
            tell(dve.memset(small[:, 2:3], 1.0), s_gcl)

            for c_, n in enumerate(tail[:3 * RC]):
                b = c_ % 2
                dst = {"r": rT, "k": kT, "v": vT}[n[0]][:, c_ % RC]
                if n == "v0":
                    wait_filled(dve, "kc")
                wait_result(dve, "pl", n)
                wait_result(dve, "pc", n)
                lat = raw[:, b, 0:RAWL].rearrange("p (y x) -> p y x", x=GW + 2)
                out = dst[:, P:T].rearrange("p (y x) -> p y x", x=GW)

                def tap(i, j):
                    q = vcv + (3 * i + j) * 3 * RC + c_
                    return vec[:, q:q + 1]
                own(TS(out, lat[:, 0:GH, 0:GW], tap(0, 0), None, ALU.mult))
                own(TS(dst[:, 0:P], raw[:, b, RAWL:RAWL + P], tap(1, 0), None, ALU.mult))
                for m in range(1, 9):
                    i, j = m // 3, m % 3
                    own(STT(out, lat[:, i:i + GH, j:j + GW], tap(i, j), out, ALU.mult, ALU.add))
                own(STT(dst[:, 0:P], raw[:, b, RAWL + 1:RAWL + 1 + P], tap(1, 1), dst[:, 0:P], ALU.mult, ALU.add))
                tell(STT(dst[:, 0:P], raw[:, b, RAWL + 2:RAWL + 2 + P], tap(1, 2), dst[:, 0:P], ALU.mult, ALU.add), s_conv)
                if n == f"k{RC - 1}":
                    for i in range(RC):
                        tell(TS(kkT[:, i], kT[:, i], vec[:, vkk + i:vkk + i + 1], None, ALU.mult), s_kk)
                    for i in range(RC):
                        tell(STT(prod[:, i], rT[:, i], vec[:, vrk + i:vrk + i + 1], kT[:, i], ALU.mult, ALU.mult), s_bon)
                    wait_filled(dve, "bonus")
                    out_of(dve.tensor_copy(bonus[:, :], bank(("bonus",))[:, 0:NT * NH]), "bonus")
            dve.wait_ge(s_kkn, 1)
            own(STT(kkT, kkT, -1.0, sq, ALU.mult, ALU.mult))
            wait_filled(dve, "pl", "lw")
            out_of(TS(tlw[:, P:T], bank(("pl", "lw"))[:, :], 20.0, None, ALU.min), "pl", "lw")
            wait_filled(dve, "pc", "lw")
            out_of(TS(tlw[:, 0:P], bank(("pc", "lw"))[:, 0:P], 20.0, None, ALU.min), "pc", "lw")
            wait_filled(dve, "pl", "lg")
            out_of(TS(slg[:, P:T], bank(("pl", "lg"))[:, :], -40.0, None, ALU.max), "pl", "lg")
            wait_filled(dve, "pc", "lg")
            out_of(TS(slg[:, 0:P], bank(("pc", "lg"))[:, 0:P], -40.0, None, ALU.max), "pc", "lg")
            tell(dve.memset(small[:, 2:3], 1.0), s_lora)
            dve.wait_ge(s_lgt, 2)
            tell(TS(tlw, tlw, -2.0, 1.0, ALU.mult, ALU.add), s_lora)

            wait_filled(dve, "pc", "lg")
            tell(dve.memset(GM[:, 0], 0.0), s_gz)
            dve.wait_ge(s_sig, 4)
            wait_filled(dve, "vt", NT - 1)
            for p in range(NT):
                for d in range(2):
                    g, t = gws[d], PAIRS[p][d]
                    cs = gcl[:, d, :, t * P:(t + 1) * P].rearrange("p c (j i) -> p c j i", j=2)
                    at = CH - 1 if d == 0 else 0
                    own(TS(g.m, cs[:, :, :, at], 0.5, None, ALU.mult))
                    own(TT(g.df.rearrange("p (c j i) -> p c j i", c=GC, j=2), cs, bc(g.m, 3, CH), ALU.subtract))
                    tell(TS(g.df, g.df, -16.0 * CLAMP, 16.0 * CLAMP, ALU.max, ALU.min), s_gseg)
                for d in range(2):
                    g, t = gws[d], PAIRS[p][d]
                    b = bank(("g1", p, d))
                    wait_filled(dve, "g1", p, d)
                    own(TT(g.sT, b[:, 0:4 * HD].rearrange("p (h i) -> p h i", h=GH_N), bc(mk[:, d, 1], 1, GH_N), ALU.mult))
                    out_of(dve.tensor_copy(g.ktok, b[:, 4 * HD:8 * HD].rearrange("p (h i) -> p h i", h=GH_N)), "g1", p, d)
                for d in range(2):
                    g, t = gws[d], PAIRS[p][d]
                    wait_filled(dve, "goA", p, d)
                    if first(p, d):
                        out_of(dve.tensor_copy(goacc[:, t], bank(("goA", p, d))[:, :]), "goA", p, d)
                    else:
                        out_of(TT(goacc[:, t], bank(("goA", p, d))[:, :], goacc[:, t], ALU.add), "goA", p, d)
                    wait_filled(dve, "gkv", p, d)
                    dve.wait_ge(s_gexp, 2 * p + d + 1)
                    out_of(TT(g.kv, bank(("gkv", p, d))[:, :].rearrange("p (c j v) -> p c j v", c=GC, j=2), bc(g.em, 3, DV), ALU.mult), "gkv", p, d)
                    st = 0 if p == 0 else 1
                    if p == 1:
                        dve.wait_ge(s_gin, 16 * 5)
                    M0, c0, c1 = GM[:, st, d], chunk(d, 0), chunk(d, 1)
                    own(TT(GM[:, 3, d], M0, bc(g.em[:, :, c0], 2, DV), ALU.mult))
                    own(TT(GM[:, 5, d], M0, bc(g.pc[:, :, c0], 2, DV), ALU.mult))
                    own(TT(GM[:, 2, d], GM[:, 5, d], g.kv[:, :, c0], ALU.add))
                    own(TT(GM[:, 4, d], GM[:, 2, d], bc(g.em[:, :, c1], 2, DV), ALU.mult))
                    own(TT(GM[:, 6, d], GM[:, 2, d], bc(g.pc[:, :, c1], 2, DV), ALU.mult))
                    tell(TT(M0, GM[:, 6, d], g.kv[:, :, c1], ALU.add), s_gM)
                for d in range(2):
                    t = PAIRS[p][d]
                    wait_filled(dve, "goB", p, d)
                    out_of(TT(goacc[:, t], bank(("goB", p, d))[:, :], goacc[:, t], ALU.add), "goB", p, d)
            go4 = goacc.rearrange("p t (h v) -> p (t h) v", v=DV)
            gsq = region3[:, 0:NT * RW].rearrange("p (n v) -> p n v", v=DV)
            own(TT(gsq, go4, go4, ALU.mult))
            tell(dve.tensor_reduce(out=grs20, in_=gsq, axis=AXX, op=ALU.add), s_gfin)
            dve.wait_ge(s_grs, 1)
            own(TT(go4, go4, bc(grs20, 2, DV), ALU.mult))
            own(TT(go4, go4, bc(gng, 1, NT * GH_N), ALU.mult))
            tell(TT(yg_b[:, :], yg_b[:, :], cl_b[:, RC * T:2 * RC * T], ALU.mult), s_gdone)

            scan_masks(smask)
            for d in range(2):
                for key, buf, off in (("w", cl, vw0), ("a", aa, va0)):
                    for i in range(RC):
                        wait_filled(dve, key + "l", d, i)
                        q = off + d * RC + i
                        out_of(TS(buf[:, d, i, P:T], bank((key + "l", d, i))[:, :], vec[:, q:q + 1], -40.0, ALU.add, ALU.max), key + "l", d, i)
                    wait_filled(dve, key + "c", d)
                    for i in range(RC):
                        q = off + d * RC + i
                        ins = TS(buf[:, d, i, 0:P], bank((key + "c", d))[:, i * P:(i + 1) * P], vec[:, q:q + 1], -40.0, ALU.add, ALU.max)
                        if i < RC - 1:
                            own(ins)
                    out_of(ins, key + "c", d)
                    tell(dve.memset(small[:, 2:3], 1.0), s_wx)
            for n in range(4, 2 * NMOD):
                ada_out(n)
            tell(STT(gscv[:, 1], modv[:, 4 * KT:5 * KT, :], 1.0, bc(vec[:, vn2:vn2 + KT], 2, 2), ALU.add, ALU.mult), s_g2)
            for d in range(2):
                dve.wait_ge(s_wm, 2 * d + 1)
                own(TS(cl[:, d], cl[:, d], DECAY, None, ALU.mult))
                for i in range(RC):
                    chunk_sums(cl[:, d, i], smask, d)
                dve.wait_ge(s_wm, 2 * d + 2)
                own(TS(aa[:, d], aa[:, d], -1.0, None, ALU.mult))
            tell(dve.memset(MR[:, 0], 0.0), s_mst)

            dve.wait_ge(s_gout, 64)
            for p in range(NT):
                cur, nxt = MCUR[p], 1 - MCUR[p]
                for d in range(2):
                    g = segs[d]
                    own(dve.memset(g.E1[:, :, 0:1], 1.0))
                    tell(dve.memset(g.E1[:, :, HD + 1:HD + 2], 1.0), s_seg)
                for d in range(2):
                    g, t = segs[d], PAIRS[p][d]
                    n = 2 * p + d
                    tok = slice(t * P, (t + 1) * P)
                    c4 = lambda v: v.rearrange("p h (c i) -> p h c i", c=2)
                    e4 = lambda a, b: g.E1[:, :, a:b].rearrange("p (h c) i -> p h c i", c=2)
                    for h in range(RC):
                        ins = TS(g.t2[:, h], aa[:, d, h, tok], negka[:, h:h + 1], oneka[:, h:h + 1], ALU.mult, ALU.add)
                        own(ins) if h < RC - 1 else tell(ins, s_f)
                    dve.wait_ge(s_E, n + 1)
                    own(TT(g.AR[:, :, :, 1, :], c4(rT[:, :, tok]), e4(1, HD + 1), ALU.mult))
                    sh = (0, HD) if d == 0 else (2, HD + 2)
                    own(TT(g.AR[:, :, :, 0, :], c4(kkT[:, :, tok]), e4(*sh), ALU.mult))
                    at = HD if d == 0 else 1
                    own(dve.tensor_copy(pcs[:, d], g.E1[:, :, at].rearrange("p (h c) -> p h c", c=2)))
                    dve.wait_ge(s_t1, 2 * n + 2)
                    own(TT(g.b, g.t1, g.E2, ALU.mult))
                    tell(TT(g.k, g.t2, g.E2, ALU.mult), s_ops)
                for d in range(2):
                    g = segs[d]
                    for n in ("b0", "k0", "A", "b1", "k1"):
                        key = (n, p, d)
                        wait_filled(dve, *key)
                        if n == "A":
                            v = bank(key)[:, :].rearrange("p (h i) -> p h i", h=NH)
                            for a in range(3):
                                ins = TT(g.A3[:, a], v, bc(mA[:, d, a], 1, NH), ALU.mult)
                                if a < 2:
                                    own(ins)
                            out_of(ins, *key)
                            continue
                        hp = int(n[1])
                        dst, m = (g.B3[:, 0:2], mD) if n[0] == "b" else (g.K2, mk)
                        out_of(TT(dst[:, :, hp::2].rearrange("p a h i -> p h a i"), bank(key)[:, :].rearrange("p (h a i) -> p h a i", a=2, i=HD),
                                  bc(m[:, d], 1, RC), ALU.mult), *key)
                    tell(TT(g.X0, g.B3[:, 0], bc(identh[:, :], 1, NH), ALU.add), s_X1)
                for n in ("X2", "X3", "X4", "X5", "X6"):
                    for d in range(2):
                        g = segs[d]
                        src, dst = (g.X0, g.X1) if n in ("X2", "X4", "X6") else (g.X1, g.X0)
                        wait_filled(dve, n, p, d)
                        out_of(TT(dst, bank((n, p, d))[:, :].rearrange("p (h i) -> p h i", h=NH), src, ALU.add), n, p, d)
                for d in range(2):
                    g = segs[d]
                    for cp in range(2):
                        v = bank(("G", p, d, cp))[:, :].rearrange("p (h a i) -> p h a i", a=2, i=HD)
                        wait_filled(dve, "G", p, d, cp)
                        own(TT(g.QT[:, :, cp], v[:, :, 0], g.AR[:, :, cp, 1], ALU.add))
                        out_of(TT(g.GT[:, :, cp], v[:, :, 1], bc(identh[:, :], 1, RC), ALU.add), "G", p, d, cp)
                    for cp in range(2):
                        wait_filled(dve, "H", p, d, cp)
                        out_of(TT(g.H[:, cp], bank(("H", p, d, cp))[:, 0:RC * HD].rearrange("p (h i) -> p h i", h=RC),
                                  bc(pcs[:, d, :, cp], 2, HD), ALU.mult), "H", p, d, cp)
                for k in range(2):
                    for d in range(2):
                        g, cp = segs[d], chunk(d, k)
                        dst = MM[:, d] if k == 0 else MR[:, nxt, d]
                        wait_filled(dve, "seq", p, d, k)
                        out_of(TT(g.tmp, bank(("seq", p, d, k))[:, 0:RC * HD].rearrange("p (h i) -> p h i", h=RC),
                                  bc(pcs[:, d, :, cp], 2, HD), ALU.mult), "seq", p, d, k)
                        tell(TT(dst, g.tmp, g.H[:, cp], ALU.add), s_mst)
                for d in range(2):
                    t = PAIRS[p][d]
                    for n in ("Ya", "Yb"):
                        if n == "Ya" and first(p, d):
                            wait_result(dve, "Ya", p, d)
                            continue
                        wait_filled(dve, n, p, d)
                        out_of(TT(yacc[:, t], bank((n, p, d))[:, :], yacc[:, t], ALU.add), n, p, d)
            tell(dve.memset(small[:, 2:3], 1.0), s_rwdone)

            dve.wait_ge(s_wo, 160)
            mu8 = small[:, 104:112]
            for t in range(NT):
                cnd = 0 if t == 0 else 1
                y3 = yacc[:, t].rearrange("p (h i) -> p h i", h=NH)
                s3 = sqj.rearrange("p (h i) -> p h i", h=NH)
                own(dve.tensor_reduce(out=mu8, in_=y3, axis=AXX, op=ALU.add))
                own(TS(mu8, mu8, 1.0 / HD, None, ALU.mult))
                own(TT(y3, y3, bc(mu8, 2, HD), ALU.subtract))
                own(TT(s3, y3, y3, ALU.mult))
                tell(dve.tensor_reduce(out=rs8, in_=s3, axis=AXX, op=ALU.add), s_y)
                dve.wait_ge(s_yr, t + 1)
                own(TT(y3, y3, bc(rs8, 2, HD), ALU.mult))
                own(TT(yacc[:, t], yacc[:, t], lnw, ALU.mult))
                own(TT(yacc[:, t], yacc[:, t], lnb, ALU.add))
                own(TT(s3, vtok[:, t].rearrange("p (h i) -> p h i", h=NH), bc(bonus[:, t * NH:(t + 1) * NH], 2, HD), ALU.mult))
                own(TT(yacc[:, t], yacc[:, t], sqj, ALU.add))
                wait_filled(dve, "gate", t)
                out_of(TT(ya, yacc[:, t], bank(("gate", t))[:, :], ALU.mult), "gate", t)
                for h in range(2):
                    wait_filled(dve, "out", t, h)
                    if h == 0:
                        wait_result(dve, "rowb", "ga1", 1, 1)
                    out_of(TT(x1[:, t, h * 512:(h + 1) * 512], bank(("out", t, h))[:, :], gbuf[:, 0, cnd, h * 512:(h + 1) * 512], ALU.mult), "out", t, h)
                dve.wait_ge(s_xt, 16 * (t + 1))
                tell(TT(x1[:, t], x1[:, t], xt, ALU.add), s_x1)
                dve.wait_ge(s_x1r, t + 1)
                wait_result(dve, "rowb", "sh2", 1, 1)
                if t >= 1:
                    wait_filled(dve, "hT2", t - 1, 1)
                    dve.wait_ge(s_h2d, 16 * t)
                own(STT(h2, x1[:, t], ss1, gbuf[:, 1, cnd], ALU.mult, ALU.mult))
                tell(TT(h2, h2, gbuf[:, 2, cnd], ALU.add), s_h2)
                wait_filled(dve, "router", t)
                out_of(TT(lgt[:, t], bank(("router", t))[:, 0:NR], br, ALU.add), "router", t)

            gl = lgt[:, :, 0:NG]
            el = lgt[:, :, NG:NR].rearrange("p t (g e) -> p t g e", g=NG)
            R = rt_v
            for j in range(NG):
                own(dve.memset(R["pref"][:, j:j + 1], float(NG - j)))

            def first_max(hot, val, mx):
                own(dve.tensor_reduce(out=mx, in_=val, axis=AXX, op=ALU.max))
                own(TT(hot, val, bc(mx, 2, NG), ALU.is_equal))
                own(TT(hot, hot, bc(R["pref"], 1, NT), ALU.mult))
                own(dve.tensor_reduce(out=R["m"], in_=hot, axis=AXX, op=ALU.max))
                own(TT(hot, hot, bc(R["m"], 2, NG), ALU.is_equal))
            first_max(R["hg"], gl, R["mg"])
            tell(TT(R["gd"], gl, bc(R["mg"], 2, NG), ALU.subtract), s_rg)
            own(TT(R["sel"], el.rearrange("p t g e -> p t e g"), bc(R["hg"], 2, EPG), ALU.mult))
            own(dve.tensor_reduce(out=R["es"], in_=R["sel"], axis=AXX, op=ALU.add))
            first_max(R["h1"], R["es"], R["m1"])
            own(STT(R["es"], R["h1"], -1e30, R["es"], ALU.mult, ALU.add))
            first_max(R["h2"], R["es"], R["m2"])
            tell(TT(R["E"], R["m2"], R["m1"], ALU.subtract), s_rg)
            dve.wait_ge(s_rex, 1)
            own(dve.tensor_reduce(out=R["m"], in_=R["ge"], axis=AXX, op=ALU.add))
            dve.wait_ge(s_rex, 2)
            own(TS(R["w1"], R["E"], 1.0, None, ALU.add))
            own(TT(R["w1"], R["w1"], R["m"], ALU.mult))
            own(dve.reciprocal(R["w1"], R["w1"]))
            own(TT(R["w2"], R["w1"], R["E"], ALU.mult))

            dve.wait_ge(s_tri, 1)
            for o_, h_ in (("o1", "h1"), ("o2", "h2")):
                v = R[o_].rearrange("p t (g e) -> p t g e", g=NG)
                for g_ in range(NG):
                    own(TT(v[:, :, g_], R[h_], bc(R["hg"][:, :, g_], 2, EPG), ALU.mult))
            tell(TT(picked_v, R["o1"], R["o2"], ALU.add), s_pick)
            wait_filled(dve, "rank")
            own(dve.tensor_reduce(out=R["mc"], in_=bank(("rank",))[:, NT * NE:(NT + 1) * NE], axis=AXX, op=ALU.max))
            tell(dve.tensor_copy(most[0:1, 0:1], R["mc"][0:1, :]), s_most)
            rank = bank(("rank",))[:, 0:NT * NE].rearrange("p (t n) -> p t n", t=NT)
            for j, o_ in enumerate(("o1", "o2")):
                js = slice(j * NT, (j + 1) * NT)
                ins = TT(rtmp, rank, R[o_], ALU.mult)
                own(ins) if j == 0 else out_of(ins, "rank")
                own(dve.tensor_reduce(out=R["rk"][:, js], in_=rtmp, axis=AXX, op=ALU.add))
                own(TT(rtmp, R[o_], bc(slot0, 1, NT), ALU.mult))
                own(dve.tensor_reduce(out=R["ps"][:, js], in_=rtmp, axis=AXX, op=ALU.add))
                own(dve.tensor_copy(R["wt"][:, js], R["w1" if j == 0 else "w2"]))
                own(TT(R[o_], R[o_], bc(tokid, 2, NE), ALU.mult))
            own(TT(R["ps"], R["ps"], R["rk"], ALU.add))

            def expert_gates(r):
                if r >= 1:
                    for s in range(3):
                        dve.wait_ge(s_xg[s], 16 * len(range(s, r * NE, 3)))
                for j in range(2):
                    for t in range(NT):
                        ins = TS(onehot[:, j, t], iota, float(r * P), R["rk"][:, j * NT + t:j * NT + t + 1], ALU.add, ALU.is_equal)
                        own(ins) if (j, t) != (1, NT - 1) else tell(ins, s_oh)
                wait_filled(dve, "ids", r)
                out_of(dve.tensor_copy(idx[:, :], bank(("ids", r))[:, 0:NE]), "ids", r)
                tell(dve.memset(small[:, 2:3], 1.0), s_idx)
                own(TS(R["in"], R["rk"], float(r * P), None, ALU.is_ge))
                own(TS(R["ib"], R["rk"], float((r + 1) * P), None, ALU.is_lt))
                own(TT(R["in"], R["in"], R["ib"], ALU.mult))
                own(STT(R["ib"], R["ps"], float(-r * P), R["in"], ALU.add, ALU.mult))
                own(TT(R["wr"], R["wt"], R["in"], ALU.mult))
                tell(dve.tensor_copy(pos[:, :], R["ib"]), s_pos)
                for e in range(NE):
                    i = r * NE + e
                    s = i % 2
                    v = bank(("ug", i))
                    dve.wait_ge(s_sg, i + 1)
                    own(TS(sg[:, s], sg[:, s], 1.0, None, ALU.add))
                    own(dve.reciprocal(sg[:, s], sg[:, s]))
                    own(TT(sg[:, s], sg[:, s], v[:, F:2 * F], ALU.mult))
                    if i >= 2:
                        wait_filled(dve, "aT", i - 2)
                    out_of(TT(ac[:, s], v[:, 0:F], sg[:, s], ALU.mult), "ug", i)
                for t in range(NT):
                    cnd = 0 if t == 0 else 1
                    g0, g1 = yg2[:, t % 2, 0], yg2[:, t % 2, 1]
                    uses = r * len(range(t % 2, NT, 2)) + t // 2 + 1
                    dve.wait_ge(s_yg[t % 2], 32 * uses)
                    own(TS(g0, g0, R["wr"][:, t:t + 1], None, ALU.mult))
                    own(STT(g0, g1, R["wr"][:, NT + t:NT + t + 1], g0, ALU.mult, ALU.add))
                    own(TT(g0, g0, ga2b[:, cnd], ALU.mult))
                    tell(TT(x1[:, t], x1[:, t], g0, ALU.add), s_comb)
            rounds(dve, expert_gates)

            own, tell, out_of = steps(dve, s_dve2)
            tell(dve.memset(small[:, 3:4], 1.0), s_fin)
            for t in range(NT):
                dve.wait_ge(s_finr, t + 1)
                tell(STT(acc[:, t], x1[:, t], rstd[:, t:t + 1], fg, ALU.mult, ALU.mult), s_yout)

        @block.tensor
        def _(pe):
            def mm(out, lhsT, rhs, start=True, stop=True):
                return pe.matmul(out, lhsT, rhs, start=start, stop=stop)

            def tr(out, in_):
                n = in_.shape[0]
                return pe.transpose(out, in_, ident[0:n, 0:n])

            def open_bank(*key):
                n = J[key]
                assert n == done[0], (key, n, done[0])
                done[0] += 1
                if n >= NB:
                    pe.wait_ge(drained[n % NB], n // NB)
                return PS[n % NB]

            def open_early(*key):
                n = J[key]
                if n >= NB:
                    pe.wait_ge(drained[n % NB], n // NB)
                return PS[n % NB]

            done, turns = [0], [0]

            def finish(ins):
                ins.then_inc(filled, 1)

            def half_done(ins):
                turns[0] += 1
                ins.then_inc(s_turn, 1)
                return turns[0]

            def slab(what):
                i = slabs.index(what)
                pe.wait_ge(slab_in[i % RING], 16 * (i // RING + 1))
                return ring[:, i % RING]

            pe.wait_ge(s_const, 1)
            pe.wait_ge(s_small, 16 * 16)
            b = open_bank("rows")
            tr(b[:, 0:NV1], region1[0:NV1, 0:P])
            tr(b[:, NV1:NV1 + NV2], region1[0:NV2, P:2 * P])
            finish(tr(b[:, vcond:vcond + 2 * KT], region1[0:2 * KT, 2 * P:3 * P]))

            def ada(n):
                w = slab(("ada", n))
                b = open_bank("ada", n)
                for k in range(KT):
                    ins = mm(b[0:2, :], condt[:, :, k], w[:, k, :], start=k == 0, stop=k == KT - 1)
                finish(ins)
                wait_result(pe, "ada", n)
                b = open_bank("adaT", n)
                for j in range(4):
                    ins = tr(b[:, 2 * j:2 * j + 2], adarow(n)[:, j * P:(j + 1) * P])
                finish(ins)

            pe.wait_ge(s_condt, 1)
            for n in range(4):
                ada(n)
            pe.wait_ge(s_xnr, 1)
            for k in range(KT):
                b = open_bank("hl", k)
                for t in range(1, NT):
                    ins = tr(b[:, (t - 1) * P:t * P], x_sb[:, t, k * P:(k + 1) * P])
                finish(ins)
            for j in range(2):
                b = open_bank("hc", j)
                for k in range(4):
                    ins = tr(b[:, k * P:(k + 1) * P], x_sb[:, 0, (4 * j + k) * P:(4 * j + k + 1) * P])
                finish(ins)
            for k in range(KT):
                wait_result(pe, "hl", k)
            wait_result(pe, "hc", 0)
            wait_result(pe, "hc", 1)

            def project(name, w, at, width=P):
                for kind, sl in (("pl", slice(P, T)), ("pc", slice(0, P))):
                    b = open_bank(kind, name)
                    n = sl.stop - sl.start
                    for k in range(KT):
                        ins = mm(b[0:width, 0:n], w[:, k, at:at + width], hT[:, k, sl], start=k == 0, stop=k == KT - 1)
                    finish(ins)

            w = slab("qk")
            for i, n in enumerate(chan):
                project(n, w, i * P)
            for what in ("vg", "og"):
                w = slab(what)
                for t in range(NT):
                    b = open_bank(what, t)
                    for k in range(KT):
                        ins = mm(b[:, :], hT[:, k, t * P:(t + 1) * P], w[:, k, :], start=k == 0, stop=k == KT - 1)
                    finish(ins)
            w = slab("lgk")
            for key, sl in (("lgkl", slice(P, T)), ("lgkc", slice(0, P))):
                b = open_bank(key)
                n = sl.stop - sl.start
                for d in range(2):
                    for k in range(KT):
                        ins = mm(b[32 * d:32 * d + GKL, 0:n], w[:, k, d * GKL:(d + 1) * GKL], hT[:, k, sl], start=k == 0, stop=k == KT - 1)
                finish(ins)
            wait_result(pe, "lgkl")
            wait_result(pe, "lgkc")
            for d in range(2):
                for i in range(GC):
                    finish(mm(open_bank("gkl", d, i)[:, :], gk2_sb[32 * d:32 * d + GKL, i * P:(i + 1) * P], lgkT[32 * d:32 * d + GKL, P:T]))
            b = open_bank("gkc")
            for d in range(2):
                if d == 1:
                    pe.wait_ge(s_turn, half_done(ins))
                for i in range(GC):
                    j = d * GC + i
                    ins = mm(b[:, j * P:(j + 1) * P], gk2_sb[32 * d:32 * d + GKL, i * P:(i + 1) * P], lgkT[32 * d:32 * d + GKL, 0:P])
            finish(ins)
            for what in ("r", "k", "v"):
                w = slab(what)
                for i in range(RC):
                    project(f"{what}{i}", w, i * P)
                if what == "k":
                    for i in range(RC):
                        pe.wait_ge(s_prod, i + 1)
                        finish(mm(open_bank("kl", i)[:, :], blk[:, :], sq[:, i, P:T]))
                    b = open_bank("kc")
                    for i in range(RC):
                        ins = mm(b[:, i * P:(i + 1) * P], blk[:, :], sq[:, i, 0:P])
                    finish(ins)
                    pe.wait_ge(s_bon, RC)
                    b = open_bank("bonus")
                    for t in range(NT):
                        for i in range(RC):
                            ins = mm(b[:, t * NH + 2 * i:t * NH + 2 * i + 2], prod[:, i, t * P:(t + 1) * P], blk[:, 0:P:HD])
                    finish(ins)
                if what == "v":
                    pe.wait_ge(s_conv, 3 * RC)
                    for t in range(NT):
                        b = open_bank("vt", t)
                        for i in range(RC):
                            ins = tr(b[:, i * P:(i + 1) * P], vT[:, i, t * P:(t + 1) * P])
                        finish(ins)
            w = slab("lora")
            for i, n in enumerate(("lw", "la", "lg")):
                project(n, w, i * P)

            pe.wait_ge(s_gcl, 1)
            for t in range(NT):
                wait_result(pe, "vg", t)
            half = lambda x: slice(HD * x, HD * x + HD)
            for p in range(NT):
                for d in range(2):
                    g = gws[d]
                    pe.wait_ge(s_gq, 2 * p + d + 1)
                    b = open_bank("g1", p, d)
                    for hp in range(2):
                        for c_ in range(GC):
                            for cp in range(2):
                                h = 2 * c_ + hp
                                ins = mm(b[half(cp), h * HD:(h + 1) * HD], g.k[half(hp), c_, half(cp)], g.q[half(hp), c_, half(cp)])
                        if hp == 0:
                            turn = half_done(ins)
                            for c_ in range(GC):
                                tr(b[:, 4 * HD + c_ * P:4 * HD + (c_ + 1) * P], g.k[:, c_])
                            pe.wait_ge(s_turn, turn)
                    finish(ins)
                for d in range(2):
                    g, t = gws[d], PAIRS[p][d]
                    wait_result(pe, "g1", p, d)
                    bA = open_early("goA", p, d)
                    bK = open_early("gkv", p, d)
                    for cp in range(2):
                        for h in range(GH_N):
                            col = (h // 2 * 2 + cp) * DV
                            ins = mm(bK[half(h % 2), col:col + DV], g.ktok[half(cp), h], vg[half(cp), t, h * DV:(h + 1) * DV])
                        if cp == 0:
                            turn = half_done(ins)
                            open_bank("goA", p, d)
                            for h in range(GH_N):
                                for c_ in range(2):
                                    insA = mm(bA[half(c_), h * DV:(h + 1) * DV], g.sT[half(c_), h], vg[half(c_), t, h * DV:(h + 1) * DV])
                            finish(insA)
                            open_bank("gkv", p, d)
                            pe.wait_ge(s_turn, turn)
                    finish(ins)
                bs, turn = [open_early("goB", p, d) for d in range(2)], [0, 0]
                for hp in range(2):
                    for d in range(2):
                        g = gws[d]
                        if hp == 0:
                            pe.wait_ge(s_gM, 2 * p + d + 1)
                        else:
                            open_bank("goB", p, d)
                            pe.wait_ge(s_turn, turn[d])
                        for c_ in range(GC):
                            for cp in range(2):
                                h = 2 * c_ + hp
                                m = GM[half(hp), 3 if cp == chunk(d, 0) else 4, d, c_]
                                ins = mm(bs[d][half(cp), h * DV:(h + 1) * DV], g.q[half(hp), c_, half(cp)], m)
                        if hp == 1:
                            finish(ins)
                        else:
                            turn[d] = half_done(ins)

            pe.wait_ge(s_lora, 2)
            wait_result(pe, "pl", "la")
            wait_result(pe, "pc", "la")
            for d in range(2):
                for key, wt, src in (("w", w2_sb, tlw), ("a", a2_sb, laT)):
                    for i in range(RC):
                        finish(mm(open_bank(key + "l", d, i)[:, :], wt[half(d), i * P:(i + 1) * P], src[half(d), P:T]))
                    b = open_bank(key + "c", d)
                    for i in range(RC):
                        ins = mm(b[:, i * P:(i + 1) * P], wt[half(d), i * P:(i + 1) * P], src[half(d), 0:P])
                    finish(ins)
            for n in range(4, 2 * NMOD):
                ada(n)

            for t in range(NT):
                wait_result(pe, "vt", t)
            for p in range(NT):
                cur = MCUR[p]
                if p == 1:
                    pe.wait_ge(s_rin, 32)
                    b = open_bank("s0")
                    for d in range(2):
                        for i in range(RC):
                            ins = tr(b[:, (d * RC + i) * HD:(d * RC + i + 1) * HD], s0buf[:, d, i * P:(i + 1) * P])
                    finish(ins)
                for d in range(2):
                    g, t = segs[d], PAIRS[p][d]
                    pe.wait_ge(s_ops, 2 * p + d + 1)
                    bA = open_early("A", p, d)
                    for hp in range(2):
                        def a_rows():
                            for i in range(RC):
                                for cp in range(2):
                                    h = 2 * i + hp
                                    ins = mm(bA[half(cp), h * HD:(h + 1) * HD], g.AR[half(hp), i, cp, 0], g.b[half(hp), i, half(cp)])
                            return ins
                        if hp == 0:
                            turn = half_done(a_rows())
                        for n, src in (("b", g.b), ("k", g.k)):
                            b = open_bank(f"{n}{hp}", p, d)
                            for i in range(RC):
                                for cp in range(2):
                                    ins = mm(b[half(cp), i * 2 * HD:(i + 1) * 2 * HD], src[half(hp), i, half(cp)], g.AR[half(hp), i, cp])
                            finish(ins)
                            if hp == 0 and n == "k":
                                open_bank("A", p, d)
                                pe.wait_ge(s_turn, turn)
                                for i in range(RC):
                                    for cp in range(2):
                                        h = 2 * i + 1
                                        ins = mm(bA[half(cp), h * HD:(h + 1) * HD], g.AR[half(1), i, cp, 0], g.b[half(1), i, half(cp)])
                                finish(ins)
                    for n in ("tA", "tB", "tK"):
                        b = open_bank(n, p, d)
                        for i in range(RC):
                            src = {"tA": g.AR[:, i, :, 0], "tB": g.b[:, i], "tK": g.k[:, i]}[n]
                            ins = tr(b[:, i * P:(i + 1) * P], src)
                        finish(ins)
                    wait_result(pe, "k0", p, d)
                    wait_result(pe, "k1", p, d)
                    b = open_bank("AV", p, d)
                    for h in range(NH):
                        for cp in range(2):
                            ins = mm(b[half(cp), h * HD:(h + 1) * HD], g.K2[half(cp), 0, h], vtok[half(cp), t, h * HD:(h + 1) * HD])
                    finish(ins)

                def blocks(n, d, lhsT, rhs):
                    b = open_bank(n, p, d)
                    for h in range(NH):
                        for cp in range(2):
                            ins = mm(b[half(cp), h * HD:(h + 1) * HD], lhsT(half(cp), h), rhs(half(cp), h))
                    finish(ins)

                def of(v):
                    return lambda part, h: v[part, h]
                for n in INV:
                    for d in range(2):
                        g = segs[d]
                        D1, Dt, U1t, U2t = g.B3[:, 0], g.A3[:, 0], g.A3[:, 1], g.A3[:, 2]
                        I64 = lambda part, h: identh[part, :]
                        plan = {"D2": (of(Dt), of(D1), ("b0", "b1", "A")), "D2t": (of(D1), of(Dt), ()),
                                "D4": (of(g.D2t), of(g.D2), ("D2", "D2t")), "X2": (of(g.D2t), of(g.X0), ()),
                                "D4t": (of(g.D2), of(g.D2t), ()), "X3": (of(Dt), of(g.X1), ("X2", "D4t")),
                                "D8t": (of(D1), of(Dt), ("D4",)), "X4": (of(g.D2t), of(g.X0), ("X3", "D8t")),
                                "X4t": (of(g.X1), I64, ("X4",)), "Z1": (of(U1t), of(g.X1), ()),
                                "X5": (of(g.D2), of(Dt), ("X4t", "Z1")), "X5t": (of(g.X0), I64, ("X5",)),
                                "Z2": (of(U2t), of(g.X0), ()), "X6": (of(g.D2), of(Dt), ("X5t", "Z2"))}
                        lhsT, rhs, needs = plan[n]
                        for m in needs:
                            wait_result(pe, m, p, d)
                        if n == "X2":
                            pe.wait_ge(s_X1, 2 * p + d + 1)
                        blocks(n, d, lhsT, rhs)
                for d in range(2):
                    g = segs[d]
                    wait_result(pe, "X6", p, d)
                    wait_result(pe, "tA", p, d)
                    wait_result(pe, "AV", p, d)
                    for j in range(2):
                        b = open_bank("WU", p, d, j)
                        for h in range(4 * j, 4 * j + 4):
                            for cp in range(2):
                                ins = mm(b[half(cp), (h % 4) * 2 * HD:(h % 4 + 1) * 2 * HD], g.X1[half(cp), h], g.X[half(cp), h])
                        finish(ins)
                for d in range(2):
                    g, t = segs[d], PAIRS[p][d]
                    for n in (("WU", p, d, 0), ("WU", p, d, 1), ("tB", p, d), ("tK", p, d)):
                        wait_result(pe, *n)
                    for cp in range(2):
                        b = open_bank("G", p, d, cp)
                        for h in range(NH):
                            ins = mm(b[half(h % 2), (h // 2) * 2 * HD:(h // 2 + 1) * 2 * HD], g.WU[half(cp), h, 0:HD], g.B3[half(cp), 1:3, h])
                        finish(ins)
                    for cp in range(2):
                        b = open_bank("H", p, d, cp)
                        for h in range(NH):
                            o = b[half(h % 2), (h // 2) * HD:(h // 2 + 1) * HD]
                            mm(o, g.B3[half(cp), 2, h], g.WU[half(cp), h, HD:2 * HD], True, False)
                            ins = mm(o, g.ktok[half(cp), h], vtok[half(cp), t, h * HD:(h + 1) * HD], False, True)
                        finish(ins)
                for k in range(2):
                    for d in range(2):
                        g, cp = segs[d], chunk(d, k)
                        src = MR[:, cur, d] if k == 0 else MM[:, d]
                        if k == 1:
                            pe.wait_ge(s_mst, 1 + 4 * p + d + 1)
                        elif p == 0:
                            pe.wait_ge(s_mst, 1)
                        elif p == 1:
                            wait_result(pe, "s0")
                        else:
                            pe.wait_ge(s_mst, 1 + 4 * (p - 1) + 2 + d + 1)
                        wait_result(pe, "G", p, d, cp)
                        b = open_bank("seq", p, d, k)
                        for h in range(NH):
                            ins = mm(b[half(h % 2), (h // 2) * HD:(h // 2 + 1) * HD], g.GT[half(h % 2), h // 2, cp], src[half(h % 2), h // 2])
                        finish(ins)
                for d in range(2):
                    g, t = segs[d], PAIRS[p][d]
                    bA, bB = open_early("Ya", p, d), open_early("Yb", p, d)

                    def from_state(hp):
                        for i in range(RC):
                            for cp in range(2):
                                h = 2 * i + hp
                                m = MR[:, cur, d] if cp == chunk(d, 0) else MM[:, d]
                                ins = mm(bB[half(cp), h * HD:(h + 1) * HD], g.QT[half(hp), i, cp], m[half(hp), i])
                        return ins
                    turn = half_done(from_state(0))
                    open_bank("Ya", p, d)
                    for h in range(NH):
                        for cp in range(2):
                            o = bA[half(cp), h * HD:(h + 1) * HD]
                            mm(o, g.B3[half(cp), 1, h], g.WU[half(cp), h, HD:2 * HD], True, False)
                            ins = mm(o, g.K2[half(cp), 1, h], vtok[half(cp), t, h * HD:(h + 1) * HD], False, True)
                    finish(ins)
                    open_bank("Yb", p, d)
                    pe.wait_ge(s_turn, turn)
                    finish(from_state(1))
                if p == 0:
                    pe.wait_ge(s_mst, 5)
                    for d in range(2):
                        b = open_bank("st", d)
                        for i in range(RC):
                            ins = tr(b[0:HD, i * P:(i + 1) * P], MR[:, 1, d, i])
                        finish(ins)

            def row_vectors(nme):
                for cnd in range(2):
                    for h in range(2):
                        b = open_bank("rowb", nme, cnd, h)
                        for j in range(4):
                            k = 4 * h + j
                            col = {"ga1": modv[:, 2 * KT + k, cnd:cnd + 1], "sc2": gscv[:, 1, k, cnd:cnd + 1],
                                   "sh2": modv[:, 3 * KT + k, cnd:cnd + 1], "ga2": modv[:, 5 * KT + k, cnd:cnd + 1]}[nme]
                            ins = mm(b[:, j * P:(j + 1) * P], col.broadcast_to([P, P]), ident[:, :])
                        finish(ins)
            pe.wait_ge(s_g2, 1)
            for nme in ("ga1", "sc2", "sh2"):
                row_vectors(nme)
            pe.wait_ge(s_wo, 160)
            for t in range(NT):
                finish(mm(open_bank("gate", t)[:, :], slg[:, t * P:(t + 1) * P], g2_sb))
                wait_result(pe, "gate", t)
                for j in range(2):
                    b = open_bank("yT", t, j)
                    src = ya if j == 0 else yg[:, t]
                    for i in range(4):
                        ins = tr(b[:, i * P:(i + 1) * P], src[:, i * P:(i + 1) * P])
                    finish(ins)
                for j in range(2):
                    wait_result(pe, "yT", t, j)
                for h in range(2):
                    b = open_bank("out", t, h)
                    for k in range(KT):
                        ins = mm(b[:, :], yT[:, k], ring[:, h, k, :], start=k == 0, stop=k == KT - 1)
                    finish(ins)
                pe.wait_ge(s_h2, t + 1)
                for j in range(2):
                    b = open_bank("hT2", t, j)
                    for i in range(4):
                        ins = tr(b[:, i * P:(i + 1) * P], h2[:, (4 * j + i) * P:(4 * j + i + 1) * P])
                    finish(ins)
                for j in range(2):
                    wait_result(pe, "hT2", t, j)
                b = open_bank("router", t)
                for k in range(KT):
                    ins = mm(b[:, 0:NR], h2T[:, k, t * P:(t + 1) * P], wr[:, k, :], start=k == 0, stop=k == KT - 1)
                finish(ins)
            row_vectors("ga2")

            pe.wait_ge(s_pick, 1)
            b = open_bank("rank")
            for t in range(NT + 1):
                o = b[:, t * NE:(t + 1) * NE]
                for u in range(min(t + 1, NT)):
                    ins = mm(o, upper if u == t else ones, picked[:, u * NE:(u + 1) * NE], start=u == 0, stop=u == min(t, NT - 1))
            finish(ins)

            def expert_products(r):
                pe.wait_ge(s_oh, r + 1)
                b = open_bank("ids", r)
                for j in range(2):
                    for t in range(NT):
                        ins = mm(b[:, 0:NE], onehot[:, j, t], rt_v["o1" if j == 0 else "o2"][:, t], start=(j, t) == (0, 0), stop=(j, t) == (1, NT - 1))
                finish(ins)

                def turn_rows(i):
                    pe.wait_ge(s_xg[i % 3], 16 * (i // 3 + 1))
                    for j in range(2):
                        b = open_bank("xT", i, j)
                        for k in range(4):
                            ins = tr(b[:, k * P:(k + 1) * P], xg[:, i % 3, (4 * j + k) * P:(4 * j + k + 1) * P])
                        finish(ins)

                def down(i):
                    wait_result(pe, "aT", i)
                    pe.wait_ge(s_w2[i % 2], 16 * (i // 2 + 1))
                    for h in range(2):
                        b = open_bank("dn", i, h)
                        for f in range(FT):
                            ins = mm(b[:, :], aT[:, i % 2, f], w2r[:, i % 2, f, h * 512:(h + 1) * 512], start=f == 0, stop=f == FT - 1)
                        finish(ins)

                for e in range(NE):
                    i = r * NE + e
                    if e == 0:
                        turn_rows(i)
                    for j in range(2):
                        wait_result(pe, "xT", i, j)
                    pe.wait_ge(s_w13[i % 2], 32 * (i // 2 + 1))
                    b = open_bank("ug", i)
                    for k in range(KT):
                        ins = mm(b[:, :], xgT[:, i % 2, k], ring[:, i % 2, k, :], start=k == 0, stop=k == KT - 1)
                    finish(ins)
                    if e < NE - 1:
                        turn_rows(i + 1)
                    if e > 0:
                        down(i - 1)
                    wait_result(pe, "ug", i)
                    b = open_bank("aT", i)
                    for f in range(FT):
                        ins = tr(b[:, f * P:(f + 1) * P], ac[:, i % 2, f * P:(f + 1) * P])
                    finish(ins)
                down(i)
            rounds(pe, expert_products)


_INS = ["x_prompt", "x_sample", "state_rwkv", "state_gla", "c", "c_ctx", "norm1_g", "norm2_g", "w_ada", "b_ada", "w_in",
        "w_out", "rw_conv", "rw_w0", "rw_w2", "rw_a0", "rw_a2", "rw_g2", "rw_k_k", "rw_k_a", "rw_r_k", "rw_ln_w", "rw_ln_b",
        "gla_gk2", "gla_gk_b", "gla_norm_g", "moe_w_group", "moe_b_group", "moe_w_expert", "moe_b_expert", "moe_w1",
        "moe_w3", "moe_w2", "final_g"]
_OUTS = [((1, 128, 1024), "float32"), ((1, 512, 1024), "float32"), ((1, 1, 2, 8, 64, 64), "float32"), ((1, 1, 2, 4, 64, 128), "float32")]


def kernel(**inputs):
    import numpy as _np
    import concourse.bacc as _bacc
    from concourse import mybir as _mybir
    from concourse.bass_utils import run_bass_kernel_spmd as _run

    nc = _bacc.Bacc("TRN2", target_bir_lowering=False, num_devices=1)
    arrays, args = {}, []
    for name in _INS:
        a = _np.ascontiguousarray(inputs[name])
        arrays[f"in_{name}_dram"] = a
        args.append(nc.dram_tensor(f"in_{name}_dram", a.shape, _mybir.dt.from_np(a.dtype), kind="ExternalInput").ap())
    for i, (shape, dtype) in enumerate(_OUTS):
        args.append(nc.dram_tensor(f"out_{i}_dram", shape, _mybir.dt.from_np(_np.dtype(dtype)), kind="ExternalOutput").ap())
    trunk_program(nc, *args)
    r = _run(nc, [arrays], core_ids=[0])
    return tuple(r.results[0][f"out_{i}_dram"] for i in range(len(_OUTS)))
```

```python
import concourse.bass as bass
from concourse import mybir
from contextlib import ExitStack


def trunk_program(nc, x_prompt, x_sample, state_rwkv, state_gla, c, c_ctx, norm1_g, norm2_g, w_ada, b_ada,
                  w_in, w_out, rw_conv, rw_w0, rw_w2, rw_a0, rw_a2, rw_g2, rw_k_k, rw_k_a, rw_r_k,
                  rw_ln_w, rw_ln_b, gla_gk2, gla_gk_b, gla_norm_g, moe_w_group, moe_b_group,
                  moe_w_expert, moe_b_expert, moe_w1, moe_w3, moe_w2, final_g,
                  y_prompt, y_sample, new_state_rwkv, new_state_gla):
    f32 = mybir.dt.float32
    i32 = mybir.dt.int32
    u32 = mybir.dt.uint32
    ALU = mybir.AluOpType
    ACT = mybir.ActivationFunctionType
    AXX = mybir.AxisListType.X

    P = 128
    D = x_prompt.shape[2]
    KT = D // P
    CTX = x_prompt.shape[1]
    LAT = x_sample.shape[1]
    NT = (CTX + LAT) // P
    T = CTX + LAT
    GW = 64
    GH = LAT // GW
    RW = rw_ln_w.shape[1]
    HD = rw_r_k.shape[2]
    RC = RW // P
    NH = RW // HD
    DV = gla_norm_g.shape[1]
    GH_N = RW // DV
    GQ = gla_gk2.shape[3]
    GC = GQ // P
    LORA = rw_w2.shape[2]
    GKL = gla_gk2.shape[2]
    NMOD = w_ada.shape[2] // D
    NE = moe_w1.shape[1]
    NG = moe_w_group.shape[2]
    EPG = NE // NG
    F = moe_w1.shape[3]
    FT = F // P
    CH = 64
    EPS = 1e-6
    LN_EPS = 64e-5
    DECAY = -0.606531
    CLAMP = 80.0
    oR, oK, oV = 0, RW, 2 * RW
    oLW, oLA, oLG = 3 * RW, 3 * RW + 2 * LORA, 3 * RW + 4 * LORA
    oQG = oLG + P
    oVG = oQG + 2 * GQ
    oOG = oVG + RW
    oLGK = oOG + RW

    ctx = ExitStack()
    with ctx:
        def sb(name, n, parts=P):
            return ctx.enter_context(nc.sbuf_tensor(name, [parts, n], f32))

        def sem(name):
            return ctx.enter_context(nc.semaphore(name))

        SLAB = KT * 512
        RING = 2
        RAWL = (GH + 2) * (GW + 2)
        RAW = RAWL + CTX + 2
        region0 = sb("region0", RING * SLAB + 2 * RAW + 4)
        region1 = sb("region1", KT * T + 2 * GC * T + 2 * GC * T)
        region2 = sb("region2", NT * RW)
        region3 = sb("region3", NT * D)
        rk_r = sb("rk_r", 2 * RC * T)
        kk_b = sb("kk_b", RC * T)
        vtok_b = sb("vtok_b", NT * RW)
        cl_b = sb("cl_b", 2 * RC * T)
        lora_b = sb("lora_b", 3 * T)
        yg_b = sb("yg_b", NT * RW)
        ident = sb("ident", P)
        blk = sb("blk", P)
        mask = sb("mask", 2 * 2 * HD)
        maskD = sb("maskD", 2 * 2 * HD)
        maskA = sb("maskA", 2 * 3 * HD)
        w2_sb = sb("w2_sb", RW)
        a2_sb = sb("a2_sb", RW)
        gk2_sb = sb("gk2_sb", GQ)
        NV1 = NMOD * KT + 2 * KT + 2 * RC * 2 + 3 * RC + 2 * GC
        NV2 = 9 * 3 * RC
        vec = sb("vec", NV1 + NV2 + 2 * KT)
        mod = sb("mod", NMOD * KT * 2)
        gsc = sb("gsc", 2 * KT * 2)
        bonus = sb("bonus", NT * NH)
        small = sb("small", 128)
        identh = sb("identh", HD)

        ring = region0[:, 0:RING * SLAB].rearrange("p (s k n) -> p s k n", s=RING, k=KT)
        raw = region0[:, RING * SLAB:RING * SLAB + 2 * RAW].rearrange("p (b n) -> p b n", b=2)
        hT = region1[:, 0:KT * T].rearrange("p (k t) -> p k t", k=KT)
        o = KT * T
        qk_g = region1[:, o:o + 2 * GC * T].rearrange("p (c t) -> p c t", t=T)
        gcl = region1[:, o + 2 * GC * T:o + 4 * GC * T].rearrange("p (d c t) -> p d c t", d=2, t=T)
        vg = region2[:, :].rearrange("p (t n) -> p t n", t=NT)
        x_sb = region3[:, :].rearrange("p (t n) -> p t n", t=NT)
        sq = region3[:, 0:RC * T].rearrange("p (c t) -> p c t", t=T)
        vT = region3[:, RC * T:2 * RC * T].rearrange("p (c t) -> p c t", t=T)
        aa = region3[:, :].rearrange("p (d c t) -> p d c t", d=2, t=T)
        rT = rk_r[:, 0:RC * T].rearrange("p (c t) -> p c t", t=T)
        kT = rk_r[:, RC * T:].rearrange("p (c t) -> p c t", t=T)
        kkT = kk_b[:, :].rearrange("p (c t) -> p c t", t=T)
        vtok = vtok_b[:, :].rearrange("p (t n) -> p t n", t=NT)
        cl = cl_b[:, :].rearrange("p (d c t) -> p d c t", d=2, t=T)
        prod = cl_b[:, 0:RC * T].rearrange("p (c t) -> p c t", t=T)
        goacc = cl_b[:, RC * T:].rearrange("p (t n) -> p t n", t=NT)
        tlw = lora_b[:, 0:T]
        laT = lora_b[:, T:2 * T]
        slg = lora_b[:, 2 * T:3 * T]
        yg = yg_b[:, :].rearrange("p (t n) -> p t n", t=NT)
        vb_ada = 0
        vn1 = NMOD * KT
        vn2 = vn1 + KT
        vw0 = vn2 + KT
        va0 = vw0 + 2 * RC
        vkk = va0 + 2 * RC
        vka = vkk + RC
        vrk = vka + RC
        vgb = vrk + RC
        vcv = NV1
        vcond = NV1 + NV2
        modv = mod[:, :].rearrange("p (b c) -> p b c", c=2)
        gscv = gsc[:, :].rearrange("p (m b c) -> p m b c", m=2, c=2)
        condv = vec[:, vcond:vcond + 2 * KT].rearrange("p (c k) -> p c k", c=2)
        eps6 = small[:, 0:1]
        epsln = small[:, 1:2]
        oneka = small[:, 4:4 + RC]
        ssum = small[:, 8:8 + NT]
        rstd = small[:, 16:16 + NT]
        scond = small[:, 32:32 + 2 * KT]
        condt = scond.rearrange("p (c k) -> p c k", c=2)
        stmp = small[:, 48:48 + 2 * KT]

        pcs = small[:, 64:80].rearrange("p (d h c) -> p d h c", d=2, c=2)

        GW_N = 2400

        def gla_view(d, off, n):
            return region3[:, d * GW_N + off:d * GW_N + off + n]

        class G:
            pass
        gws = []
        for d in range(2):
            g = G()
            g.q = gla_view(d, 0, 256).rearrange("p (c t) -> p c t", c=GC)
            g.k = gla_view(d, 256, 256).rearrange("p (c t) -> p c t", c=GC)
            g.ktok = gla_view(d, 512, 256).rearrange("p (h k) -> p h k", h=GH_N)
            g.sT = gla_view(d, 768, 256).rearrange("p (h i) -> p h i", h=GH_N)
            g.df = gla_view(d, 1024, 256)
            g.e1 = gla_view(d, 1280, 256)
            g.e2 = gla_view(d, 1536, 256)
            g.m = gla_view(d, 1792, 4).rearrange("p (c j) -> p c j", c=GC)
            g.em = gla_view(d, 1796, 4).rearrange("p (c j) -> p c j", c=GC)
            g.pc = gla_view(d, 1800, 4).rearrange("p (c j) -> p c j", c=GC)
            g.kv = gla_view(d, 1808, 512).rearrange("p (c j v) -> p c j v", c=GC, j=2)
            gws.append(g)
        GM = region1[:, 1280:1280 + 3584].rearrange("p (n d c v) -> p n d c v", d=2, c=GC, v=DV)
        gng = region1[:, 1280 + 3584:1280 + 3584 + DV]
        smask = region1[:, 0:2 * T].rearrange("p (d t) -> p d t", d=2)
        gmask = lora_b[:, 0:2 * T].rearrange("p (d t) -> p d t", d=2)

        segs = []
        for d, reg in enumerate((region0, region1)):
            g = G()

            def view(off, n, pat=None, **kw):
                v = reg[:, off:off + n]
                return v.rearrange(pat, **kw) if pat else v
            g.AR = view(0, 1024, "p (a h c i) -> p h c a i", h=RC, c=2, a=2)
            g.b = view(1024, 512, "p (h t) -> p h t", h=RC)
            g.k = view(1536, 512, "p (h t) -> p h t", h=RC)
            g.WU = view(1024, 1024, "p (h n) -> p h n", h=NH)
            g.D2 = view(1024, 512, "p (h i) -> p h i", h=NH)
            g.XB = view(7680, 1024, "p (h n) -> p h n", h=NH)
            g.X = view(2048, 1024, "p (h n) -> p h n", h=NH)
            g.t2 = view(2048, 512, "p (h t) -> p h t", h=RC)
            g.B3 = view(3072, 1536, "p (a h i) -> p a h i", a=3, h=NH)
            g.ktok = view(4608, 512, "p (h k) -> p h k", h=NH)
            g.K2 = view(5120, 1024, "p (a h i) -> p a h i", a=2, h=NH)
            g.A3 = view(6144, 1536, "p (a h i) -> p a h i", a=3, h=NH)
            g.GT = view(6144, 512, "p (h c i) -> p h c i", h=RC, c=2)
            g.QT = view(6656, 512, "p (h c i) -> p h c i", h=RC, c=2)
            g.H = view(7168, 512, "p (c h i) -> p c h i", c=2, h=RC)
            g.D2t = view(8192, 512, "p (h i) -> p h i", h=NH)
            g.X0 = view(8704, 512, "p (h i) -> p h i", h=NH)
            g.X1 = view(9216, 512, "p (h i) -> p h i", h=NH)
            g.E1 = view(7680, 528, "p (h i) -> p h i", h=2 * RC)
            g.E2 = view(8208, 512, "p (h t) -> p h t", h=RC)
            g.t1 = view(8720, 512, "p (h t) -> p h t", h=RC)
            g.tmp = view(7680, 256, "p (h v) -> p h v", h=RC)
            segs.append(g)
        BL = segs[0].D2t[:, :, :].rearrange("p h i -> p (h i)")[:, 0:256]
        BX = segs[0].D2t[:, :, :].rearrange("p h i -> p (h i)")[:, 256:512]
        BXt = segs[1].D2t[:, :, :].rearrange("p h i -> p (h i)")[:, 0:256]
        BT = segs[1].D2t[:, :, :].rearrange("p h i -> p (h i)")[:, 256:512]
        BXW = segs[1].X0[:, :, :].rearrange("p h i -> p (h i)")
        HS = HD * HD + HD
        a_dram = nc.dram_tensor("a_rows_dram", (2, 2 * NH * HS), f32, kind="Internal").ap()
        inv_dram = nc.dram_tensor("inverse_rows_dram", (4, 2 * NH * HS), f32, kind="Internal").ap()

        def chunk_rows(m, cp):
            return m[cp * NH * HS:(cp + 1) * NH * HS].rearrange("(h x) -> h x", h=NH)[:, 0:HD * HD].rearrange("h (i j) -> i h j", j=HD)

        def diagonal_blocks(m):
            return bass.AP(tensor=m.tensor, offset=m.offset, ap=[[16 * HD + 16, 2 * NH * HD // 16], [HD, 16], [1, 16]])
        MR = lora_b[:, 0:1024].rearrange("p (n d h v) -> p n d h v", n=2, d=2, h=RC)
        MM = region1[:, 9728:10240].rearrange("p (d h v) -> p d h v", d=2, h=RC)
        s0buf = region2[0:HD, 512:512 + 2 * RW].rearrange("v (d n) -> v d n", d=2)
        stbuf = region2[0:HD, 1536:1536 + 2 * RW].rearrange("v (d n) -> v d n", d=2)
        yacc = region2[:, :].rearrange("p (t n) -> p t n", t=NT)

        gbuf = region1[:, 0:6 * D].rearrange("p (v c n) -> p v c n", v=3, c=2)
        xt = region1[:, 6 * D:7 * D]
        ya = region1[:, 7 * D:7 * D + RW]
        rs8 = small[:, 116:124]
        ss1 = small[:, 28:29]
        grs20 = small[:, 84:84 + NT * GH_N]
        sqj = region1[:, 7 * D + RW:7 * D + 2 * RW]
        yT = region1[:, 8 * D:9 * D].rearrange("p (k t) -> p k t", k=KT)
        h2 = region1[:, 9 * D:10 * D]
        lnw = region0[:, RING * SLAB:RING * SLAB + RW]
        lnb = region0[:, RING * SLAB + RW:RING * SLAB + 2 * RW]
        g2_sb = region0[:, RING * SLAB + 2 * RW:RING * SLAB + 3 * RW]
        NR = NG + NE
        wr = w2_sb[:, 0:KT * NR].rearrange("p (k n) -> p k n", k=KT)
        br = w2_sb[:, KT * NR:KT * NR + NR]
        lgt = w2_sb[:, 200:200 + NT * NR].rearrange("p (t n) -> p t n", t=NT)
        picked = w2_sb[:, 304:304 + NT * NE]
        picked_v = picked.rearrange("p (t n) -> p t n", t=NT)
        rtmp = w2_sb[:, 384:384 + NT * NE].rearrange("p (t n) -> p t n", t=NT)
        slot0 = w2_sb[:, 464:464 + NE]
        tokid = w2_sb[:, 480:480 + NT]
        upper = maskA[:, 0:P]
        ones = maskA[:, P:2 * P]
        iota = maskA[:, 2 * P:3 * P]
        onehot = vtok_b[:, 0:2 * NT * P].rearrange("p (j t s) -> p j t s", j=2, t=NT)
        rt = a2_sb[:, :]
        fg = kk_b[:, 0:D]
        junk = kk_b[:, D:2 * D]
        x1 = region3[:, :].rearrange("p (t n) -> p t n", t=NT)
        xg = rk_r[:, 0:3 * D].rearrange("p (s n) -> p s n", s=3)
        xgT = rk_r[:, 3 * D:5 * D].rearrange("p (s k t) -> p s k t", s=2, k=KT)
        yg2 = rk_r[:, 0:4 * D].rearrange("p (s j n) -> p s j n", s=2, j=2)
        yo = cl_b[:, 0:2 * D].rearrange("p (s n) -> p s n", s=2)
        idx = ctx.enter_context(nc.sbuf_tensor("slot_tokens", [P, NE], u32))
        pos = ctx.enter_context(nc.sbuf_tensor("pick_slots", [P, 2 * NT], u32))
        most = ctx.enter_context(nc.sbuf_tensor("largest_count", [1, 1], i32))
        h2_dram = nc.dram_tensor("h2_rows_dram", (T, D), f32, kind="Internal").ap()
        ys_dram = nc.dram_tensor("expert_rows_dram", (NE * P, D), f32, kind="Internal").ap()
        h2T = rk_r[:, :].rearrange("p (k t) -> p k t", k=KT)
        acc = cl_b[:, :].rearrange("p (t n) -> p t n", t=NT)
        w2r = region1[:, 0:4 * D].rearrange("p (s f n) -> p s f n", s=2, f=FT)
        ga2b = region1[:, 4 * D:6 * D].rearrange("p (c n) -> p c n", c=2)
        sg = region1[:, 6 * D:6 * D + 2 * F].rearrange("p (s f) -> p s f", s=2)
        ac = region1[:, 7 * D:7 * D + 2 * F].rearrange("p (s f) -> p s f", s=2)
        aT = region1[:, 8 * D:8 * D + 2 * F].rearrange("p (s f t) -> p s f t", s=2, f=FT)

        NB = 8
        PS = [ctx.enter_context(nc.psum_tensor(f"bank{i}", [P, 512], f32)) for i in range(NB)]
        filled = sem("filled")
        drained = [sem(f"drained{i}") for i in range(NB)]

        PAIRS = [(0, 0)] + [(i, NT - i) for i in range(1, NT)]

        jobs = [("rows",)]
        jobs += [("ada", 0)]
        for n in range(4):
            jobs += ([("ada", n + 1)] if n < 3 else []) + [("adaT", n)]
        jobs += [("hl", k) for k in range(KT)] + [("hc", 0), ("hc", 1)]
        chan = ["q0", "q1", "g0", "g1"]
        tail = [f"r{i}" for i in range(RC)] + [f"k{i}" for i in range(RC)] + [f"v{i}" for i in range(RC)] + ["lw", "la", "lg"]
        for n in chan:
            jobs += [("pl", n), ("pc", n)]
        jobs += [("vg", t) for t in range(NT)] + [("og", t) for t in range(NT)]
        jobs += [("lgkl",), ("lgkc",)]
        jobs += [("gkl", d, i) for d in range(2) for i in range(GC)] + [("gkc",)]
        for n in tail:
            jobs += [("pl", n), ("pc", n)]
        jobs += [("kl", i) for i in range(RC)] + [("kc",), ("bonus",)] + [("vt", t) for t in range(NT)]
        for p in range(NT):
            jobs += [("g1", p, d) for d in range(2)]
            for d in range(2):
                jobs += [("goA", p, d), ("gkv", p, d)]
            if p < NT - 1:
                jobs += [("ada", 4 + p)]
            jobs += [("goB", p, 0), ("goB", p, 1)]
            if p < NT - 1:
                jobs += [("adaT", 4 + p)]
            if p == 2:
                jobs += [("wl", 0, i) for i in range(RC)] + [("wc", 0)]
        for d in range(2):
            if d == 1:
                jobs += [("wl", d, i) for i in range(RC)] + [("wc", d)]
            jobs += [("al", d, i) for i in range(RC)] + [("ac", d)]
        jobs += [("ada", 4 + NT - 1)]
        for n in range(4 + NT - 1, 2 * NMOD):
            jobs += ([("ada", n + 1)] if n < 2 * NMOD - 1 else []) + [("adaT", n)]
        SEG = ["tA", "tB", "tK"]
        INV = ["Z1", "X5", "X5t", "Z2", "X6"]
        for p in range(NT):
            if p == 1:
                jobs += [("s0",)]
            for d in range(2):
                jobs += [(n, p, d) for n in ("b0", "A", "b1", "k0", "k1")]
            for d in range(2):
                jobs += [(n, p, d) for n in ("tA", "tB", "tK", "AV")]
            for n in INV:
                jobs += [(n, p, d) for d in range(2)]
            for d in range(2):
                jobs += [("WU", p, d, 0), ("WU", p, d, 1)]
            for d in range(2):
                jobs += [("G", p, d, 0), ("G", p, d, 1), ("H", p, d, 0), ("H", p, d, 1)]
            jobs += [("seq", p, d, 0) for d in range(2)]
            jobs += [("seq", p, d, 1) for d in range(2)]
            for d in range(2):
                jobs += [("Ya", p, d), ("Yb", p, d)]
            if p == 0:
                jobs += [("st", 0), ("st", 1)]
        jobs += [("rowb", v, cnd, h) for v in ("ga1", "sc2", "sh2") for cnd in range(2) for h in range(2)]
        jobs += [("gate", 0), ("yT", 0, 0), ("yT", 0, 1)]
        for t in range(NT):
            if t + 1 < NT:
                jobs += [("gate", t + 1)]
            jobs += [("out", t, 0), ("out", t, 1)]
            if t + 1 < NT:
                jobs += [("yT", t + 1, 0), ("yT", t + 1, 1)]
            if t >= 1:
                jobs += [("hT2", t - 1, 0), ("hT2", t - 1, 1), ("router", t - 1)]
        jobs += [("hT2", NT - 1, 0), ("hT2", NT - 1, 1), ("router", NT - 1)]
        jobs += [("rowb", "ga2", cnd, h) for cnd in range(2) for h in range(2)]
        jobs += [("rank",)]
        for r in range(NT):
            jobs += [("ids", r)]
            for e in range(NE):
                i = r * NE + e
                if e == 0:
                    jobs += [("xT", i, 0), ("xT", i, 1)]
                jobs += [("ug", i)]
                if e < NE - 1:
                    jobs += [("xT", i + 1, 0), ("xT", i + 1, 1)]
                if e > 0:
                    jobs += [("dn", i - 1, 0), ("dn", i - 1, 1)]
                jobs += [("aT", i)]
            jobs += [("dn", i, 0), ("dn", i, 1)]
        J = {k: i for i, k in enumerate(jobs)}
        assert len(J) == len(jobs)

        def bank(key):
            return PS[J[key] % NB]

        def wait_filled(eng, *key):
            eng.wait_ge(filled, J[key] + 1)

        def wait_result(eng, *key):
            eng.wait_ge(drained[J[key] % NB], J[key] // NB + 1)

        slabs = [("ada", n) for n in range(4)] + ["qk", "vg", "og", "lgk", "r", "k", "v", "lora"] + \
                [("ada", n) for n in range(4, 2 * NMOD)]
        NS1 = len(slabs)
        slab_in = [sem(f"slab_in{i}") for i in range(RING)]

        s_small = sem("small_loads")
        s_x = sem("x_loads")
        s_const = sem("constants")
        s_ident = sem("identity_ready")
        s_xn = sem("xn_ready")
        s_cond = sem("cond_ready")
        s_g1 = sem("gain1_ready")
        s_adarow = sem("ada_rows")
        s_conv = sem("conv_done")
        s_kk = sem("kk_squares")
        s_prod = sem("bonus_products")
        s_lora = sem("lora_inputs")
        s_lgx = sem("gla_gates_in")
        s_lgt = sem("gla_gates_mid")
        s_gcl = sem("gla_cumsums")
        s_wx = sem("decay_in")
        s_wm = sem("decay_mid")
        s_cl = sem("decay_cumsums")
        s_dve = sem("vector_steps")
        s_act = sem("scalar_steps")
        s_pool = sem("pool_steps")

        block = ctx.enter_context(nc.Block())

        def steps(eng, chain):
            count = {}

            def tell(ins, s):
                count[s.name] = count.get(s.name, 0) + 1
                ins.then_inc(s, 1)
                eng.wait_ge(s, count[s.name])

            def own(ins):
                tell(ins, chain)

            def out_of(ins, *key):
                ins.then_inc(drained[J[key] % NB], 1)
                eng.wait_ge(drained[J[key] % NB], J[key] // NB + 1)
            return own, tell, out_of


        s_turn = sem("array_half_done")
        s_eps = sem("epsilons")
        s_ogx = sem("og_bounded")
        s_xnr = sem("x_normalised")
        s_bon = sem("bonus_inputs")
        s_gz = sem("gla_zero_states")
        s_g2 = sem("adaln_complete")
        s_zero_src = sem("zero_rows_ready")
        s_zd = sem("zero_rows_stored")
        s_blk = [sem(f"block_rows_stored{d}") for d in range(2)]
        s_L = sem("blocks_in")
        s_sub = sem("blocks_inverted")
        s_back = [sem(f"inverse_blocks_stored{k}") for k in range(2)]
        s_zx = sem("inverse_zeros")
        s_inv = [sem(f"inverse_in{k}") for k in range(2)]
        MCUR = [0] + [(p - 1) % 2 for p in range(1, NT)]
        lgkT = kk_b[0:48, 0:T]

        def adarow(n):
            return region0[0:2, RING * SLAB + (n % 2) * 512:RING * SLAB + (n % 2) * 512 + 512]
        rt_v, at_ = {}, 0
        for nme, shp in (("pref", (NG,)), ("hg", (NT, NG)), ("mg", (NT,)), ("gd", (NT, NG)), ("ge", (NT, NG)), ("sel", (NT, EPG, NG)),
                         ("es", (NT, EPG)), ("h1", (NT, EPG)), ("h2", (NT, EPG)), ("m", (NT,)), ("m1", (NT,)), ("m2", (NT,)),
                         ("E", (NT,)), ("w1", (NT,)), ("w2", (NT,)), ("o1", (NT, NE)), ("o2", (NT, NE)), ("rk", (2 * NT,)),
                         ("ps", (2 * NT,)), ("wt", (2 * NT,)), ("in", (2 * NT,)), ("ib", (2 * NT,)), ("wr", (2 * NT,)), ("mc", (1,))):
            n_ = 1
            for z in shp:
                n_ *= z
            v_ = a2_sb[:, at_:at_ + n_]
            if len(shp) == 2:
                v_ = v_.rearrange("p (t n) -> p t n", t=shp[0])
            if len(shp) == 3:
                v_ = v_.rearrange("p (t n m) -> p t n m", t=shp[0], n=shp[1])
            rt_v[nme] = v_
            at_ += n_
        first_ids = maskD[:, 0:NT * NE].rearrange("p (t n) -> p t n", t=NT)
        second_ids = maskD[:, NT * NE:2 * NT * NE].rearrange("p (t n) -> p t n", t=NT)
        LAST = {("ada", n): ("ada", n) for n in range(2 * NMOD)}
        LAST.update({"qk": ("pc", "g1"), "vg": ("vg", NT - 1), "og": ("og", NT - 1), "lgk": ("lgkc",), "r": ("pc", f"r{RC - 1}"),
                     "k": ("pc", f"k{RC - 1}"), "v": ("pc", f"v{RC - 1}"), "lora": ("pc", "lg")})
        s_condt = sem("condition_columns")
        s_rawz = sem("conv_borders_zero")
        s_sig = sem("silu_gate")
        s_gm = sem("gla_masks")
        s_kkn = sem("kk_normalised")
        s_gseg = sem("gla_exponents")
        s_gexp = sem("gla_exps")
        s_gq = sem("gla_qk_scaled")
        s_gM = sem("gla_decayed_states")
        s_gst = sem("gla_context_states")
        s_gin = sem("gla_states_loaded")
        s_gfin = sem("gla_sums")
        s_grs = sem("gla_rstd")
        s_gdone = sem("gla_done")
        s_seg = sem("segment_start")
        s_E = sem("segment_exps")
        s_t1 = sem("segment_products")
        s_f = sem("segment_k_factors")
        s_ops = sem("segment_operands")
        s_mst = sem("rwkv_state_steps")
        s_zero = sem("rwkv_zero_states")
        s_rin = sem("rwkv_states_loaded")
        s_rst = sem("rwkv_states_out")
        s_gout = sem("gla_states_out")
        s_wo = sem("late_loads")
        s_wout = sem("w_out_loaded")
        s_rwdone = sem("rwkv_done")
        s_y = sem("head_norm_stats")
        s_yr = sem("head_norm_rstd")
        s_ya = sem("rwkv_rows")
        s_xt = sem("x_again")
        s_x1 = sem("x1_rows")
        s_x1r = sem("x1_rstd")
        s_h2 = sem("h2_rows")
        s_rg = sem("router_in")
        s_rex = sem("router_exps")
        s_sg = sem("gate_exps")
        s_ac = sem("expert_acts")
        s_w13 = [sem(f"w13_in{i}") for i in range(2)]
        s_w2 = [sem(f"w2_in{i}") for i in range(2)]
        s_h2d = sem("h2_stored")
        s_tri = sem("routing_constants")
        s_pick = sem("picks_ready")
        s_most = sem("largest_count_ready")
        s_oh = sem("slot_onehots")
        s_idx = sem("slot_tokens_ready")
        s_xg = [sem(f"gathered{i}") for i in range(3)]
        s_ys = [sem(f"expert_rows_stored{i}") for i in range(2)]
        s_moe = sem("experts_done")
        s_yg = [sem(f"expert_rows_in{i}") for i in range(2)]
        s_pos = sem("pick_slots_ready")
        s_comb = sem("expert_rows_added")
        s_finr = sem("final_rstd")
        s_yout = sem("y_out")
        s_ydma = sem("y_stored")

        def first(p, d):
            return d == 0 if p == 0 else p < NT - p

        def rounds(eng, body):
            body(0)
            eng.wait_ge(s_most, 1)
            n = eng.value_load(most[0:1, 0:1], min_val=0, max_val=T)
            for r in range(1, NT):
                with eng.If(n > r * P):
                    body(r)

        def chunk(d, k):
            return k if d == 0 else 1 - k

        def bc(ap, axis, n):
            v = ap.unsqueeze(axis)
            shape = list(v.shape)
            shape[axis] = n
            return v.broadcast_to(shape)

        w_in_v = w_in[0].rearrange("(k p) n -> p k n", p=P)
        w_out_v = w_out[0].rearrange("(k p) n -> p k n", p=P)
        w_ada_v = w_ada[0].rearrange("(k p) n -> p k n", p=P)

        def slab_dmas(sp, i):
            what = slabs[i]
            s = i % RING
            if isinstance(what, tuple):
                n = what[1]
                sp.dma_start(ring[:, s], w_ada_v[:, :, n * 512:(n + 1) * 512]).then_inc(slab_in[s], 16)
                return
            lo, n = {"qk": (oQG, 512), "vg": (oVG, 512), "og": (oOG, 512), "lgk": (oLGK, 2 * GKL), "r": (oR, 512),
                     "k": (oK, 512), "v": (oV, 512), "lora": (oLW, 384)}[what]
            sp.dma_start(ring[:, s, :, 0:n], w_in_v[:, :, lo:lo + n]).then_inc(slab_in[s], 16)

        @block.sync
        def _(sp):
            rows1 = [(b_ada[0].rearrange("(r c) -> r c", c=P), NMOD * KT), (norm1_g[0].rearrange("(r c) -> r c", c=P), KT),
                     (norm2_g[0].rearrange("(r c) -> r c", c=P), KT),
                     (rw_w0[0].rearrange("d (r c) -> (d r) c", c=P), 2 * RC), (rw_a0[0].rearrange("d (r c) -> (d r) c", c=P), 2 * RC),
                     (rw_k_k[0].rearrange("(r c) -> r c", c=P), RC), (rw_k_a[0].rearrange("(r c) -> r c", c=P), RC),
                     (rw_r_k[0].rearrange("(r a) c -> r (a c)", a=2), RC), (gla_gk_b[0].rearrange("d (r c) -> (d r) c", c=P), 2 * GC)]
            at = 0
            for src, n in rows1:
                sp.dma_start(region1[at:at + n, 0:P], src).then_inc(s_small, 16)
                at += n
            sp.dma_start(region1[0:NV2, P:2 * P], rw_conv[0].rearrange("i j (r c) -> (i j r) c", c=P)).then_inc(s_small, 16)
            sp.dma_start(region1[0:KT, 2 * P:3 * P], c_ctx.rearrange("(r c) -> r c", c=P)).then_inc(s_small, 16)
            sp.dma_start(region1[KT:2 * KT, 2 * P:3 * P], c[0].rearrange("(r c) -> r c", c=P)).then_inc(s_small, 16)
            sp.dma_start(w2_sb[:, :], rw_w2[0].rearrange("d k n -> (d k) n")).then_inc(s_small, 16)
            sp.dma_start(a2_sb[:, :], rw_a2[0].rearrange("d k n -> (d k) n")).then_inc(s_small, 16)
            sp.dma_start(gk2_sb[0:GKL, :], gla_gk2[0, 0]).then_inc(s_small, 16)
            sp.dma_start(gk2_sb[32:32 + GKL, :], gla_gk2[0, 1]).then_inc(s_small, 16)
            for i in range(RING):
                slab_dmas(sp, i)
            sp.dma_start(x_sb[:, 0], x_prompt[0]).then_inc(s_x, 16)
            for t in range(1, NT):
                sp.dma_start(x_sb[:, t], x_sample[0, (t - 1) * P:t * P, :]).then_inc(s_x, 16)
            for i in range(RING, NS1):
                if i == 2 * RING:
                    sp.wait_ge(s_zero_src, 1)
                    for n in range(4):
                        sp.dma_start(inv_dram[n].rearrange("(p x) -> p x", p=P), cl_b[:, 0:2 * NH * HS // P]).then_inc(s_zd, 16)
                wait_filled(sp, *LAST[slabs[i - RING]])
                slab_dmas(sp, i)
            sp.wait_ge(s_gdone, 1)
            for d in range(2):
                sp.dma_start(s0buf[:, d].rearrange("v (h k) -> v h k", h=NH), state_rwkv[0, 0, d].rearrange("h v k -> v h k")).then_inc(s_rin, 16)
            for p in range(NT):
                for d in range(2):
                    g = segs[d]
                    if d == 0:
                        wait_result(sp, "A", p, 0)
                    else:
                        wait_result(sp, "b0", p, 1)
                        wait_result(sp, "b1", p, 1)
                    if p >= 1:
                        sp.wait_ge(s_L, 32 * p)
                    src = g.A3[:, 0] if d == 0 else g.B3[:, 0]
                    for cp in range(2):
                        sp.dma_start(chunk_rows(a_dram[d], cp), src[cp * HD:(cp + 1) * HD]).then_inc(s_blk[d], 16)
                for d in range(2):
                    sp.wait_ge(s_blk[d], 32 * (p + 1))
                    if d == 0:
                        sp.wait_ge(s_ops, 2 * p + 2)
                    sp.dma_start(BL[64 * d:64 * d + 64, :].rearrange("p (i j) -> p i j", i=16), diagonal_blocks(a_dram[d])).then_inc(s_L, 16)
                sp.wait_ge(s_sub, p + 1)
                if p == 0:
                    sp.wait_ge(s_zd, 64)
                for k in range(2):
                    if p >= 1:
                        sp.wait_ge(s_inv[k], 64 * p)
                    for d in range(2):
                        src = BXt if d == k else BX
                        sp.dma_start(diagonal_blocks(inv_dram[2 * k + d]), src[64 * d:64 * d + 64, :].rearrange("p (i j) -> p i j", i=16)).then_inc(s_back[k], 16)
                for k in range(2):
                    sp.wait_ge(s_back[k], 32 * (p + 1))
                    for d in range(2):
                        if k == 1:
                            wait_filled(sp, "tK", p, d)
                        for cp in range(2):
                            sc = slice(cp * HD, (cp + 1) * HD)
                            dst = segs[d].X1[sc] if k == 0 else segs[d].D2[sc]
                            sp.dma_start(dst, chunk_rows(inv_dram[2 * k + d], cp)).then_inc(s_inv[k], 16)
            sp.wait_ge(s_rwdone, 1)
            sp.dma_start(lnw, rw_ln_w[0].partition_broadcast(P)).then_inc(s_wo, 16)
            sp.dma_start(lnb, rw_ln_b[0].partition_broadcast(P)).then_inc(s_wo, 16)
            sp.dma_start(g2_sb, rw_g2[0]).then_inc(s_wo, 16)
            sp.dma_start(wr[:, :, 0:NG], moe_w_group[0].rearrange("(k p) n -> p k n", p=P)).then_inc(s_wo, 16)
            sp.dma_start(wr[:, :, NG:NR], moe_w_expert[0].rearrange("(k p) n -> p k n", p=P)).then_inc(s_wo, 16)
            sp.dma_start(br[:, 0:NG], moe_b_group[0].partition_broadcast(P)).then_inc(s_wo, 16)
            sp.dma_start(br[:, NG:NR], moe_b_expert[0].partition_broadcast(P)).then_inc(s_wo, 16)
            sp.dma_start(fg, final_g.partition_broadcast(P)).then_inc(s_wo, 16)
            for h in range(2):
                sp.dma_start(ring[:, h], w_out_v[:, :, h * 512:(h + 1) * 512]).then_inc(s_wout, 16)
            sp.dma_start(xt, x_prompt[0]).then_inc(s_xt, 16)
            for t in range(NT):
                if t < NT - 1:
                    sp.wait_ge(s_x1, t + 1)
                    sp.dma_start(xt, x_sample[0, t * P:(t + 1) * P, :]).then_inc(s_xt, 16)
                sp.wait_ge(s_h2, t + 1)
                sp.dma_start(h2_dram[t * P:(t + 1) * P, :], h2).then_inc(s_h2d, 16)

            def load_experts(r):
                for e in range(NE):
                    i = r * NE + e
                    s = i % 2
                    if i < 2:
                        wait_filled(sp, "router", NT - 1)
                    else:
                        wait_filled(sp, "ug", i - 2)
                    sp.dma_start(ring[:, s, :, 0:F], moe_w1[0, e].rearrange("(k p) n -> p k n", p=P)).then_inc(s_w13[s], 16)
                    sp.dma_start(ring[:, s, :, F:2 * F], moe_w3[0, e].rearrange("(k p) n -> p k n", p=P)).then_inc(s_w13[s], 16)
                    if i >= 2:
                        wait_filled(sp, "dn", i - 2, 1)
                    sp.dma_start(w2r[:, s], moe_w2[0, e].rearrange("(f p) n -> p f n", p=P)).then_inc(s_w2[s], 16)
                for t in range(NT):
                    sp.wait_ge(s_yout, r * NT + t + 1)
                    sp.dma_start(y_prompt[0] if t == 0 else y_sample[0, (t - 1) * P:t * P, :], acc[:, t]).then_inc(s_ydma, 16)
                sp.wait_ge(s_ydma, 16 * (r + 1) * NT)
            rounds(sp, load_experts)

        @block.gpsimd
        def _(pool):
            own, tell, _o = steps(pool, s_pool)

            def select(ap, pattern, base, ch, op, fill=0.0):
                own(pool.affine_select(out=ap, in_=ap, compare_op=op, fill=fill, base=base, pattern=pattern, channel_multiplier=ch))
            own(pool.memset(ident[:, :], 0.0))
            select(ident[:, :], [[-1, P]], 0, 1, ALU.not_equal, 1.0)
            tell(pool.memset(small[:, 3:4], 1.0), s_ident)
            tell(pool.memset(cl_b[:, 0:2 * NH * HS // P], 0.0), s_zero_src)
            own(pool.memset(blk[:, :], 0.0))
            own(pool.memset(blk[0:HD, 0:HD], 1.0))
            own(pool.memset(blk[HD:P, HD:P], 1.0))
            own(pool.tensor_tensor(identh[:, :], ident[:, 0:HD], ident[:, HD:P], ALU.add))
            own(pool.memset(mask[:, :], 1.0))
            own(pool.memset(maskA[:, :], 1.0))
            mk = mask[:, :].rearrange("p (d a i) -> p d a i", d=2, a=2)
            mD = maskD[:, :].rearrange("p (d a i) -> p d a i", d=2, a=2)
            mA = maskA[:, :].rearrange("p (d a i) -> p d a i", d=2, a=3)
            for half in (slice(0, HD), slice(HD, P)):
                select(mk[half, 0, 0], [[1, HD]], -1, -1, ALU.is_ge)
                select(mk[half, 0, 1], [[1, HD]], 0, -1, ALU.is_ge)
                select(mk[half, 1, 0], [[-1, HD]], -1, 1, ALU.is_ge)
                select(mk[half, 1, 1], [[-1, HD]], 0, 1, ALU.is_ge)
                for d in range(2):
                    for a, w in ((0, 16), (1, 32)):
                        v = mA[half, d, a].rearrange("p (n w) -> p n w", w=w)
                        select(v, [[-w, HD // w], [0, w]], 0, 1, ALU.is_ge)
                        select(v, [[w, HD // w], [0, w]], w - 1, -1, ALU.is_ge)
            for d in range(2):
                own(pool.tensor_tensor(mD[:, d, 0], mk[:, d, 0], mA[:, d, 0], ALU.mult))
                own(pool.tensor_copy(mD[:, d, 1], mk[:, d, 1]))
                own(pool.tensor_tensor(mA[:, d, 2], mA[:, d, 2], mA[:, d, 1], ALU.subtract))
                own(pool.tensor_tensor(mA[:, d, 1], mA[:, d, 1], mA[:, d, 0], ALU.subtract))
                for a in range(3):
                    own(pool.tensor_tensor(mA[:, d, a], mA[:, d, a], mk[:, 1 - d, 0], ALU.mult))
            tell(pool.memset(small[:, 2:3], 1.0), s_const)
            pool.wait_ge(s_g1, 1)
            tell(pool.memset(region0[:, RING * SLAB:RING * SLAB + 2 * RAW], 0.0), s_rawz)
            pool.wait_ge(s_sig, 3)
            tell(pool.tensor_tensor(yg_b[:, :], yg_b[:, :], cl_b[:, RC * T:2 * RC * T], ALU.mult), s_sig)
            for i in range(RC):
                pool.wait_ge(s_kk, i + 1)
                tell(pool.tensor_tensor(sq[:, i], kkT[:, i], kkT[:, i], ALU.mult), s_prod)
            for p in range(NT):
                for d in range(2):
                    g, t = gws[d], PAIRS[p][d]
                    pool.wait_ge(s_gexp, 2 * p + d + 1)
                    if p >= 1:
                        wait_filled(pool, "goB", p - 1, 1)
                    own(pool.tensor_tensor(g.q, qk_g[:, 0:GC, t * P:(t + 1) * P], g.e1.rearrange("p (c t) -> p c t", c=GC), ALU.mult))
                    tell(pool.tensor_tensor(g.k, qk_g[:, GC:2 * GC, t * P:(t + 1) * P], g.e2.rearrange("p (c t) -> p c t", c=GC), ALU.mult), s_gq)
            for p in range(NT):
                for d in range(2):
                    g, t = segs[d], PAIRS[p][d]
                    tok = slice(t * P, (t + 1) * P)
                    pool.wait_ge(s_seg, 2 * p + d + 1)
                    tell(pool.tensor_tensor(g.t1, kkT[:, :, tok], aa[:, d, :, tok], ALU.mult), s_t1)
                    pool.wait_ge(s_f, 2 * p + d + 1)
                    tell(pool.tensor_tensor(g.t2, g.t2, kT[:, :, tok], ALU.mult), s_t1)
                for k in range(2):
                    pool.wait_ge(s_inv[k], 64 * (p + 1))
                for d in range(2):
                    tell(pool.memset(segs[d].XB, 0.0), s_zx)
            pool.wait_ge(s_rwdone, 1)
            pool.wait_ge(s_wo, 128)
            own(pool.memset(upper, 1.0))
            select(upper, [[1, P]], -1, -1, ALU.is_ge)
            own(pool.memset(ones, 1.0))
            own(pool.iota(iota, [[1, P]], base=0, channel_multiplier=0, allow_small_or_imprecise_dtypes=True))
            own(pool.iota(slot0, [[P, NE]], base=0, channel_multiplier=0, allow_small_or_imprecise_dtypes=True))
            tell(pool.iota(tokid, [[P, NT]], base=0, channel_multiplier=1, allow_small_or_imprecise_dtypes=True), s_tri)

            def gather_rows(r):
                if r == 0:
                    pool.wait_ge(s_h2d, 16 * NT)
                else:
                    pool.wait_ge(s_comb, NT * r)
                pool.wait_ge(s_idx, r + 1)
                for e in range(NE):
                    i = r * NE + e
                    if i >= 3:
                        wait_filled(pool, "xT", i - 3, 1)
                    pool.indirect_dma_start(out=xg[:, i % 3], out_offset=None, in_=h2_dram,
                                            in_offset=bass.IndirectOffsetOnAxis(ap=idx[:, e:e + 1], axis=0)).then_inc(s_xg[i % 3], 16)
                pool.wait_ge(s_moe, r + 1)
                pool.wait_ge(s_pos, r + 1)
                for t in range(NT):
                    n = r * NT + t
                    if t >= 2:
                        pool.wait_ge(s_comb, n - 1)
                    for j in range(2):
                        pool.indirect_dma_start(out=yg2[:, t % 2, j], out_offset=None, in_=ys_dram,
                                                in_offset=bass.IndirectOffsetOnAxis(ap=pos[:, j * NT + t:j * NT + t + 1], axis=0)).then_inc(s_yg[t % 2], 16)
            rounds(pool, gather_rows)
        @block.scalar
        def _(act):
            own, tell, out_of = steps(act, s_act)

            def A(out, in_, func=ACT.Copy, **kw):
                return act.activation(out, in_, func, **kw)

            def copy_out(dst, key, src=None, scale=1.0):
                wait_filled(act, *key)
                src = bank(key)[:, :] if src is None else src
                out_of(A(dst, src, scale=scale), *key)

            act.preload_act_table_set("natural_log_exp_and_others")
            wait_result(act, "rows")
            tell(A(stmp, vec[:, vcond:vcond + 2 * KT], ACT.Exp, scale=-1.0), s_cond)
            act.wait_ge(s_x, 16 * NT)
            act.wait_ge(s_eps, 1)
            for t in range(NT):
                own(A(kk_b[:, 0:D], x_sb[:, t], ACT.Square, accum_out=ssum[:, t:t + 1]))
            own(A(rstd, ssum, ACT.Ln, scale=1.0 / D, bias=eps6))
            tell(A(rstd, rstd, ACT.Exp, scale=-0.5), s_xn)
            act.wait_ge(s_g1, 1)
            for k in range(0, KT, 2):
                wait_filled(act, "hl", k)
                out_of(A(hT[:, k, P:T], bank(("hl", k))[:, :], ACT.Identity, scale=gscv[:, 0, k, 1:2], bias=modv[:, k, 1:2]), "hl", k)
            wait_filled(act, "hc", 0)
            for k in range(KT // 2):
                ins = A(hT[:, k, 0:P], bank(("hc", 0))[:, k * P:(k + 1) * P], ACT.Identity, scale=gscv[:, 0, k, 0:1], bias=modv[:, k, 0:1])
                if k < KT // 2 - 1:
                    own(ins)
            out_of(ins, "hc", 0)
            for n, i in (("q0", 0), ("q1", 1), ("g0", GC), ("g1", GC + 1)):
                sc = HD ** -0.5 if n[0] == "q" else 1.0
                copy_out(qk_g[:, i, P:T], ("pl", n), scale=sc)
                copy_out(qk_g[:, i, 0:P], ("pc", n), bank(("pc", n))[:, 0:P], scale=sc)
            for t in range(NT):
                copy_out(vg[:, t], ("vg", t))
            act.wait_ge(s_ogx, 1)
            sgm = cl_b[:, RC * T:2 * RC * T]
            tell(A(sgm, yg_b[:, :], ACT.Exp, scale=-1.0), s_sig)
            tell(A(sgm, sgm, ACT.Ln, bias=1.0), s_sig)
            tell(A(sgm, sgm, ACT.Exp, scale=-1.0), s_sig)
            act.wait_ge(s_lgx, 1)
            glt = cl_b[:, 0:RC * T]
            act.wait_ge(s_zd, 64)
            own(A(glt, region1[:, KT * T + 2 * GC * T:KT * T + 4 * GC * T], ACT.Abs))
            own(A(glt, glt, ACT.Exp, scale=-1.0))
            tell(A(glt, glt, ACT.Ln, bias=1.0), s_lgt)
            act.wait_ge(s_rawz, 1)
            for c_, n in enumerate(tail[:3 * RC]):
                b = c_ % 2
                if c_ >= 2:
                    act.wait_ge(s_conv, c_ - 1)
                lat = raw[:, b, 0:RAWL].rearrange("p (y x) -> p y x", x=GW + 2)
                copy_out(lat[:, 1:GH + 1, 1:GW + 1], ("pl", n), bank(("pl", n))[:, :].rearrange("p (y x) -> p y x", x=GW))
                copy_out(raw[:, b, RAWL + 1:RAWL + 1 + P], ("pc", n), bank(("pc", n))[:, 0:P])
            act.wait_ge(s_gcl, 1)
            copy_out(laT[:, P:T], ("pl", "la"))
            copy_out(laT[:, 0:P], ("pc", "la"), bank(("pc", "la"))[:, 0:P])
            for i in range(RC):
                wait_filled(act, "kl", i)
                if i == 0:
                    wait_filled(act, "kc")
                out_of(A(sq[:, i, P:T], bank(("kl", i))[:, :], ACT.Ln, bias=eps6), "kl", i)
            out_of(A(sq[:, :, 0:P], bank(("kc",))[:, :].rearrange("p (c t) -> p c t", c=RC), ACT.Ln, bias=eps6), "kc")
            tell(A(sq, sq, ACT.Exp, scale=-0.5), s_kkn)
            for t in range(NT):
                copy_out(vtok[:, t], ("vt", t))
            act.wait_ge(s_gz, 1)
            wait_filled(act, "pc", "lg")
            for d in range(2):
                for h in range(2):
                    act.dma_start(GM[h * HD:(h + 1) * HD, 1, d], state_gla[0, 0, d].rearrange("(c a) k v -> a k c v", a=2)[h]).then_inc(s_gin, 16)
            act.dma_start(gng, gla_norm_g[0].partition_broadcast(P)).then_inc(s_gin, 16)
            def sigmoid(d, j, buf):
                act.wait_ge(s_wx, 2 * d + j + 1)
                v = buf[:, d]
                own(A(v, v, ACT.Exp, scale=-1.0))
                own(A(v, v, ACT.Ln, bias=1.0))
                tell(A(v, v, ACT.Exp, scale=-1.0), s_wm)

            for p in range(NT):
                if p == 1:
                    act.wait_ge(s_gM, 2)
                    for d in range(2):
                        for h in range(2):
                            act.dma_start(new_state_gla[0, 0, d].rearrange("(c a) k v -> a k c v", a=2)[h], GM[h * HD:(h + 1) * HD, 0, d]).then_inc(s_gout, 16)
                if p == 4:
                    sigmoid(0, 0, cl)
                for d in range(2):
                    g = gws[d]
                    act.wait_ge(s_gseg, 2 * p + d + 1)
                    own(A(g.e1, g.df, ACT.Exp, scale=1.0 / 16))
                    own(A(g.e2, g.df, ACT.Exp, scale=-1.0 / 16))
                    own(A(g.em, g.m, ACT.Exp, scale=1.0 / 16))
                    tell(A(g.pc, g.m, ACT.Exp, scale=2.0 / 16), s_gexp)
                if p == 0:
                    act.wait_ge(s_lora, 1)
                    own(A(tlw, tlw, ACT.Exp, scale=2.0))
                    own(A(tlw, tlw, ACT.Ln, bias=1.0))
                    tell(A(tlw, tlw, ACT.Exp, scale=-1.0), s_lgt)
                    own(A(slg, slg, ACT.Exp, scale=-1.0))
                    own(A(slg, slg, ACT.Ln, bias=1.0))
                    tell(A(slg, slg, ACT.Exp, scale=-1.0), s_lgt)
            act.wait_ge(s_gfin, 1)
            own(A(grs20, grs20, ACT.Ln, scale=1.0 / DV, bias=eps6))
            tell(A(grs20, grs20, ACT.Exp, scale=-0.5), s_grs)
            for d in range(2):
                for j, buf in ((0, cl), (1, aa)):
                    if (d, j) != (0, 0):
                        sigmoid(d, j, buf)
            def decay_exps(p):
                for d in range(2):
                    g, t = segs[d], PAIRS[p][d]
                    act.wait_ge(s_seg, 2 * p + d + 1)
                    cs = cl[:, d, :, t * P:(t + 1) * P]
                    own(A(g.E1[:, :, 1:HD + 1].rearrange("p (h c) i -> p h c i", c=2), cs.rearrange("p h (c i) -> p h c i", c=2), ACT.Exp, scale=DECAY))
                    tell(A(g.E2, cs, ACT.Exp, scale=-DECAY), s_E)
            decay_exps(0)
            for p in range(NT):
                for d in range(2):
                    g = segs[d]
                    copy_out(g.X[:, :, 0:HD], ("tA", p, d), bank(("tA", p, d))[:, :].rearrange("p (h k) -> p h k", k=HD))
                    copy_out(g.B3[:, 2], ("tB", p, d), bank(("tB", p, d))[:, :].rearrange("p (h k) -> p h k", k=HD))
                    copy_out(g.ktok, ("tK", p, d), bank(("tK", p, d))[:, :].rearrange("p (h k) -> p h k", k=HD))
                    copy_out(g.X[:, :, HD:2 * HD], ("AV", p, d), bank(("AV", p, d))[:, :].rearrange("p (h k) -> p h k", k=HD))
                for n in ("Z1", "X5t", "Z2"):
                    for d in range(2):
                        g = segs[d]
                        to = g.D2 if n == "X5t" else g.A3[:, 0]
                        copy_out(to, (n, p, d), bank((n, p, d))[:, :].rearrange("p (h k) -> p h k", k=HD))
                for d in range(2):
                    g = segs[d]
                    for j in range(2):
                        copy_out(g.WU[:, 4 * j:4 * j + 4], ("WU", p, d, j), bank(("WU", p, d, j))[:, :].rearrange("p (h k) -> p h k", k=2 * HD))
                if p < NT - 1:
                    decay_exps(p + 1)
                for d in range(2):
                    t = PAIRS[p][d]
                    if first(p, d):
                        if p == 1:
                            act.wait_ge(s_rst, 32)
                        copy_out(yacc[:, t], ("Ya", p, d))
                if p == 0:
                    for d in range(2):
                        wait_filled(act, "st", d)
                        out_of(A(stbuf[:, d], bank(("st", d))[0:HD, :]), "st", d)
                        act.dma_start(new_state_rwkv[0, 0, d].rearrange("h v k -> v h k"),
                                      stbuf[:, d].rearrange("v (h k) -> v h k", h=NH)).then_inc(s_rst, 16)
                    wait_filled(act, "s0")
                    wait_filled(act, "st", 1)
                    out_of(A(MR[:, 0], bank(("s0",))[:, :].rearrange("p (d h v) -> p d h v", d=2, h=RC)), "s0")
            for v, nme in enumerate(("ga1", "sc2", "sh2")):
                for cnd in range(2):
                    for h in range(2):
                        copy_out(gbuf[:, v, cnd, h * 512:(h + 1) * 512], ("rowb", nme, cnd, h))
            def head_rstd(t):
                act.wait_ge(s_y, t + 1)
                own(A(rs8, rs8, ACT.Ln, scale=1.0 / HD, bias=epsln))
                tell(A(rs8, rs8, ACT.Exp, scale=-0.5), s_yr)

            def y_columns(t):
                if t >= 1:
                    wait_filled(act, "out", t - 1, 1)
                for j in range(2):
                    copy_out(yT[:, 4 * j:4 * j + 4], ("yT", t, j), bank(("yT", t, j))[:, :].rearrange("p (k t) -> p k t", k=4))

            def x1_rstd(t):
                act.wait_ge(s_x1, t + 1)
                own(A(junk, x1[:, t], ACT.Square, accum_out=ss1))
                own(A(ss1, ss1, ACT.Ln, scale=1.0 / D, bias=eps6))
                tell(A(ss1, ss1, ACT.Exp, scale=-0.5), s_x1r)

            def h2_columns(t):
                for j in range(2):
                    copy_out(h2T[:, 4 * j:4 * j + 4, t * P:(t + 1) * P], ("hT2", t, j), bank(("hT2", t, j))[:, :].rearrange("p (k t) -> p k t", k=4))
            head_rstd(0)
            y_columns(0)
            head_rstd(1)
            for t in range(NT):
                if t + 1 < NT:
                    y_columns(t + 1)
                if t >= 1:
                    h2_columns(t - 1)
                x1_rstd(t)
                if t + 2 < NT:
                    head_rstd(t + 2)
            h2_columns(NT - 1)
            act.wait_ge(s_rg, 1)
            tell(A(rt_v["ge"], rt_v["gd"], ACT.Exp), s_rex)
            act.wait_ge(s_rg, 2)
            tell(A(rt_v["E"], rt_v["E"], ACT.Exp), s_rex)
            for cnd in range(2):
                for h in range(2):
                    copy_out(ga2b[:, cnd, h * 512:(h + 1) * 512], ("rowb", "ga2", cnd, h))

            def expert_copies(r):
                def expert_rows(i):
                    if i >= 2:
                        act.wait_ge(s_ys[i % 2], 16 * (i // 2))
                    for h in range(2):
                        copy_out(yo[:, i % 2, h * 512:(h + 1) * 512], ("dn", i, h))
                    at = (i % NE) * P
                    act.dma_start(ys_dram[at:at + P, :], yo[:, i % 2]).then_inc(s_ys[i % 2], 16)

                for e in range(NE):
                    i = r * NE + e
                    if e == 0:
                        for j in range(2):
                            copy_out(xgT[:, i % 2, 4 * j:4 * j + 4], ("xT", i, j), bank(("xT", i, j))[:, :].rearrange("p (k t) -> p k t", k=4))
                    wait_filled(act, "ug", i)
                    if i >= 2:
                        wait_result(act, "ug", i - 2)
                    tell(A(sg[:, i % 2], bank(("ug", i))[:, F:2 * F], ACT.Exp, scale=-1.0), s_sg)
                    if e < NE - 1:
                        for j in range(2):
                            copy_out(xgT[:, (i + 1) % 2, 4 * j:4 * j + 4], ("xT", i + 1, j),
                                     bank(("xT", i + 1, j))[:, :].rearrange("p (k t) -> p k t", k=4))
                    if e > 0:
                        expert_rows(i - 1)
                    copy_out(aT[:, i % 2], ("aT", i), bank(("aT", i))[:, 0:FT * P].rearrange("p (f t) -> p f t", f=FT))
                expert_rows(i)
                for s in range(2):
                    act.wait_ge(s_ys[s], 8 * (i + 1))
                tell(A(small[:, 3:4], ss1), s_moe)
                for t in range(NT):
                    act.wait_ge(s_comb, r * NT + t + 1)
                    if r >= 1:
                        act.wait_ge(s_yout, (r - 1) * NT + t + 1)
                    own(A(junk, x1[:, t], ACT.Square, accum_out=rstd[:, t:t + 1]))
                    own(A(rstd[:, t:t + 1], rstd[:, t:t + 1], ACT.Ln, scale=1.0 / D, bias=eps6))
                    tell(A(rstd[:, t:t + 1], rstd[:, t:t + 1], ACT.Exp, scale=-0.5), s_finr)
            rounds(act, expert_copies)
            act.wait_ge(s_rst, 32)

        @block.vector
        def _(dve):
            own, tell, out_of = steps(dve, s_dve)
            TT, TS, STT = dve.tensor_tensor, dve.tensor_scalar, dve.scalar_tensor_tensor
            mk = mask[:, :].rearrange("p (d a i) -> p d a i", d=2, a=2)
            mD = maskD[:, :].rearrange("p (d a i) -> p d a i", d=2, a=2)
            mA = maskA[:, :].rearrange("p (d a i) -> p d a i", d=2, a=3)

            def scan_masks(m):
                own(dve.memset(m, 1.0))
                for d in range(2):
                    at = 0 if d == 0 else CH - 1
                    own(dve.memset(m[:, d].rearrange("p (n i) -> p n i", i=CH)[:, :, at:at + 1], 0.0))

            def chunk_sums(v, m, d):
                if d == 0:
                    own(dve.tensor_tensor_scan(v, m[:, 0], v, 0.0, ALU.mult, ALU.add))
                else:
                    own(dve.tensor_tensor_scan(v[:, ::-1], m[:, 1, ::-1], v[:, ::-1], 0.0, ALU.mult, ALU.add))

            own(dve.memset(eps6, EPS))
            tell(dve.memset(epsln, LN_EPS), s_eps)
            scan_masks(gmask)
            wait_filled(dve, "rows")
            out_of(dve.tensor_copy(vec[:, :], bank(("rows",))[:, 0:NV1 + NV2 + 2 * KT]), "rows")
            dve.wait_ge(s_cond, 1)
            own(TS(stmp, stmp, 1.0, None, ALU.add))
            own(dve.reciprocal(stmp, stmp))
            tell(TT(scond, stmp, vec[:, vcond:vcond + 2 * KT], ALU.mult), s_condt)
            own(TS(oneka, vec[:, vka:vka + RC], -1.0, 1.0, ALU.mult, ALU.add))

            def ada_rows_out(n):
                wait_filled(dve, "ada", n)
                if n >= 2:
                    wait_filled(dve, "adaT", n - 2)
                out_of(dve.tensor_copy(adarow(n), bank(("ada", n))[0:2, :]), "ada", n)

            def ada_turned_out(n):
                wait_filled(dve, "adaT", n)
                out_of(TT(modv[:, 4 * n:4 * n + 4, :], bank(("adaT", n))[:, 0:8].rearrange("p (b c) -> p b c", c=2),
                          bc(vec[:, vb_ada + 4 * n:vb_ada + 4 * n + 4], 2, 2), ALU.add), "adaT", n)

            def normalise_x(tiles):
                for t in tiles:
                    ins = TS(x_sb[:, t], x_sb[:, t], rstd[:, t:t + 1], None, ALU.mult)
                    own(ins) if t < NT - 1 else tell(ins, s_xnr)
            ada_rows_out(0)
            for n in range(4):
                if n < 3:
                    ada_rows_out(n + 1)
                ada_turned_out(n)
                if n == 1:
                    dve.wait_ge(s_xn, 1)
                    normalise_x(range(0, 2))
                if n == 2:
                    normalise_x(range(2, NT))
            tell(STT(gscv[:, 0], modv[:, KT:2 * KT, :], 1.0, bc(vec[:, vn1:vn1 + KT], 2, 2), ALU.add, ALU.mult), s_g1)
            for k in range(1, KT, 2):
                wait_filled(dve, "hl", k)
                out_of(TS(hT[:, k, P:T], bank(("hl", k))[:, :], gscv[:, 0, k, 1:2], modv[:, k, 1:2], ALU.mult, ALU.add), "hl", k)
            wait_filled(dve, "hc", 1)
            for j in range(KT // 2):
                k = KT // 2 + j
                ins = TS(hT[:, k, 0:P], bank(("hc", 1))[:, j * P:(j + 1) * P], gscv[:, 0, k, 0:1], modv[:, k, 0:1], ALU.mult, ALU.add)
                if j < KT // 2 - 1:
                    own(ins)
            out_of(ins, "hc", 1)
            for t in range(NT):
                wait_filled(dve, "og", t)
                out_of(TS(yg[:, t], bank(("og", t))[:, :], -40.0, None, ALU.max), "og", t)
            tell(dve.memset(small[:, 2:3], 1.0), s_ogx)
            dve.wait_ge(s_xn, 1)
            for key, sl, n in ((("lgkl",), slice(P, T), LAT), (("lgkc",), slice(0, P), P)):
                wait_filled(dve, *key)
                own(dve.tensor_copy(lgkT[0:GKL, sl], bank(key)[0:GKL, 0:n]))
                out_of(dve.tensor_copy(lgkT[32:32 + GKL, sl], bank(key)[32:32 + GKL, 0:n]), *key)
            for d in range(2):
                for i in range(GC):
                    wait_filled(dve, "gkl", d, i)
                    out_of(TS(gcl[:, d, i, P:T], bank(("gkl", d, i))[:, :], vec[:, vgb + d * GC + i:vgb + d * GC + i + 1], None, ALU.add), "gkl", d, i)
            wait_filled(dve, "gkc")
            for d in range(2):
                for i in range(GC):
                    j = d * GC + i
                    ins = TS(gcl[:, d, i, 0:P], bank(("gkc",))[:, j * P:(j + 1) * P], vec[:, vgb + j:vgb + j + 1], None, ALU.add)
                    if j < 2 * GC - 1:
                        own(ins)
            out_of(ins, "gkc")
            tell(dve.memset(small[:, 2:3], 1.0), s_lgx)
            dve.wait_ge(s_lgt, 1)
            g_all = region1[:, KT * T + 2 * GC * T:KT * T + 4 * GC * T]
            own(STT(g_all, g_all, 0.0, cl_b[:, 0:RC * T], ALU.min, ALU.subtract))
            for d in range(2):
                for i in range(GC):
                    chunk_sums(gcl[:, d, i], gmask, d)
            tell(dve.memset(small[:, 2:3], 1.0), s_gcl)

            for c_, n in enumerate(tail[:3 * RC]):
                b = c_ % 2
                dst = {"r": rT, "k": kT, "v": vT}[n[0]][:, c_ % RC]
                wait_result(dve, "pl", n)
                wait_result(dve, "pc", n)
                lat = raw[:, b, 0:RAWL].rearrange("p (y x) -> p y x", x=GW + 2)
                out = dst[:, P:T].rearrange("p (y x) -> p y x", x=GW)

                def tap(i, j):
                    q = vcv + (3 * i + j) * 3 * RC + c_
                    return vec[:, q:q + 1]
                own(TS(out, lat[:, 0:GH, 0:GW], tap(0, 0), None, ALU.mult))
                own(TS(dst[:, 0:P], raw[:, b, RAWL:RAWL + P], tap(1, 0), None, ALU.mult))
                for m in range(1, 9):
                    i, j = m // 3, m % 3
                    own(STT(out, lat[:, i:i + GH, j:j + GW], tap(i, j), out, ALU.mult, ALU.add))
                own(STT(dst[:, 0:P], raw[:, b, RAWL + 1:RAWL + 1 + P], tap(1, 1), dst[:, 0:P], ALU.mult, ALU.add))
                tell(STT(dst[:, 0:P], raw[:, b, RAWL + 2:RAWL + 2 + P], tap(1, 2), dst[:, 0:P], ALU.mult, ALU.add), s_conv)
                if n == f"k{RC - 1}":
                    for i in range(RC):
                        tell(TS(kkT[:, i], kT[:, i], vec[:, vkk + i:vkk + i + 1], None, ALU.mult), s_kk)
                    for i in range(RC):
                        tell(STT(prod[:, i], rT[:, i], vec[:, vrk + i:vrk + i + 1], kT[:, i], ALU.mult, ALU.mult), s_bon)
            wait_filled(dve, "pl", "lw")
            out_of(TS(tlw[:, P:T], bank(("pl", "lw"))[:, :], 20.0, None, ALU.min), "pl", "lw")
            wait_filled(dve, "pc", "lw")
            out_of(TS(tlw[:, 0:P], bank(("pc", "lw"))[:, 0:P], 20.0, None, ALU.min), "pc", "lw")
            wait_filled(dve, "pl", "lg")
            out_of(TS(slg[:, P:T], bank(("pl", "lg"))[:, :], -40.0, None, ALU.max), "pl", "lg")
            wait_filled(dve, "pc", "lg")
            out_of(TS(slg[:, 0:P], bank(("pc", "lg"))[:, 0:P], -40.0, None, ALU.max), "pc", "lg")
            tell(dve.memset(small[:, 2:3], 1.0), s_lora)
            wait_filled(dve, "bonus")
            out_of(dve.tensor_copy(bonus[:, :], bank(("bonus",))[:, 0:NT * NH]), "bonus")
            dve.wait_ge(s_kkn, 1)
            own(STT(kkT, kkT, -1.0, sq, ALU.mult, ALU.mult))

            wait_filled(dve, "pc", "lg")
            tell(dve.memset(GM[:, 0], 0.0), s_gz)
            dve.wait_ge(s_sig, 4)
            wait_filled(dve, "vt", NT - 1)

            def centred_exponents(p):
                for d in range(2):
                    g, t = gws[d], PAIRS[p][d]
                    cs = gcl[:, d, :, t * P:(t + 1) * P].rearrange("p c (j i) -> p c j i", j=2)
                    at = CH - 1 if d == 0 else 0
                    own(TS(g.m, cs[:, :, :, at], 0.5, None, ALU.mult))
                    own(TT(g.df.rearrange("p (c j i) -> p c j i", c=GC, j=2), cs, bc(g.m, 3, CH), ALU.subtract))
                    tell(TS(g.df, g.df, -16.0 * CLAMP, 16.0 * CLAMP, ALU.max, ALU.min), s_gseg)
            def low_rank(key, d):
                buf, off = (cl, vw0) if key == "w" else (aa, va0)
                for i in range(RC):
                    wait_filled(dve, key + "l", d, i)
                    q = off + d * RC + i
                    out_of(TS(buf[:, d, i, P:T], bank((key + "l", d, i))[:, :], vec[:, q:q + 1], -40.0, ALU.add, ALU.max), key + "l", d, i)
                wait_filled(dve, key + "c", d)
                for i in range(RC):
                    q = off + d * RC + i
                    ins = TS(buf[:, d, i, 0:P], bank((key + "c", d))[:, i * P:(i + 1) * P], vec[:, q:q + 1], -40.0, ALU.add, ALU.max)
                    if i < RC - 1:
                        own(ins)
                out_of(ins, key + "c", d)
                tell(dve.memset(small[:, 2:3], 1.0), s_wx)

            centred_exponents(0)
            for p in range(NT):
                for d in range(2):
                    g, t = gws[d], PAIRS[p][d]
                    b = bank(("g1", p, d))
                    wait_filled(dve, "g1", p, d)
                    own(TT(g.sT, b[:, 0:4 * HD].rearrange("p (h i) -> p h i", h=GH_N), bc(mk[:, d, 1], 1, GH_N), ALU.mult))
                    out_of(dve.tensor_copy(g.ktok, b[:, 4 * HD:8 * HD].rearrange("p (h i) -> p h i", h=GH_N)), "g1", p, d)
                for d in range(2):
                    g, t = gws[d], PAIRS[p][d]
                    wait_filled(dve, "goA", p, d)
                    if first(p, d):
                        out_of(dve.tensor_copy(goacc[:, t], bank(("goA", p, d))[:, :]), "goA", p, d)
                    else:
                        out_of(TT(goacc[:, t], bank(("goA", p, d))[:, :], goacc[:, t], ALU.add), "goA", p, d)
                    wait_filled(dve, "gkv", p, d)
                    dve.wait_ge(s_gexp, 2 * p + d + 1)
                    out_of(TT(g.kv, bank(("gkv", p, d))[:, :].rearrange("p (c j v) -> p c j v", c=GC, j=2), bc(g.em, 3, DV), ALU.mult), "gkv", p, d)
                    st = 0 if p == 0 else 1
                    if p == 1:
                        dve.wait_ge(s_gin, 16 * 5)
                    M0, c0, c1 = GM[:, st, d], chunk(d, 0), chunk(d, 1)
                    own(TT(GM[:, 3, d], M0, bc(g.em[:, :, c0], 2, DV), ALU.mult))
                    own(TT(GM[:, 5, d], M0, bc(g.pc[:, :, c0], 2, DV), ALU.mult))
                    own(TT(GM[:, 2, d], GM[:, 5, d], g.kv[:, :, c0], ALU.add))
                    own(TT(GM[:, 4, d], GM[:, 2, d], bc(g.em[:, :, c1], 2, DV), ALU.mult))
                    own(TT(GM[:, 6, d], GM[:, 2, d], bc(g.pc[:, :, c1], 2, DV), ALU.mult))
                    tell(TT(M0, GM[:, 6, d], g.kv[:, :, c1], ALU.add), s_gM)
                if p < NT - 1:
                    centred_exponents(p + 1)
                    ada_rows_out(4 + p)
                for d in range(2):
                    t = PAIRS[p][d]
                    wait_filled(dve, "goB", p, d)
                    out_of(TT(goacc[:, t], bank(("goB", p, d))[:, :], goacc[:, t], ALU.add), "goB", p, d)
                if p < NT - 1:
                    ada_turned_out(4 + p)
                if p == 2:
                    low_rank("w", 0)
                if p == 0:
                    dve.wait_ge(s_lgt, 2)
                    tell(TS(tlw, tlw, -2.0, 1.0, ALU.mult, ALU.add), s_lora)
            go4 = goacc.rearrange("p t (h v) -> p (t h) v", v=DV)
            gsq = region3[:, 0:NT * RW].rearrange("p (n v) -> p n v", v=DV)
            own(TT(gsq, go4, go4, ALU.mult))
            tell(dve.tensor_reduce(out=grs20, in_=gsq, axis=AXX, op=ALU.add), s_gfin)
            dve.wait_ge(s_grs, 1)
            own(TT(go4, go4, bc(grs20, 2, DV), ALU.mult))
            own(TT(go4, go4, bc(gng, 1, NT * GH_N), ALU.mult))
            tell(TT(yg_b[:, :], yg_b[:, :], cl_b[:, RC * T:2 * RC * T], ALU.mult), s_gdone)

            scan_masks(smask)
            low_rank("a", 0)
            low_rank("w", 1)
            low_rank("a", 1)
            rest = list(range(4 + NT - 1, 2 * NMOD))
            ada_rows_out(rest[0])
            for d in range(2):
                ada_rows_out(rest[d + 1])
                ada_turned_out(rest[d])
                dve.wait_ge(s_wm, 2 * d + 1)
                for i in range(RC):
                    chunk_sums(cl[:, d, i], smask, d)
                dve.wait_ge(s_wm, 2 * d + 2)
            ada_rows_out(rest[3])
            ada_turned_out(rest[2])
            ada_turned_out(rest[3])
            tell(STT(gscv[:, 1], modv[:, 4 * KT:5 * KT, :], 1.0, bc(vec[:, vn2:vn2 + KT], 2, 2), ALU.add, ALU.mult), s_g2)
            tell(dve.memset(MR[:, 0], 0.0), s_mst)

            dve.wait_ge(s_gout, 64)
            c4 = lambda v: v.rearrange("p h (c i) -> p h c i", c=2)

            def decayed_ra(p):
                for d in range(2):
                    g = segs[d]
                    own(dve.memset(g.E1[:, :, 0:1], 1.0))
                    tell(dve.memset(g.E1[:, :, HD + 1:HD + 2], 1.0), s_seg)
                for d in range(2):
                    g, t = segs[d], PAIRS[p][d]
                    tok = slice(t * P, (t + 1) * P)
                    e4 = lambda a, b: g.E1[:, :, a:b].rearrange("p (h c) i -> p h c i", c=2)
                    for h in range(RC):
                        ins = TS(g.t2[:, h], aa[:, d, h, tok], vec[:, vka + h:vka + h + 1], oneka[:, h:h + 1], ALU.mult, ALU.add)
                        own(ins) if h < RC - 1 else tell(ins, s_f)
                    dve.wait_ge(s_E, 2 * p + d + 1)
                    own(TT(g.AR[:, :, :, 1, :], c4(rT[:, :, tok]), e4(1, HD + 1), ALU.mult))
                    sh = (0, HD) if d == 0 else (2, HD + 2)
                    own(TT(g.AR[:, :, :, 0, :], c4(kkT[:, :, tok]), e4(*sh), ALU.mult))
                    at = HD if d == 0 else 1
                    own(dve.tensor_copy(pcs[:, d], g.E1[:, :, at].rearrange("p (h c) -> p h c", c=2)))

            def decayed_bk(p, d):
                g = segs[d]
                dve.wait_ge(s_t1, 2 * (2 * p + d) + 2)
                own(STT(g.b, g.t1, -1.0, g.E2, ALU.mult, ALU.mult))
                tell(TT(g.k, g.t2, g.E2, ALU.mult), s_ops)
            decayed_ra(0)
            decayed_bk(0, 0)
            decayed_bk(0, 1)
            for p in range(NT):
                cur, nxt = MCUR[p], 1 - MCUR[p]
                for d in range(2):
                    g = segs[d]
                    for n in ("b0", "A", "b1", "k0", "k1"):
                        key = (n, p, d)
                        wait_filled(dve, *key)
                        if n == "A":
                            v = bank(key)[:, :].rearrange("p (h i) -> p h i", h=NH)
                            for a in range(d, 3):
                                ins = TT(g.A3[:, a], v, bc(mA[:, d, a], 1, NH), ALU.mult)
                                if a < 2:
                                    own(ins)
                            out_of(ins, *key)
                            continue
                        hp = int(n[1])
                        dst, m = (g.B3[:, 0:2], mD) if n[0] == "b" else (g.K2, mk)
                        out_of(TT(dst[:, :, hp::2].rearrange("p a h i -> p h a i"), bank(key)[:, :].rearrange("p (h a i) -> p h a i", a=2, i=HD),
                                  bc(m[:, d], 1, RC), ALU.mult), *key)

                L3, X3, T3 = (v.rearrange("p (i j) -> p i j", i=16) for v in (BL, BX, BT))
                if p >= 1:
                    for k in range(2):
                        dve.wait_ge(s_back[k], 32 * p)
                own(dve.memset(BX, 0.0))
                own(dve.memset(BX[:, 0:256:17], 1.0))
                dve.wait_ge(s_L, 32 * (p + 1))
                def two(v, row, col, r, w):
                    a = v[:, 16 * row + col:16 * row + col + 1]
                    return bass.AP(tensor=a.tensor, offset=a.offset, ap=[a.ap[0], [8 * 16 + 8, 2], [16, r], [1, w]])
                for m in range(7):
                    r, w = 7 - m, m + 1
                    t_ = BT[:, 0:2 * r * w].rearrange("p (b i j) -> p b i j", b=2, i=r)
                    own(TT(t_, two(BL, m + 1, m, r, 1).broadcast_to([P, 2, r, w]), two(BX, m, 0, 1, w).broadcast_to([P, 2, r, w]), ALU.mult))
                    own(TT(two(BX, m + 1, 0, r, w), two(BX, m + 1, 0, r, w), t_, ALU.add))
                t4 = BXW.rearrange("p (i j m) -> p i j m", i=8, j=8)
                T21 = BT[:, 0:64].rearrange("p (i j) -> p i j", i=8)
                own(TT(t4, bc(L3[:, 8:16, 0:8], 2, 8), bc(X3[:, 0:8, 0:8].rearrange("p m j -> p j m"), 1, 8), ALU.mult))
                own(dve.tensor_reduce(out=T21, in_=t4, axis=AXX, op=ALU.add))
                own(TT(t4, bc(X3[:, 8:16, 8:16], 2, 8), bc(T21.rearrange("p m j -> p j m"), 1, 8), ALU.mult))
                own(dve.tensor_reduce(out=X3[:, 8:16, 0:8], in_=t4, axis=AXX, op=ALU.add))
                tell(dve.tensor_copy(BXt.rearrange("p (i j) -> p i j", i=16), X3.rearrange("p i j -> p j i")), s_sub)
                for n in ("X5", "X6"):
                    for d in range(2):
                        g = segs[d]
                        src, dst = g.X1, g.X0
                        wait_filled(dve, n, p, d)
                        if n == "X6":
                            dve.wait_ge(s_zx, 2 * p + d + 1)
                            v = bank((n, p, d))[:, :].rearrange("p (h i) -> p h i", h=NH)
                            own(TT(g.XB[0:HD, :, 0:HD], v[0:HD], g.X0[0:HD], ALU.add))
                            out_of(TT(g.XB[HD:P, :, HD:P], v[HD:P], g.X0[HD:P], ALU.add), n, p, d)
                            continue
                        out_of(TT(dst, bank((n, p, d))[:, :].rearrange("p (h i) -> p h i", h=NH), src, ALU.add), n, p, d)
                for d in range(2):
                    g = segs[d]
                    for cp in range(2):
                        v = bank(("G", p, d, cp))[:, :].rearrange("p (h a i) -> p h a i", a=2, i=HD)
                        wait_filled(dve, "G", p, d, cp)
                        own(TT(g.QT[:, :, cp], v[:, :, 0], g.AR[:, :, cp, 1], ALU.add))
                        out_of(TT(g.GT[:, :, cp], v[:, :, 1], bc(identh[:, :], 1, RC), ALU.add), "G", p, d, cp)
                    for cp in range(2):
                        wait_filled(dve, "H", p, d, cp)
                        out_of(TT(g.H[:, cp], bank(("H", p, d, cp))[:, 0:RC * HD].rearrange("p (h i) -> p h i", h=RC),
                                  bc(pcs[:, d, :, cp], 2, HD), ALU.mult), "H", p, d, cp)
                for k in range(2):
                    for d in range(2):
                        g, cp = segs[d], chunk(d, k)
                        dst = MM[:, d] if k == 0 else MR[:, nxt, d]
                        wait_filled(dve, "seq", p, d, k)
                        out_of(TT(g.tmp, bank(("seq", p, d, k))[:, 0:RC * HD].rearrange("p (h i) -> p h i", h=RC),
                                  bc(pcs[:, d, :, cp], 2, HD), ALU.mult), "seq", p, d, k)
                        tell(TT(dst, g.tmp, g.H[:, cp], ALU.add), s_mst)
                if p < NT - 1:
                    decayed_ra(p + 1)
                for d in range(2):
                    t = PAIRS[p][d]
                    for n in ("Ya", "Yb"):
                        if n == "Ya" and first(p, d):
                            wait_result(dve, "Ya", p, d)
                            continue
                        wait_filled(dve, n, p, d)
                        out_of(TT(yacc[:, t], bank((n, p, d))[:, :], yacc[:, t], ALU.add), n, p, d)
                    if p < NT - 1:
                        decayed_bk(p + 1, d)
            tell(dve.memset(small[:, 2:3], 1.0), s_rwdone)

            mu8 = small[:, 104:112]
            s3 = sqj.rearrange("p (h i) -> p h i", h=NH)

            def head_norm(t):
                y3 = yacc[:, t].rearrange("p (h i) -> p h i", h=NH)
                own(dve.tensor_reduce(out=mu8, in_=y3, axis=AXX, op=ALU.add))
                own(TS(mu8, mu8, 1.0 / HD, None, ALU.mult))
                own(TT(y3, y3, bc(mu8, 2, HD), ALU.subtract))
                own(TT(s3, y3, y3, ALU.mult))
                tell(dve.tensor_reduce(out=rs8, in_=s3, axis=AXX, op=ALU.add), s_y)
                dve.wait_ge(s_yr, t + 1)
                own(TT(y3, y3, bc(rs8, 2, HD), ALU.mult))
                if t == 0:
                    dve.wait_ge(s_wo, 128)
                own(TT(yacc[:, t], yacc[:, t], lnw, ALU.mult))
                own(TT(yacc[:, t], yacc[:, t], lnb, ALU.add))
                own(TT(s3, vtok[:, t].rearrange("p (h i) -> p h i", h=NH), bc(bonus[:, t * NH:(t + 1) * NH], 2, HD), ALU.mult))
                own(TT(yacc[:, t], yacc[:, t], sqj, ALU.add))
                wait_filled(dve, "gate", t)
                if t >= 1:
                    wait_filled(dve, "yT", t - 1, 0)
                out_of(TT(ya, yacc[:, t], bank(("gate", t))[:, :], ALU.mult), "gate", t)

            def residual(t):
                cnd = 0 if t == 0 else 1
                for h in range(2):
                    wait_filled(dve, "out", t, h)
                    if h == 0:
                        wait_result(dve, "rowb", "ga1", 1, 1)
                    out_of(TT(x1[:, t, h * 512:(h + 1) * 512], bank(("out", t, h))[:, :], gbuf[:, 0, cnd, h * 512:(h + 1) * 512], ALU.mult), "out", t, h)
                dve.wait_ge(s_xt, 16 * (t + 1))
                tell(TT(x1[:, t], x1[:, t], xt, ALU.add), s_x1)
                dve.wait_ge(s_x1r, t + 1)
                wait_result(dve, "rowb", "sh2", 1, 1)
                if t >= 1:
                    wait_filled(dve, "hT2", t - 1, 1)
                    dve.wait_ge(s_h2d, 16 * t)
                own(STT(h2, x1[:, t], ss1, gbuf[:, 1, cnd], ALU.mult, ALU.mult))
                tell(TT(h2, h2, gbuf[:, 2, cnd], ALU.add), s_h2)

            def router_logits(t):
                wait_filled(dve, "router", t)
                out_of(TT(lgt[:, t], bank(("router", t))[:, 0:NR], br, ALU.add), "router", t)
            head_norm(0)
            head_norm(1)
            for t in range(NT):
                residual(t)
                if t >= 1:
                    router_logits(t - 1)
                if t + 2 < NT:
                    head_norm(t + 2)
            router_logits(NT - 1)

            gl = lgt[:, :, 0:NG]
            el = lgt[:, :, NG:NR].rearrange("p t (g e) -> p t g e", g=NG)
            R = rt_v
            for j in range(NG):
                own(dve.memset(R["pref"][:, j:j + 1], float(NG - j)))

            def first_max(hot, val, mx):
                own(dve.tensor_reduce(out=mx, in_=val, axis=AXX, op=ALU.max))
                own(TT(hot, val, bc(mx, 2, NG), ALU.is_equal))
                own(TT(hot, hot, bc(R["pref"], 1, NT), ALU.mult))
                own(dve.tensor_reduce(out=R["m"], in_=hot, axis=AXX, op=ALU.max))
                own(TT(hot, hot, bc(R["m"], 2, NG), ALU.is_equal))
            first_max(R["hg"], gl, R["mg"])
            tell(TT(R["gd"], gl, bc(R["mg"], 2, NG), ALU.subtract), s_rg)
            own(TT(R["sel"], el.rearrange("p t g e -> p t e g"), bc(R["hg"], 2, EPG), ALU.mult))
            own(dve.tensor_reduce(out=R["es"], in_=R["sel"], axis=AXX, op=ALU.add))
            first_max(R["h1"], R["es"], R["m1"])
            own(STT(R["es"], R["h1"], -1e30, R["es"], ALU.mult, ALU.add))
            first_max(R["h2"], R["es"], R["m2"])
            tell(TT(R["E"], R["m2"], R["m1"], ALU.subtract), s_rg)
            dve.wait_ge(s_tri, 1)
            for o_, h_ in (("o1", "h1"), ("o2", "h2")):
                v = R[o_].rearrange("p t (g e) -> p t g e", g=NG)
                for g_ in range(NG):
                    own(TT(v[:, :, g_], R[h_], bc(R["hg"][:, :, g_], 2, EPG), ALU.mult))
            tell(TT(picked_v, R["o1"], R["o2"], ALU.add), s_pick)
            dve.wait_ge(s_rex, 1)
            own(dve.tensor_reduce(out=R["m"], in_=R["ge"], axis=AXX, op=ALU.add))
            dve.wait_ge(s_rex, 2)
            own(TS(R["w1"], R["E"], 1.0, None, ALU.add))
            own(TT(R["w1"], R["w1"], R["m"], ALU.mult))
            own(dve.reciprocal(R["w1"], R["w1"]))
            own(TT(R["w2"], R["w1"], R["E"], ALU.mult))
            for j, o_ in enumerate(("o1", "o2")):
                js = slice(j * NT, (j + 1) * NT)
                own(TT(rtmp, R[o_], bc(slot0, 1, NT), ALU.mult))
                own(dve.tensor_reduce(out=R["ps"][:, js], in_=rtmp, axis=AXX, op=ALU.add))
                own(dve.tensor_copy(R["wt"][:, js], R["w1" if j == 0 else "w2"]))
                own(TT((first_ids if j == 0 else second_ids), R[o_], bc(tokid, 2, NE), ALU.mult))
            wait_filled(dve, "rank")
            own(dve.tensor_reduce(out=R["mc"], in_=bank(("rank",))[:, NT * NE:(NT + 1) * NE], axis=AXX, op=ALU.max))
            tell(dve.tensor_copy(most[0:1, 0:1], R["mc"][0:1, :]), s_most)
            rank = bank(("rank",))[:, 0:NT * NE].rearrange("p (t n) -> p t n", t=NT)
            for j, o_ in enumerate(("o1", "o2")):
                js = slice(j * NT, (j + 1) * NT)
                ins = TT(rtmp, rank, R[o_], ALU.mult)
                own(ins) if j == 0 else out_of(ins, "rank")
                own(dve.tensor_reduce(out=R["rk"][:, js], in_=rtmp, axis=AXX, op=ALU.add))

            def final_rows(r, t):
                dve.wait_ge(s_finr, r * NT + t + 1)
                if r >= 1:
                    dve.wait_ge(s_ydma, 16 * r * NT)
                tell(STT(acc[:, t], x1[:, t], rstd[:, t:t + 1], fg, ALU.mult, ALU.mult), s_yout)

            def expert_gates(r):
                if r >= 1:
                    for s in range(3):
                        dve.wait_ge(s_xg[s], 16 * len(range(s, r * NE, 3)))
                for j in range(2):
                    for t in range(NT):
                        ins = TS(onehot[:, j, t], iota, float(r * P), R["rk"][:, j * NT + t:j * NT + t + 1], ALU.add, ALU.is_equal)
                        own(ins) if (j, t) != (1, NT - 1) else tell(ins, s_oh)
                wait_filled(dve, "ids", r)
                out_of(dve.tensor_copy(idx[:, :], bank(("ids", r))[:, 0:NE]), "ids", r)
                tell(dve.memset(small[:, 2:3], 1.0), s_idx)
                if r == 0:
                    own(TT(R["ps"], R["ps"], R["rk"], ALU.add))
                own(TS(R["in"], R["rk"], float(r * P), None, ALU.is_ge))
                own(TS(R["ib"], R["rk"], float((r + 1) * P), None, ALU.is_lt))
                own(TT(R["in"], R["in"], R["ib"], ALU.mult))
                own(STT(R["ib"], R["ps"], float(-r * P), R["in"], ALU.add, ALU.mult))
                own(TT(R["wr"], R["wt"], R["in"], ALU.mult))
                tell(dve.tensor_copy(pos[:, :], R["ib"]), s_pos)
                for e in range(NE):
                    i = r * NE + e
                    s = i % 2
                    v = bank(("ug", i))
                    dve.wait_ge(s_sg, i + 1)
                    own(TS(sg[:, s], sg[:, s], 1.0, None, ALU.add))
                    own(dve.reciprocal(sg[:, s], sg[:, s]))
                    own(TT(sg[:, s], sg[:, s], v[:, F:2 * F], ALU.mult))
                    if i >= 2:
                        wait_filled(dve, "aT", i - 2)
                    out_of(TT(ac[:, s], v[:, 0:F], sg[:, s], ALU.mult), "ug", i)
                for t in range(NT):
                    cnd = 0 if t == 0 else 1
                    g0, g1 = yg2[:, t % 2, 0], yg2[:, t % 2, 1]
                    uses = r * len(range(t % 2, NT, 2)) + t // 2 + 1
                    dve.wait_ge(s_yg[t % 2], 32 * uses)
                    own(TS(g0, g0, R["wr"][:, t:t + 1], None, ALU.mult))
                    own(STT(g0, g1, R["wr"][:, NT + t:NT + t + 1], g0, ALU.mult, ALU.add))
                    own(TT(g0, g0, ga2b[:, cnd], ALU.mult))
                    tell(TT(x1[:, t], x1[:, t], g0, ALU.add), s_comb)
                    if t >= 1:
                        final_rows(r, t - 1)
                final_rows(r, NT - 1)
            rounds(dve, expert_gates)

        @block.tensor
        def _(pe):
            def mm(out, lhsT, rhs, start=True, stop=True):
                return pe.matmul(out, lhsT, rhs, start=start, stop=stop)

            def tr(out, in_):
                n = in_.shape[0]
                return pe.transpose(out, in_, ident[0:n, 0:n])

            def open_bank(*key):
                n = J[key]
                assert n == done[0], (key, n, done[0])
                done[0] += 1
                if n >= NB:
                    pe.wait_ge(drained[n % NB], n // NB)
                return PS[n % NB]

            def open_early(*key):
                n = J[key]
                if n >= NB:
                    pe.wait_ge(drained[n % NB], n // NB)
                return PS[n % NB]

            done, turns = [0], [0]

            def finish(ins):
                ins.then_inc(filled, 1)

            def half_done(ins):
                turns[0] += 1
                ins.then_inc(s_turn, 1)
                return turns[0]

            def slab(what):
                i = slabs.index(what)
                pe.wait_ge(slab_in[i % RING], 16 * (i // RING + 1))
                return ring[:, i % RING]

            pe.wait_ge(s_ident, 1)
            pe.wait_ge(s_small, 16 * 16)
            b = open_bank("rows")
            tr(b[:, 0:NV1], region1[0:NV1, 0:P])
            tr(b[:, NV1:NV1 + NV2], region1[0:NV2, P:2 * P])
            finish(tr(b[:, vcond:vcond + 2 * KT], region1[0:2 * KT, 2 * P:3 * P]))

            def ada_rows(n):
                w = slab(("ada", n))
                b = open_bank("ada", n)
                for k in range(KT):
                    ins = mm(b[0:2, :], condt[:, :, k], w[:, k, :], start=k == 0, stop=k == KT - 1)
                finish(ins)

            def ada_turn(n):
                wait_result(pe, "ada", n)
                b = open_bank("adaT", n)
                for j in range(4):
                    ins = tr(b[:, 2 * j:2 * j + 2], adarow(n)[:, j * P:(j + 1) * P])
                finish(ins)

            pe.wait_ge(s_condt, 1)
            def ada_group(first_, end):
                ada_rows(first_)
                for n in range(first_, end):
                    if n + 1 < end:
                        ada_rows(n + 1)
                    ada_turn(n)
            ada_group(0, 4)
            pe.wait_ge(s_const, 1)
            pe.wait_ge(s_xnr, 1)
            for k in range(KT):
                b = open_bank("hl", k)
                for t in range(1, NT):
                    ins = tr(b[:, (t - 1) * P:t * P], x_sb[:, t, k * P:(k + 1) * P])
                finish(ins)
            for j in range(2):
                b = open_bank("hc", j)
                for k in range(4):
                    ins = tr(b[:, k * P:(k + 1) * P], x_sb[:, 0, (4 * j + k) * P:(4 * j + k + 1) * P])
                finish(ins)
            for k in range(KT):
                wait_result(pe, "hl", k)
            wait_result(pe, "hc", 0)
            wait_result(pe, "hc", 1)

            def project(name, w, at, width=P):
                for kind, sl in (("pl", slice(P, T)), ("pc", slice(0, P))):
                    b = open_bank(kind, name)
                    n = sl.stop - sl.start
                    for k in range(KT):
                        ins = mm(b[0:width, 0:n], w[:, k, at:at + width], hT[:, k, sl], start=k == 0, stop=k == KT - 1)
                    finish(ins)

            w = slab("qk")
            for i, n in enumerate(chan):
                project(n, w, i * P)
            for what in ("vg", "og"):
                w = slab(what)
                for t in range(NT):
                    b = open_bank(what, t)
                    for k in range(KT):
                        ins = mm(b[:, :], hT[:, k, t * P:(t + 1) * P], w[:, k, :], start=k == 0, stop=k == KT - 1)
                    finish(ins)
            w = slab("lgk")
            for key, sl in (("lgkl", slice(P, T)), ("lgkc", slice(0, P))):
                b = open_bank(key)
                n = sl.stop - sl.start
                for d in range(2):
                    for k in range(KT):
                        ins = mm(b[32 * d:32 * d + GKL, 0:n], w[:, k, d * GKL:(d + 1) * GKL], hT[:, k, sl], start=k == 0, stop=k == KT - 1)
                finish(ins)
            wait_result(pe, "lgkl")
            wait_result(pe, "lgkc")
            for d in range(2):
                for i in range(GC):
                    finish(mm(open_bank("gkl", d, i)[:, :], gk2_sb[32 * d:32 * d + GKL, i * P:(i + 1) * P], lgkT[32 * d:32 * d + GKL, P:T]))
            b = open_bank("gkc")
            for d in range(2):
                if d == 1:
                    pe.wait_ge(s_turn, half_done(ins))
                for i in range(GC):
                    j = d * GC + i
                    ins = mm(b[:, j * P:(j + 1) * P], gk2_sb[32 * d:32 * d + GKL, i * P:(i + 1) * P], lgkT[32 * d:32 * d + GKL, 0:P])
            finish(ins)
            for what in ("r", "k", "v"):
                w = slab(what)
                for i in range(RC):
                    project(f"{what}{i}", w, i * P)
            w = slab("lora")
            for i, n in enumerate(("lw", "la", "lg")):
                project(n, w, i * P)
            for i in range(RC):
                pe.wait_ge(s_prod, i + 1)
                finish(mm(open_bank("kl", i)[:, :], blk[:, :], sq[:, i, P:T]))
            b = open_bank("kc")
            for i in range(RC):
                ins = mm(b[:, i * P:(i + 1) * P], blk[:, :], sq[:, i, 0:P])
            finish(ins)
            pe.wait_ge(s_bon, RC)
            b = open_bank("bonus")
            for t in range(NT):
                for i in range(RC):
                    ins = mm(b[:, t * NH + 2 * i:t * NH + 2 * i + 2], prod[:, i, t * P:(t + 1) * P], blk[:, 0:P:HD])
            finish(ins)
            pe.wait_ge(s_conv, 3 * RC)
            for t in range(NT):
                b = open_bank("vt", t)
                for i in range(RC):
                    ins = tr(b[:, i * P:(i + 1) * P], vT[:, i, t * P:(t + 1) * P])
                finish(ins)

            def low_rank(key, d):
                wt, src = (w2_sb, tlw) if key == "w" else (a2_sb, laT)
                for i in range(RC):
                    finish(mm(open_bank(key + "l", d, i)[:, :], wt[half(d), i * P:(i + 1) * P], src[half(d), P:T]))
                b = open_bank(key + "c", d)
                for i in range(RC):
                    ins = mm(b[:, i * P:(i + 1) * P], wt[half(d), i * P:(i + 1) * P], src[half(d), 0:P])
                finish(ins)

            pe.wait_ge(s_gcl, 1)
            for t in range(NT):
                wait_result(pe, "vg", t)
            half = lambda x: slice(HD * x, HD * x + HD)
            for p in range(NT):
                for d in range(2):
                    g = gws[d]
                    pe.wait_ge(s_gq, 2 * p + d + 1)
                    b = open_bank("g1", p, d)
                    for hp in range(2):
                        for c_ in range(GC):
                            for cp in range(2):
                                h = 2 * c_ + hp
                                ins = mm(b[half(cp), h * HD:(h + 1) * HD], g.k[half(hp), c_, half(cp)], g.q[half(hp), c_, half(cp)])
                        if hp == 0:
                            turn = half_done(ins)
                            for c_ in range(GC):
                                tr(b[:, 4 * HD + c_ * P:4 * HD + (c_ + 1) * P], g.k[:, c_])
                            pe.wait_ge(s_turn, turn)
                    finish(ins)
                for d in range(2):
                    g, t = gws[d], PAIRS[p][d]
                    wait_result(pe, "g1", p, d)
                    bA = open_early("goA", p, d)
                    bK = open_early("gkv", p, d)
                    for cp in range(2):
                        for h in range(GH_N):
                            col = (h // 2 * 2 + cp) * DV
                            ins = mm(bK[half(h % 2), col:col + DV], g.ktok[half(cp), h], vg[half(cp), t, h * DV:(h + 1) * DV])
                        if cp == 0:
                            turn = half_done(ins)
                            open_bank("goA", p, d)
                            for h in range(GH_N):
                                for c_ in range(2):
                                    insA = mm(bA[half(c_), h * DV:(h + 1) * DV], g.sT[half(c_), h], vg[half(c_), t, h * DV:(h + 1) * DV])
                            finish(insA)
                            open_bank("gkv", p, d)
                            pe.wait_ge(s_turn, turn)
                    finish(ins)
                if p < NT - 1:
                    ada_rows(4 + p)
                bs, turn = [open_early("goB", p, d) for d in range(2)], [0, 0]
                for hp in range(2):
                    for d in range(2):
                        g = gws[d]
                        if hp == 0:
                            pe.wait_ge(s_gM, 2 * p + d + 1)
                        else:
                            open_bank("goB", p, d)
                            pe.wait_ge(s_turn, turn[d])
                        for c_ in range(GC):
                            for cp in range(2):
                                h = 2 * c_ + hp
                                m = GM[half(hp), 3 if cp == chunk(d, 0) else 4, d, c_]
                                ins = mm(bs[d][half(cp), h * DV:(h + 1) * DV], g.q[half(hp), c_, half(cp)], m)
                        if hp == 1:
                            finish(ins)
                        else:
                            turn[d] = half_done(ins)
                if p < NT - 1:
                    ada_turn(4 + p)
                if p == 2:
                    pe.wait_ge(s_lora, 2)
                    low_rank("w", 0)

            wait_result(pe, "pl", "la")
            wait_result(pe, "pc", "la")
            low_rank("a", 0)
            low_rank("w", 1)
            low_rank("a", 1)
            ada_group(4 + NT - 1, 2 * NMOD)

            for t in range(NT):
                wait_result(pe, "vt", t)
            for p in range(NT):
                cur = MCUR[p]
                if p == 1:
                    pe.wait_ge(s_rin, 32)
                    b = open_bank("s0")
                    for d in range(2):
                        for i in range(RC):
                            ins = tr(b[:, (d * RC + i) * HD:(d * RC + i + 1) * HD], s0buf[:, d, i * P:(i + 1) * P])
                    finish(ins)
                for d in range(2):
                    g, t = segs[d], PAIRS[p][d]
                    pe.wait_ge(s_ops, 2 * p + d + 1)
                    bA = open_early("A", p, d)

                    def a_rows(hp):
                        for i in range(RC):
                            for cp in range(2):
                                h = 2 * i + hp
                                ins = mm(bA[half(cp), h * HD:(h + 1) * HD], g.AR[half(hp), i, cp, 0], g.b[half(hp), i, half(cp)])
                        return ins

                    def scores(n, hp):
                        src = g.b if n == "b" else g.k
                        b = open_bank(f"{n}{hp}", p, d)
                        for i in range(RC):
                            for cp in range(2):
                                ins = mm(b[half(cp), i * 2 * HD:(i + 1) * 2 * HD], src[half(hp), i, half(cp)], g.AR[half(hp), i, cp])
                        finish(ins)
                    turn = half_done(a_rows(0))
                    scores("b", 0)
                    open_bank("A", p, d)
                    pe.wait_ge(s_turn, turn)
                    finish(a_rows(1))
                    scores("b", 1)
                    scores("k", 0)
                    scores("k", 1)
                for d in range(2):
                    g, t = segs[d], PAIRS[p][d]
                    for n in ("tA", "tB", "tK"):
                        b = open_bank(n, p, d)
                        for i in range(RC):
                            src = {"tA": g.AR[:, i, :, 0], "tB": g.b[:, i], "tK": g.k[:, i]}[n]
                            ins = tr(b[:, i * P:(i + 1) * P], src)
                        finish(ins)
                    wait_result(pe, "k0", p, d)
                    wait_result(pe, "k1", p, d)
                    b = open_bank("AV", p, d)
                    for h in range(NH):
                        for cp in range(2):
                            ins = mm(b[half(cp), h * HD:(h + 1) * HD], g.K2[half(cp), 0, h], vtok[half(cp), t, h * HD:(h + 1) * HD])
                    finish(ins)

                def blocks(n, d, lhsT, rhs):
                    b = open_bank(n, p, d)
                    for h in range(NH):
                        for cp in range(2):
                            ins = mm(b[half(cp), h * HD:(h + 1) * HD], lhsT(half(cp), h), rhs(half(cp), h))
                    finish(ins)

                def of(v):
                    return lambda part, h: v[part, h]
                for n in INV:
                    for d in range(2):
                        g = segs[d]
                        Z, U1t, U2t = g.A3[:, 0], g.A3[:, 1], g.A3[:, 2]
                        I64 = lambda part, h: identh[part, :]
                        plan = {"Z1": (of(U1t), of(g.X1), ("A",)), "X5": (of(g.D2), of(Z), ("Z1",)), "X5t": (of(g.X0), I64, ("X5",)),
                                "Z2": (of(U2t), of(g.X0), ()), "X6": (of(g.D2), of(Z), ("X5t", "Z2"))}
                        if n in ("Z1", "X5") and d == 0:
                            pe.wait_ge(s_inv[0 if n == "Z1" else 1], 64 * (p + 1))
                        lhsT, rhs, needs = plan[n]
                        for m in needs:
                            wait_result(pe, m, p, d)
                        blocks(n, d, lhsT, rhs)
                for d in range(2):
                    g = segs[d]
                    wait_result(pe, "X6", p, d)
                    wait_result(pe, "tA", p, d)
                    wait_result(pe, "AV", p, d)
                    for j in range(2):
                        b = open_bank("WU", p, d, j)
                        for h in range(4 * j, 4 * j + 4):
                            ins = mm(b[:, (h % 4) * 2 * HD:(h % 4 + 1) * 2 * HD], g.XB[:, h], g.X[:, h])
                        finish(ins)
                for d in range(2):
                    g, t = segs[d], PAIRS[p][d]
                    for n in (("WU", p, d, 0), ("WU", p, d, 1), ("tB", p, d), ("tK", p, d)):
                        wait_result(pe, *n)
                    for cp in range(2):
                        b = open_bank("G", p, d, cp)
                        for h in range(NH):
                            ins = mm(b[half(h % 2), (h // 2) * 2 * HD:(h // 2 + 1) * 2 * HD], g.WU[half(cp), h, 0:HD], g.B3[half(cp), 1:3, h])
                        finish(ins)
                    for cp in range(2):
                        b = open_bank("H", p, d, cp)
                        for h in range(NH):
                            o = b[half(h % 2), (h // 2) * HD:(h // 2 + 1) * HD]
                            mm(o, g.B3[half(cp), 2, h], g.WU[half(cp), h, HD:2 * HD], True, False)
                            ins = mm(o, g.ktok[half(cp), h], vtok[half(cp), t, h * HD:(h + 1) * HD], False, True)
                        finish(ins)
                for k in range(2):
                    for d in range(2):
                        g, cp = segs[d], chunk(d, k)
                        src = MR[:, cur, d] if k == 0 else MM[:, d]
                        if k == 1:
                            pe.wait_ge(s_mst, 1 + 4 * p + d + 1)
                        elif p == 0:
                            pe.wait_ge(s_mst, 1)
                        elif p == 1:
                            wait_result(pe, "s0")
                        else:
                            pe.wait_ge(s_mst, 1 + 4 * (p - 1) + 2 + d + 1)
                        wait_result(pe, "G", p, d, cp)
                        b = open_bank("seq", p, d, k)
                        for h in range(NH):
                            ins = mm(b[half(h % 2), (h // 2) * HD:(h // 2 + 1) * HD], g.GT[half(h % 2), h // 2, cp], src[half(h % 2), h // 2])
                        finish(ins)
                for d in range(2):
                    g, t = segs[d], PAIRS[p][d]
                    bA, bB = open_early("Ya", p, d), open_early("Yb", p, d)

                    def from_state(hp):
                        for i in range(RC):
                            for cp in range(2):
                                h = 2 * i + hp
                                m = MR[:, cur, d] if cp == chunk(d, 0) else MM[:, d]
                                ins = mm(bB[half(cp), h * HD:(h + 1) * HD], g.QT[half(hp), i, cp], m[half(hp), i])
                        return ins
                    turn = half_done(from_state(0))
                    open_bank("Ya", p, d)
                    for h in range(NH):
                        for cp in range(2):
                            o = bA[half(cp), h * HD:(h + 1) * HD]
                            mm(o, g.B3[half(cp), 1, h], g.WU[half(cp), h, HD:2 * HD], True, False)
                            ins = mm(o, g.K2[half(cp), 1, h], vtok[half(cp), t, h * HD:(h + 1) * HD], False, True)
                    finish(ins)
                    open_bank("Yb", p, d)
                    pe.wait_ge(s_turn, turn)
                    finish(from_state(1))
                if p == 0:
                    pe.wait_ge(s_mst, 5)
                    for d in range(2):
                        b = open_bank("st", d)
                        for i in range(RC):
                            ins = tr(b[0:HD, i * P:(i + 1) * P], MR[:, 1, d, i])
                        finish(ins)

            def row_vectors(nme):
                for cnd in range(2):
                    for h in range(2):
                        b = open_bank("rowb", nme, cnd, h)
                        for j in range(4):
                            k = 4 * h + j
                            col = {"ga1": modv[:, 2 * KT + k, cnd:cnd + 1], "sc2": gscv[:, 1, k, cnd:cnd + 1],
                                   "sh2": modv[:, 3 * KT + k, cnd:cnd + 1], "ga2": modv[:, 5 * KT + k, cnd:cnd + 1]}[nme]
                            ins = mm(b[:, j * P:(j + 1) * P], col.broadcast_to([P, P]), ident[:, :])
                        finish(ins)
            pe.wait_ge(s_g2, 1)
            for nme in ("ga1", "sc2", "sh2"):
                row_vectors(nme)
            pe.wait_ge(s_wo, 128)
            def gate(t):
                finish(mm(open_bank("gate", t)[:, :], slg[:, t * P:(t + 1) * P], g2_sb))

            def turn_y(t):
                wait_result(pe, "gate", t)
                for j in range(2):
                    b = open_bank("yT", t, j)
                    src = ya if j == 0 else yg[:, t]
                    for i in range(4):
                        ins = tr(b[:, i * P:(i + 1) * P], src[:, i * P:(i + 1) * P])
                    finish(ins)

            def turn_h2(t):
                pe.wait_ge(s_h2, t + 1)
                for j in range(2):
                    b = open_bank("hT2", t, j)
                    for i in range(4):
                        ins = tr(b[:, i * P:(i + 1) * P], h2[:, (4 * j + i) * P:(4 * j + i + 1) * P])
                    finish(ins)

            def router(t):
                for j in range(2):
                    wait_result(pe, "hT2", t, j)
                b = open_bank("router", t)
                for k in range(KT):
                    ins = mm(b[:, 0:NR], h2T[:, k, t * P:(t + 1) * P], wr[:, k, :], start=k == 0, stop=k == KT - 1)
                finish(ins)
            gate(0)
            turn_y(0)
            for t in range(NT):
                if t + 1 < NT:
                    gate(t + 1)
                for j in range(2):
                    wait_result(pe, "yT", t, j)
                if t == 0:
                    pe.wait_ge(s_wout, 32)
                for h in range(2):
                    b = open_bank("out", t, h)
                    for k in range(KT):
                        ins = mm(b[:, :], yT[:, k], ring[:, h, k, :], start=k == 0, stop=k == KT - 1)
                    finish(ins)
                if t + 1 < NT:
                    turn_y(t + 1)
                if t >= 1:
                    turn_h2(t - 1)
                    router(t - 1)
            turn_h2(NT - 1)
            router(NT - 1)
            row_vectors("ga2")

            pe.wait_ge(s_pick, 1)
            b = open_bank("rank")
            for t in range(NT + 1):
                o = b[:, t * NE:(t + 1) * NE]
                for u in range(min(t + 1, NT)):
                    ins = mm(o, upper if u == t else ones, picked[:, u * NE:(u + 1) * NE], start=u == 0, stop=u == min(t, NT - 1))
            finish(ins)

            def expert_products(r):
                pe.wait_ge(s_oh, r + 1)
                b = open_bank("ids", r)
                for j in range(2):
                    for t in range(NT):
                        ins = mm(b[:, 0:NE], onehot[:, j, t], (first_ids if j == 0 else second_ids)[:, t], start=(j, t) == (0, 0), stop=(j, t) == (1, NT - 1))
                finish(ins)

                def turn_rows(i):
                    pe.wait_ge(s_xg[i % 3], 16 * (i // 3 + 1))
                    for j in range(2):
                        b = open_bank("xT", i, j)
                        for k in range(4):
                            ins = tr(b[:, k * P:(k + 1) * P], xg[:, i % 3, (4 * j + k) * P:(4 * j + k + 1) * P])
                        finish(ins)

                def down(i):
                    wait_result(pe, "aT", i)
                    pe.wait_ge(s_w2[i % 2], 16 * (i // 2 + 1))
                    for h in range(2):
                        b = open_bank("dn", i, h)
                        for f in range(FT):
                            ins = mm(b[:, :], aT[:, i % 2, f], w2r[:, i % 2, f, h * 512:(h + 1) * 512], start=f == 0, stop=f == FT - 1)
                        finish(ins)

                for e in range(NE):
                    i = r * NE + e
                    if e == 0:
                        turn_rows(i)
                    for j in range(2):
                        wait_result(pe, "xT", i, j)
                    pe.wait_ge(s_w13[i % 2], 32 * (i // 2 + 1))
                    b = open_bank("ug", i)
                    for k in range(KT):
                        ins = mm(b[:, :], xgT[:, i % 2, k], ring[:, i % 2, k, :], start=k == 0, stop=k == KT - 1)
                    finish(ins)
                    if e < NE - 1:
                        turn_rows(i + 1)
                    if e > 0:
                        down(i - 1)
                    wait_result(pe, "ug", i)
                    b = open_bank("aT", i)
                    for f in range(FT):
                        ins = tr(b[:, f * P:(f + 1) * P], ac[:, i % 2, f * P:(f + 1) * P])
                    finish(ins)
                down(i)
            rounds(pe, expert_products)


_INS = ["x_prompt", "x_sample", "state_rwkv", "state_gla", "c", "c_ctx", "norm1_g", "norm2_g", "w_ada", "b_ada", "w_in",
        "w_out", "rw_conv", "rw_w0", "rw_w2", "rw_a0", "rw_a2", "rw_g2", "rw_k_k", "rw_k_a", "rw_r_k", "rw_ln_w", "rw_ln_b",
        "gla_gk2", "gla_gk_b", "gla_norm_g", "moe_w_group", "moe_b_group", "moe_w_expert", "moe_b_expert", "moe_w1",
        "moe_w3", "moe_w2", "final_g"]
_OUTS = [((1, 128, 1024), "float32"), ((1, 512, 1024), "float32"), ((1, 1, 2, 8, 64, 64), "float32"), ((1, 1, 2, 4, 64, 128), "float32")]


def kernel(**inputs):
    import numpy as _np
    import concourse.bacc as _bacc
    from concourse import mybir as _mybir
    from concourse.bass_utils import run_bass_kernel_spmd as _run

    nc = _bacc.Bacc("TRN2", target_bir_lowering=False, num_devices=1)
    arrays, args = {}, []
    for name in _INS:
        a = _np.ascontiguousarray(inputs[name])
        arrays[f"in_{name}_dram"] = a
        args.append(nc.dram_tensor(f"in_{name}_dram", a.shape, _mybir.dt.from_np(a.dtype), kind="ExternalInput").ap())
    for i, (shape, dtype) in enumerate(_OUTS):
        args.append(nc.dram_tensor(f"out_{i}_dram", shape, _mybir.dt.from_np(_np.dtype(dtype)), kind="ExternalOutput").ap())
    trunk_program(nc, *args)
    r = _run(nc, [arrays], core_ids=[0])
    return tuple(r.results[0][f"out_{i}_dram"] for i in range(len(_OUTS)))
```
